# Optimizing a Trainium2 kernel written in Bass

```python
import math
import jax
import jax.numpy as jnp
from jax import lax
import numpy as np

D_MODEL = 1024
BATCH = 1
SEQ = 128
DEPTH = 2
DEC_BATCH = 1
DEC_SEQ = 256
PAST_LEN = 128

GRID_W = 64
MIX_WIDTH = D_MODEL
GM_HEADS = 4
GM_HEAD_DIM = 64
GM_WIDTH = GM_HEADS * GM_HEAD_DIM
CHUNK = 128
HY_WIDTH = MIX_WIDTH // 4
HY_ORDER = 2
HY_SHORT = 3
HY_EMB_DIM = 33
HY_FILTER_HIDDEN = 64
HY_DECAY_TARGET = 1e-2
HY_DECAY_PCT_SHORT = 0.3
HY_DECAY_PCT_LONG = 1.5
MLA_NOPE = 64
MLA_ROPE = 32
MLA_V = 64
MLA_WIDTH = MIX_WIDTH - GM_WIDTH - HY_WIDTH
MLA_HEADS = MLA_WIDTH // MLA_V
MLA_Q_LORA = D_MODEL // 4
MLA_KV_LORA = D_MODEL // 8
ROPE_THETA = 10000.0
Q_BLOCK = 128
SPLIT_SIZES = (GM_WIDTH, GM_WIDTH, 3 * HY_WIDTH, MLA_Q_LORA, MLA_KV_LORA, MLA_ROPE)
SPLIT_POINTS = tuple(int(s) for s in np.cumsum(SPLIT_SIZES)[:-1])
IN_COLS = sum(SPLIT_SIZES)
MOE_GROUPS = 4
MOE_EXPERTS_PER_GROUP = 8
MOE_N_EXPERTS = MOE_GROUPS * MOE_EXPERTS_PER_GROUP
MOE_TOP_K = 2
MOE_D_EXPERT = 256
ALPHA = (2.0 * DEPTH) ** 0.25
BETA = (8.0 * DEPTH) ** -0.25
LN_EPS = 1e-5
RMS_EPS = 1e-6
F32 = jnp.float32

kernel_name = 'hybrid_gmlp_hyena_mla_hmoe_diffusion_step'

def layer_norm(x, g, b):
    xf = x.astype(F32)
    xc = xf - jnp.mean(xf, -1, keepdims=True)
    var = jnp.mean(xc * xc, -1, keepdims=True)
    return (xc * lax.rsqrt(var + LN_EPS) * g.astype(F32) + b.astype(F32)).astype(x.dtype)

def rms_norm(x, g):
    xf = x.astype(F32)
    return (xf * lax.rsqrt(jnp.mean(xf * xf, -1, keepdims=True) + RMS_EPS) * g.astype(F32)).astype(x.dtype)

def axial_rope(L):
    rows = L // GRID_W
    row = jnp.repeat(jnp.arange(rows, dtype=F32), GRID_W)
    col = jnp.tile(jnp.arange(GRID_W, dtype=F32), rows)
    n = MLA_ROPE // 4
    inv = ROPE_THETA ** (-jnp.arange(n, dtype=F32) / n)
    ang = jnp.concatenate([row[:, None] * inv, col[:, None] * inv], -1)
    return jnp.cos(ang), jnp.sin(ang)

def apply_rope(x, cos, sin):
    x1, x2 = x[..., 0::2], x[..., 1::2]
    return jnp.stack([x1 * cos - x2 * sin, x1 * sin + x2 * cos], -1).reshape(x.shape).astype(x.dtype)

def gmlp_chunk_mixer(u, v, p):
    B, L, _ = u.shape
    n = L // CHUNK
    u = jax.nn.gelu(u)
    vh = jax.nn.gelu(v).reshape(B, L, GM_HEADS, GM_HEAD_DIM)
    vh = layer_norm(vh, p['gm_ln_g'].reshape(GM_HEADS, GM_HEAD_DIM), p['gm_ln_b'].reshape(GM_HEADS, GM_HEAD_DIM))
    vh = vh.reshape(B, n, CHUNK, GM_HEADS, GM_HEAD_DIM)
    s = jnp.einsum('hqk,bnkhd->bnqhd', p['gm_ws'], vh) + p['gm_bs'].T[:, :, None]
    return u * s.reshape(B, L, GM_WIDTH)

def hyena_filter_spectrum(L, p):
    t = jnp.linspace(0.0, 1.0, L, dtype=F32)[:, None]
    bands = (HY_EMB_DIM - 1) // 2
    w = 2.0 * math.pi * jnp.arange(L, dtype=F32)[:, None] / L
    f = jnp.linspace(1e-4, bands - 1, bands, dtype=F32)[None]
    z = jnp.concatenate([t, jnp.cos(f * w), -jnp.sin(f * w)], -1)
    freq = p['hy_f_freq'].astype(F32)
    hid = jnp.sin(freq[0] * (z @ p['hy_f_w1'].astype(F32) + p['hy_f_b1'].astype(F32)))
    hid = jnp.sin(freq[1] * (hid @ p['hy_f_w2'].astype(F32) + p['hy_f_b2'].astype(F32)))
    filt = (hid @ p['hy_f_w3'].astype(F32)).reshape(L, HY_ORDER, 2, HY_WIDTH)
    min_decay = math.log(HY_DECAY_TARGET) / HY_DECAY_PCT_LONG
    max_decay = math.log(HY_DECAY_TARGET) / HY_DECAY_PCT_SHORT
    deltas = jnp.abs(jnp.linspace(min_decay, max_decay, HY_WIDTH, dtype=F32))
    filt = filt * jnp.exp(-t * deltas)[:, None, None, :]
    fwd, bwd = filt[:, :, 0], filt[:, :, 1]
    two_sided = jnp.concatenate([fwd, jnp.zeros_like(fwd[:1]), bwd[:0:-1]], axis=0)
    return jnp.fft.rfft(two_sided, axis=0)

def long_conv(u, k_spec, bias):
    L = u.shape[1]
    u_f = jnp.fft.rfft(u.astype(F32), n=2 * L, axis=1)
    y = jnp.fft.irfft(u_f * k_spec[None], n=2 * L, axis=1)[:, :L]
    return (y + u.astype(F32) * bias.astype(F32)).astype(u.dtype)

def hyena_mixer(z, p):
    B, L, _ = z.shape
    pad = HY_SHORT // 2
    zp = jnp.pad(z, ((0, 0), (pad, pad), (0, 0)))
    z = sum(zp[:, j:j + L] * p['hy_conv_w'][j] for j in range(HY_SHORT)) + p['hy_conv_b']
    x1, x2, v = jnp.split(z, 3, axis=-1)
    k_spec = hyena_filter_spectrum(L, p)
    y = v
    for o, gate in enumerate((x1, x2)):
        y = gate * long_conv(y, k_spec[:, o], p['hy_bias'][o])
    return y

def mla_attend(q_nope, q_pe, k_nope, k_pe, v):
    B, Lq, H, _ = q_nope.shape
    nb = Lq // Q_BLOCK
    qn = q_nope.reshape(B, nb, Q_BLOCK, H, MLA_NOPE).swapaxes(0, 1)
    qp = q_pe.reshape(B, nb, Q_BLOCK, H, MLA_ROPE).swapaxes(0, 1)
    scale = 1.0 / math.sqrt(MLA_NOPE + MLA_ROPE)

    def one_block(qs):
        qn_b, qp_b = qs
        s = jnp.einsum('bqhd,bkhd->bhqk', qn_b, k_nope) + jnp.einsum('bqhr,bkr->bhqk', qp_b, k_pe)
        prob = jax.nn.softmax(s.astype(F32) * scale, axis=-1).astype(v.dtype)
        return jnp.einsum('bhqk,bkhd->bqhd', prob, v)

    o = lax.map(one_block, (qn, qp))
    return o.swapaxes(0, 1).reshape(B, Lq, H * MLA_V)

def mla_mixer(c_q, c_kv, k_pe, rope, ctx_cache, p):
    B, L, _ = c_q.shape
    q = (rms_norm(c_q, p['mla_gq']) @ p['mla_wuq']).reshape(B, L, MLA_HEADS, MLA_NOPE + MLA_ROPE)
    q_nope, q_pe = q[..., :MLA_NOPE], q[..., MLA_NOPE:]
    ckv = rms_norm(c_kv, p['mla_gkv'])
    if rope is not None:
        cos, sin = rope
        q_pe = apply_rope(q_pe, cos[:, None], sin[:, None])
        k_pe = apply_rope(k_pe, cos, sin)
    keys_ckv, keys_kpe = ckv, k_pe
    if ctx_cache is not None:
        keys_ckv = jnp.concatenate([ctx_cache[0].astype(ckv.dtype), ckv], axis=1)
        keys_kpe = jnp.concatenate([ctx_cache[1].astype(k_pe.dtype), k_pe], axis=1)
    Lk = keys_ckv.shape[1]
    kv = (keys_ckv @ p['mla_wukv']).reshape(B, Lk, MLA_HEADS, MLA_NOPE + MLA_V)
    out = mla_attend(q_nope, q_pe, kv[..., :MLA_NOPE], keys_kpe, kv[..., MLA_NOPE:])
    return out, ckv, k_pe

def token_mixers(h, rope, ctx_cache, p):
    proj = h @ p['w_in']
    u, v, hy_in, c_q, c_kv, k_pe = jnp.split(proj, SPLIT_POINTS, axis=-1)
    a = gmlp_chunk_mixer(u, v, p)
    b = hyena_mixer(hy_in, p)
    m, ckv, kpe = mla_mixer(c_q, c_kv, k_pe, rope, ctx_cache, p)
    out = jnp.concatenate([a, b.astype(a.dtype), m.astype(a.dtype)], axis=-1) @ p['w_out']
    return out, ckv, kpe

def hier_moe(h, p):
    B, L, D = h.shape
    t = h.reshape(B * L, D)
    g_logits = (t @ p['moe_w_gr'] + p['moe_b_gr']).astype(F32)
    g_idx = jnp.argmax(g_logits, -1)
    g_w = jnp.max(jax.nn.softmax(g_logits, -1), -1, keepdims=True)
    e_logits = (jnp.einsum('td,dge->tge', t, p['moe_w_er']) + p['moe_b_er']).astype(F32)
    e_in = jnp.einsum('tge,tg->te', e_logits, jax.nn.one_hot(g_idx, MOE_GROUPS, dtype=F32))
    top_v, top_i = lax.top_k(e_in, MOE_TOP_K)
    top_w = jax.nn.softmax(top_v, -1) * g_w
    flat = g_idx[:, None] * MOE_EXPERTS_PER_GROUP + top_i
    dense_w = jnp.sum(jax.nn.one_hot(flat, MOE_N_EXPERTS, dtype=F32) * top_w[..., None], 1).astype(t.dtype)
    gate = jnp.einsum('td,edf->tef', t, p['moe_w_gate'])
    up = jnp.einsum('td,edf->tef', t, p['moe_w_up'])
    hid = jax.nn.silu(gate) * up * dense_w[..., None]
    return jnp.einsum('tef,efd->td', hid, p['moe_w_down']).reshape(B, L, D)

def trunk_layer(x, cond, rope, ctx_cache, p):
    D = x.shape[-1]
    mod = (jax.nn.silu(cond) @ p['w_mod'] + p['b_mod']).reshape(cond.shape[0], 1, 6, D)
    sh1, sc1, g1, sh2, sc2, g2 = [mod[:, :, i] for i in range(6)]
    h = x * (1 + sc1) + sh1
    mixed, ckv, kpe = token_mixers(h, rope, ctx_cache, p)
    x = layer_norm(ALPHA * x + g1 * mixed, p['ln1_g'], p['ln1_b'])
    h = x * (1 + sc2) + sh2
    x = layer_norm(ALPHA * x + g2 * hier_moe(h, p), p['ln2_g'], p['ln2_b'])
    return x, ckv, kpe

def setup_inputs(seed: int = 0) -> dict:
    key = jax.random.key(seed)
    keys = iter(jax.random.split(key, 48))

    def nrm(shape, scale):
        return jax.random.normal(next(keys), shape, F32) * scale

    D = D_MODEL
    FH = HY_FILTER_HIDDEN
    return {
        'x_prompt': nrm((BATCH, SEQ, D), 1.0),
        'x_sample': nrm((DEC_BATCH, DEC_SEQ, D), 1.0),
        'c': nrm((DEC_BATCH, D), 1.0),
        'cache_ckv': nrm((DEC_BATCH, DEPTH, PAST_LEN, MLA_KV_LORA), 1.0),
        'cache_kpe': nrm((DEC_BATCH, DEPTH, PAST_LEN, MLA_ROPE), 1.0),
        'c_ctx': nrm((D,), 1.0),
        'ln_in_g': 1.0 + nrm((D,), 0.02),
        'ln_in_b': nrm((D,), 0.02),
        'w_mod': nrm((DEPTH, D, 6 * D), 0.5 * D ** -0.5),
        'b_mod': nrm((DEPTH, 6 * D), 0.02),
        'w_in': nrm((DEPTH, D, IN_COLS), D ** -0.5),
        'gm_ln_g': 1.0 + nrm((DEPTH, GM_WIDTH), 0.02),
        'gm_ln_b': nrm((DEPTH, GM_WIDTH), 0.02),
        'gm_ws': nrm((DEPTH, GM_HEADS, CHUNK, CHUNK), CHUNK ** -0.5),
        'gm_bs': 1.0 + nrm((DEPTH, GM_HEADS, CHUNK), 0.02),
        'hy_conv_w': nrm((DEPTH, HY_SHORT, 3 * HY_WIDTH), HY_SHORT ** -0.5),
        'hy_conv_b': nrm((DEPTH, 3 * HY_WIDTH), 0.02),
        'hy_f_w1': nrm((DEPTH, HY_EMB_DIM, FH), HY_EMB_DIM ** -0.5),
        'hy_f_b1': nrm((DEPTH, FH), 0.02),
        'hy_f_w2': nrm((DEPTH, FH, FH), FH ** -0.5),
        'hy_f_b2': nrm((DEPTH, FH), 0.02),
        'hy_f_w3': nrm((DEPTH, FH, HY_ORDER * 2 * HY_WIDTH), 0.1 * FH ** -0.5),
        'hy_f_freq': 1.0 + nrm((DEPTH, 2, FH), 0.02),
        'hy_bias': nrm((DEPTH, HY_ORDER, HY_WIDTH), 0.1),
        'mla_gq': 1.0 + nrm((DEPTH, MLA_Q_LORA), 0.02),
        'mla_gkv': 1.0 + nrm((DEPTH, MLA_KV_LORA), 0.02),
        'mla_wuq': nrm((DEPTH, MLA_Q_LORA, MLA_HEADS * (MLA_NOPE + MLA_ROPE)), MLA_Q_LORA ** -0.5),
        'mla_wukv': nrm((DEPTH, MLA_KV_LORA, MLA_HEADS * (MLA_NOPE + MLA_V)), MLA_KV_LORA ** -0.5),
        'w_out': nrm((DEPTH, MIX_WIDTH, D), BETA * MIX_WIDTH ** -0.5),
        'ln1_g': 1.0 + nrm((DEPTH, D), 0.02),
        'ln1_b': nrm((DEPTH, D), 0.02),
        'ln2_g': 1.0 + nrm((DEPTH, D), 0.02),
        'ln2_b': nrm((DEPTH, D), 0.02),
        'moe_w_gr': nrm((DEPTH, D, MOE_GROUPS), D ** -0.5),
        'moe_b_gr': nrm((DEPTH, MOE_GROUPS), 0.01),
        'moe_w_er': nrm((DEPTH, D, MOE_GROUPS, MOE_EXPERTS_PER_GROUP), D ** -0.5),
        'moe_b_er': nrm((DEPTH, MOE_GROUPS, MOE_EXPERTS_PER_GROUP), 0.01),
        'moe_w_gate': nrm((DEPTH, MOE_N_EXPERTS, D, MOE_D_EXPERT), D ** -0.5),
        'moe_w_up': nrm((DEPTH, MOE_N_EXPERTS, D, MOE_D_EXPERT), D ** -0.5),
        'moe_w_down': nrm((DEPTH, MOE_N_EXPERTS, MOE_D_EXPERT, D), BETA * MOE_D_EXPERT ** -0.5),
    }

def reference(x_prompt, x_sample, c, cache_ckv, cache_kpe, c_ctx, ln_in_g, ln_in_b, w_mod, b_mod, w_in,
              gm_ln_g, gm_ln_b, gm_ws, gm_bs, hy_conv_w, hy_conv_b, hy_f_w1, hy_f_b1, hy_f_w2, hy_f_b2,
              hy_f_w3, hy_f_freq, hy_bias, mla_gq, mla_gkv, mla_wuq, mla_wukv, w_out, ln1_g, ln1_b,
              ln2_g, ln2_b, moe_w_gr, moe_b_gr, moe_w_er, moe_b_er, moe_w_gate, moe_w_up, moe_w_down):
    def layer_params(l):
        return dict(w_mod=w_mod[l], b_mod=b_mod[l], w_in=w_in[l], gm_ln_g=gm_ln_g[l], gm_ln_b=gm_ln_b[l],
                    gm_ws=gm_ws[l], gm_bs=gm_bs[l], hy_conv_w=hy_conv_w[l], hy_conv_b=hy_conv_b[l],
                    hy_f_w1=hy_f_w1[l], hy_f_b1=hy_f_b1[l], hy_f_w2=hy_f_w2[l], hy_f_b2=hy_f_b2[l],
                    hy_f_w3=hy_f_w3[l], hy_f_freq=hy_f_freq[l], hy_bias=hy_bias[l], mla_gq=mla_gq[l],
                    mla_gkv=mla_gkv[l], mla_wuq=mla_wuq[l], mla_wukv=mla_wukv[l], w_out=w_out[l],
                    ln1_g=ln1_g[l], ln1_b=ln1_b[l], ln2_g=ln2_g[l], ln2_b=ln2_b[l],
                    moe_w_gr=moe_w_gr[l], moe_b_gr=moe_b_gr[l], moe_w_er=moe_w_er[l], moe_b_er=moe_b_er[l],
                    moe_w_gate=moe_w_gate[l], moe_w_up=moe_w_up[l], moe_w_down=moe_w_down[l])

    xp = layer_norm(x_prompt, ln_in_g, ln_in_b)
    cond_ctx = c_ctx[None]
    ckv_list, kpe_list = [], []
    for l in range(DEPTH):
        xp, ckv_l, kpe_l = trunk_layer(xp, cond_ctx, None, None, layer_params(l))
        ckv_list.append(ckv_l)
        kpe_list.append(kpe_l)
    state_ckv = jnp.stack(ckv_list, axis=1)
    state_kpe = jnp.stack(kpe_list, axis=1)

    rope_lat = axial_rope(x_sample.shape[1])
    xs = layer_norm(x_sample, ln_in_g, ln_in_b)
    for l in range(DEPTH):
        xs, _, _ = trunk_layer(xs, c, rope_lat, (cache_ckv[:, l], cache_kpe[:, l]), layer_params(l))

    return (xp, xs, state_ckv, state_kpe)


_drawn_inputs = setup_inputs


def setup_inputs(seed=0):
    import zlib

    import numpy as np

    out = dict(_drawn_inputs(seed))
    spreads = {}
    factors = {'cache_ckv': 8.0,
     'cache_kpe': 8.0,
     'ln_in_b': 2.768,
     'gm_ln_g': 184.083,
     'gm_ln_b': 184.649,
     'gm_bs': 200.0,
     'hy_conv_w': 3.762,
     'hy_conv_b': 8.0,
     'hy_f_w1': 3.688,
     'hy_f_b1': 8.0,
     'hy_f_w2': 3.582,
     'hy_f_b2': 8.0,
     'hy_f_w3': 3.917,
     'hy_f_freq': 8.0,
     'hy_bias': 8.0,
     'mla_gq': 23.298,
     'mla_gkv': 9.131,
     'mla_wuq': 3.8,
     'moe_b_gr': 34.478,
     'moe_b_er': 31.164}
    for name, (base, spread) in spreads.items():
        noise = np.random.default_rng([zlib.crc32(name.encode()), seed]).standard_normal(out[name].shape)
        drawn = base * np.exp(spread * noise) if base else spread * noise
        out[name] = jnp.asarray(drawn.astype(out[name].dtype))
    for name, factor in factors.items():
        out[name] = (out[name] * factor).astype(out[name].dtype)
    return out
```

```python
from contextlib import ExitStack
import math

import numpy as np
import concourse.bass as bass
from concourse import mybir

F32 = mybir.dt.float32
I32 = mybir.dt.int32
ACT = mybir.ActivationFunctionType
ALU = mybir.AluOpType
AX = mybir.AxisListType

P = 128
D = 1024
K8 = D // P
DEPTH = 2
TT = 3
TOK = TT * P
LAT = 2 * P
KEYS = 4 * P
GW = 64
HEADS = 8
QK = 96
ROPE = 32
CH = 256
FH = 64
EMB = 33
MLA_COLS = 416
GROUPS = 4
EPG = 8
FF = 256
EXTRA = 2
RING = 6
CHUNK = 2048
MOD_CHUNKS = 6 * D // 256
IN_CHUNKS = ((0, 256), (256, 256), (512, 256), (768, 256), (1024, 256), (1280, 144), (1424, 136), (1560, 136))
MIX_CHUNKS = len(IN_CHUNKS) + 4
MOE_CHUNKS = GROUPS * EPG * 3
ALPHA = (2.0 * DEPTH) ** 0.25
LN_EPS = 1e-5
RMS_EPS = 1e-6
QK_SCALE = 1.0 / math.sqrt(QK)
SMALL_LOADS = 10
MAGIC = 1.5 * 2.0 ** 23
TWO_PI_HI = 6.28125
TWO_PI_LO = 2.0 * math.pi - 6.28125
PI_SAFE = 3.1415925
BIG = 1.0e30

C_ID, C_TRI, C_ONE, C_IOTA = 0, 128, 256, 384
C_RANK, C_GE, C_COS, C_SIN = 512, 516, 524, 588
C_GI, C_VI, C_MASK = 652, 656, 662
C_END = 665
F_C, F_S, F_CT, F_ST = 128, 640, 1280, 1792
G_C, G_S, G_CT, G_ST = 0, 1152, 2304, 2432
DFT_COLS = 2560

PER = dict(
    filt_in=1, hid_in=1, sin_in=2, hid=2, filt_raw=6, filt_eo=3, spec_raw=3, spec=3, 
    h=3, hT_raw=8, hT=8, uv=3, hy=3, mla=3,
    zc=6, gm_var=1, gm_std=1, vh=1, s_raw=2, a=1, aT_raw=2, aT=2,
    rms_ss=1, rms_var=1, rms_std=1, mla_n=1, wuq_sw=1, latT_raw=4, latT=4,
    ut_raw=4, ut=4, uf_raw=6, yf=6, yc_raw=4, yc=4,
    q_raw=8, q_nope=8, q_pe=8, k_raw=4, kT=4, v_raw=4, v=4,
    sc_raw=8, mx=8, pexp=8, pn=8, pT_raw=16, pT=16, pv=8, oT=4,
    ln1_var=3, ln1_std=3, x1=3, h2=3, h2T_raw=8, h2T=8, lg_raw=1, oh=1, lg_sh=1, lg_exp=1, cum_raw=1, tgt=1, regs=1,
    ln2_var=3, ln2_std=3, x2=3,
)


def pos(kind, e):
    if kind == "D":
        return 3 * e + 4 if e < EPG - 1 else 3 * e + 2
    return (0 if e == 0 else 3 * e - 1) + (kind == "U")


VISIT = sorted(((pos(kind, e), kind, e) for kind in "GUD" for e in range(EPG)))


def build(nc, a, outs):
    ctx = ExitStack()

    def sb(name, shape, dt=F32):
        return ctx.enter_context(nc.sbuf_tensor(name, shape, dt))

    def sem(name):
        return ctx.enter_context(nc.semaphore(name))

    ps = [ctx.enter_context(nc.psum_tensor(f"bank{i}", [P, 512], F32)) for i in range(8)]
    ring = sb("ring", [P, RING, CHUNK])
    x = sb("x", [P, TT, D])
    region_a = sb("region_a", [P, TT * D])
    act_t = sb("act_t", [P, K8, TOK])
    modr = sb("modr", [P, 4, D])
    lnr = sb("lnr", [P, 2, D])
    region_k = sb("region_k", [P, 4096])
    region_s = sb("region_s", [P, TT * D])
    region_q = sb("region_q", [P, HEADS * TOK])
    region_v = sb("region_v", [P, 2048])
    region_u = sb("region_u", [P, 2304])
    mla = sb("mla", [P, TT, MLA_COLS])
    utok = sb("utok", [P, TT, CH])
    dft = sb("dft", [P, DFT_COLS])
    cst = sb("cst", [P, C_END])
    ropeT = sb("ropeT", [QK, 2, LAT])
    wuq = sb("wuq", [P, 2, HEADS * QK])
    wuq_sw = sb("wuq_sw", [P, 2, HEADS * ROPE])
    wukv = sb("wukv", [P, HEADS * 128])
    wsT = sb("wsT", [P, 4, P])
    wr = sb("wr", [P, K8, 36])
    rows = sb("rows", [P, 932])
    cols = sb("cols", [P, 32])
    fw = sb("fw", [FH, 132])
    st = sb("st", [P, 96])
    xi = sb("xi", [P, 4], I32)

    bs_c = cols[:, 0:4]
    cw = cols[:, 4:28].rearrange("p (j c) -> p j c", j=4)
    hyb = cols[:, 28:32].rearrange("p (o c) -> p o c", o=2)
    cT = utok[:, 0, :].rearrange("p (k n) -> p k n", k=K8)
    craw = utok[:, 1, 0:2 * K8].rearrange("p (c k) -> p c k", c=2)
    h = region_a[:].rearrange("p (t d) -> p t d", t=TT)
    zc = region_a[:, 0:6 * TOK].rearrange("p (c t) -> p c t", c=6)
    kT = region_k[:].rearrange("p (h t) -> p h t", h=HEADS)
    v_sb = region_v[:].rearrange("p (k n) -> p k n", k=4)
    spec = region_s[:].rearrange("p (b c n) -> p b c n", b=3, c=2)
    hy = region_q[:, 0:6 * 387].rearrange("p (c t) -> p c t", c=6)
    qT = region_q[:].rearrange("p (h t) -> p h t", h=HEADS)
    uv = region_u[:, 0:1536].rearrange("p (t n) -> p t n", t=TT)
    vh = region_u[:, 1536:2304].rearrange("p (t n) -> p t n", t=TT)
    probs = region_u[:, 0:896]
    probsT = region_u[:, 896:1792].rearrange("p (b n) -> p b n", n=128)
    yfre = region_v[:, 0:1536].rearrange("p (b c n) -> p b c n", b=3, c=2)
    ytmp = region_v[:, 1536:2048]
    f_sum = region_k[:, 0:1536].rearrange("p (t n) -> p t n", t=TT)
    f_dif = region_k[:, 1536:3072].rearrange("p (t n) -> p t n", t=TT)
    w3 = region_k[0:FH, 3072:4096]
    decay = region_v[:, 0:768].rearrange("p (t n) -> p t n", t=TT)
    f_tmp = region_v[:, 768:1280]
    f_arg = region_u[0:FH, 0:384]
    f_n = region_u[0:FH, 384:768]
    hid1 = region_u[0:FH, 768:1152]
    hid2 = region_u[0:FH, 1152:1536]
    zT = region_u[0:EMB, 1536:1920]
    spare = modr[:].rearrange("p a d -> p (a d)")
    cqT = spare[:, 2048:2816].rearrange("p (c t) -> p c t", c=2)
    ckvT = spare[:, 2816:3328]
    kpeb = spare[:, 3328:3712].rearrange("p (t n) -> p t n", t=4)
    cckv = spare[:, 3712:3840]
    qtmp = spare[:, 3840:4096]
    xT = region_k[:].rearrange("p (v k n) -> p v k n", v=4, k=K8)
    moe = region_s[:].rearrange("p (t d) -> p t d", t=TT)
    selT = region_v[:, 0:1536].rearrange("p (v t n) -> p v t n", v=4, t=TT)
    sel = region_q[:, 0:384].rearrange("p (t n) -> p t n", t=TT)
    y_sb = region_q[:, 384:1408]
    sg = region_q[:, 1408:1920].rearrange("p (b n) -> p b n", b=2)
    hd = region_q[:, 1920:2432].rearrange("p (b n) -> p b n", b=2)
    hdT = region_q[:, 2432:2944].rearrange("p (b n) -> p b n", b=2)
    rt = region_v[:, 1536:2048]
    wslot = region_q[:, 2944:3008].rearrange("p (v n) -> p v n", n=8)

    ident = cst[:, C_ID:C_ID + P]
    tri = cst[:, C_TRI:C_TRI + P]
    ones = cst[:, C_ONE:C_ONE + P]
    iota = cst[:, C_IOTA:C_IOTA + P]

    s = {name: sem(name) for name in PER}
    for name in ("const_in", "dft_in", "x_in", "cond_in", "cT", "mod_zero", "bmod_in", "mod_sum", "mod_out",
                 "x0_var", "x0_std", "x0", "chunk_done", "small_in", "cache_in",
                 "mod12_in", "gate_in", "ln_in", "dve_step", "state_out", "y_out"):
        s[name] = sem(name)
    ring_full = [sem(f"ring_full{i}") for i in range(RING)]
    MOE_NAMES = ("sel", "xT_raw", "xT", "silu", "hid_e", "hidT_raw", "hidT", "y", "sct", "acc")
    e_main = {n: sem("e_" + n) for n in MOE_NAMES}
    e_extra = [{n: sem(f"x{l}_" + n) for n in MOE_NAMES + ("chunk_done",)} for l in range(DEPTH)]
    x_full = [[sem(f"x{l}_full{i}") for i in range(RING)] for l in range(DEPTH)]

    def at(name, l, i=None):
        return l * PER[name] + (PER[name] if i is None else i)

    mod_dram = nc.dram_tensor("mod_rows", (DEPTH, 2, 6 * D), F32, kind="Internal").ap()

    LAYER_CHUNKS = MIX_CHUNKS + MOE_CHUNKS
    MOD_ALL = DEPTH * MOD_CHUNKS

    def first_chunk(l):
        return MOD_ALL + l * LAYER_CHUNKS

    block = ctx.enter_context(nc.Block())

    @block.sync
    def _(sp):
        sp.dma_start(cst[:], a["consts"]).then_inc(s["const_in"], 16)
        sp.dma_start(craw[:, 0, :], a["c_ctx"].rearrange("(p k) -> p k", k=K8)).then_inc(s["cond_in"], 16)
        sp.dma_start(craw[:, 1, :], a["c"].rearrange("a (p k) -> p (a k)", k=K8)).then_inc(s["cond_in"], 16)

        def chunk(n, dst, src):
            if n >= RING:
                sp.wait_ge(s["chunk_done"], n - RING + 1)
            sp.dma_start(dst, src).then_inc(ring_full[n % RING], 16)

        def slot(n, cols, k):
            return ring[:, n % RING, 0:cols * k].rearrange("p (k n) -> p k n", k=k)

        for l in range(DEPTH):
            wm = a["w_mod"][l].rearrange("(p k) n -> p k n", k=K8)
            for c in range(MOD_CHUNKS):
                n = l * MOD_CHUNKS + c
                chunk(n, slot(n, 256, K8), wm[:, :, c * 256:(c + 1) * 256])

        for l in range(DEPTH):
            n0 = first_chunk(l)
            wi = a["w_in"][l].rearrange("(p k) n -> p k n", k=K8)
            wo = a["w_out"][l].rearrange("(k p) n -> p k n", p=P)
            for c, (c0, n) in enumerate(IN_CHUNKS):
                chunk(n0 + c, slot(n0 + c, n, K8), wi[:, :, c0:c0 + n])
            for c in range(4):
                chunk(n0 + 8 + c, slot(n0 + 8 + c, D, 2), wo[:, 2 * c:2 * c + 2, :])
            n1 = n0 + MIX_CHUNKS
            w_of = {"G": a["moe_w_gate"][l], "U": a["moe_w_up"][l], "D": a["moe_w_down"][l]}

            def expert(kind, e):
                return w_of[kind][bass.ds(e, 1)].rearrange("a (p k) n -> p (a k n)", k=2 if kind == "D" else K8)

            for v in range(GROUPS):
                nv = n1 + 24 * v

                def load(i, kind, e, loop=0):
                    sp.wait_ge(s["chunk_done"], loop * 6 + (nv + i - RING + 1))
                    sp.dma_start(ring[:, i % RING, :], expert(kind, loop * 2 + (v * EPG + e)))\
                        .then_inc(ring_full[i % RING], 16)

                for i, kind, e in VISIT[:2]:
                    load(i, kind, e)
                with sp.Fori(0, 3) as it:
                    for i, kind, e in VISIT[2:8]:
                        load(i, kind, e, it)
                for i, kind, e in VISIT[20:]:
                    load(i, kind, e)
            sp.wait_ge(s["regs"], at("regs", l))
            extra = sp.value_load(xi[0:1, 0:1], min_val=0, max_val=EXTRA)

            def extra_loads(i):
                g = sp.value_load(xi[0:1, 1 + i:2 + i], min_val=0, max_val=GROUPS - 1)
                for j, kind, e in VISIT:
                    if i == 0 and j < RING:
                        sp.wait_ge(s["chunk_done"], n1 + MOE_CHUNKS - RING + j + 1)
                    else:
                        sp.wait_ge(e_extra[l]["chunk_done"], i * EPG * 3 + j - RING + 1)
                    sp.dma_start(ring[:, j % RING, :], expert(kind, g * EPG + e)).then_inc(x_full[l][j % RING], 16)

            with sp.If(extra >= 1):
                extra_loads(0)
                with sp.If(extra >= 2):
                    extra_loads(1)
                    sp.wait_ge(e_extra[l]["chunk_done"], 2 * EPG * 3)
                sp.wait_ge(e_extra[l]["chunk_done"], EPG * 3)

    @block.gpsimd
    def _(pool):
        pool.dma_start(x[:, 0, :], a["x_prompt"][0]).then_inc(s["x_in"], 16)
        for t in range(2):
            pool.dma_start(x[:, 1 + t, :], a["x_sample"][0, t * P:(t + 1) * P]).then_inc(s["x_in"], 16)

        def row(dst, src):
            return pool.dma_start(dst, src.rearrange("(a n) -> a n", a=1).to_broadcast([P, src.shape[0]]))

        row(lnr[:, 0, :], a["ln_in_g"]).then_inc(s["ln_in"], 16)
        row(lnr[:, 1, :], a["ln_in_b"]).then_inc(s["ln_in"], 16)
        pool.dma_start(dft[:], a["dft"]).then_inc(s["dft_in"], 16)
        pool.dma_start(ropeT[64:96], a["rope_t"]).then_inc(s["dft_in"], 16)
        pool.wait_ge(s["mod_zero"], 1)
        for l in range(DEPTH):
            bview = a["b_mod"][l].rearrange("(a b j n) -> a b j n", a=1, j=4, n=64)
            for j in range(4):
                for c in range(2):
                    pool.dma_start(region_a[32 * j + c:32 * j + c + 1, l * 1536:(l + 1) * 1536].rearrange(
                        "p (b n) -> p b n", n=64), bview[:, :, j, :]).then_inc(s["bmod_in"], 16)

        for l in range(DEPTH):
            if l > 0:
                pool.wait_ge(s["lg_exp"], at("lg_exp", l - 1))
                pool.wait_ge(s["lg_raw"], at("lg_raw", l - 1))
                pool.wait_ge(s["v_raw"], at("v_raw", l - 1))
                pool.wait_ge(s["x2"], at("x2", l - 1))
            small = s["small_in"]
            row(rows[:], a["rows"][l]).then_inc(small, 16)
            pool.dma_start(cols[:], a["cols"][l]).then_inc(small, 16)
            pool.dma_start(fw[:], a["fw"][l]).then_inc(small, 16)
            pool.dma_start(w3, a["hy_f_w3"][l]).then_inc(small, 16)
            pool.dma_start(decay, a["decay"]).then_inc(small, 16)
            pool.dma_start(zT, a["z_t"]).then_inc(small, 16)
            pool.dma_start(wsT[:].rearrange("p h q -> p (h q)"), a["gm_ws_t"][l]).then_inc(small, 16)
            pool.dma_start(wuq[:], a["mla_wuq"][l].rearrange("(c p) n -> p c n", p=P)).then_inc(small, 16)
            pool.dma_start(wukv[:], a["mla_wukv"][l]).then_inc(small, 16)
            pool.dma_start(wr[:].rearrange("p k n -> p (k n)"), a["w_router"][l]).then_inc(small, 16)

            def mod_row(dst, c, i):
                src = mod_dram[l, c:c + 1, i * D:(i + 1) * D]
                return pool.dma_start(dst, src.to_broadcast([P, D]))

            pool.wait_ge(s["mod_out"], 16 * 24 * DEPTH)
            for c in range(2):
                for i in range(2):
                    mod_row(modr[:, 2 * c + i, :], c, i).then_inc(s["mod12_in"], 16)
            pool.wait_ge(s["h"], at("h", l))
            for c in range(2):
                mod_row(modr[:, c, :], c, 2).then_inc(s["gate_in"], 16)
            pool.dma_start(cckv, a["cache_ckv"][0, l]).then_inc(s["cache_in"], 16)
            if l == 0:
                pool.wait_ge(s["x0"], TT)
            else:
                pool.wait_ge(s["x2"], at("x2", l - 1))
            row(lnr[:, 0, :], a["ln1_g"][l]).then_inc(s["ln_in"], 16)
            row(lnr[:, 1, :], a["ln1_b"][l]).then_inc(s["ln_in"], 16)
            pool.dma_start(kpeb[:, 3, 64:96], a["cache_kpe"][0, l]).then_inc(s["cache_in"], 16)
            pool.wait_ge(s["mla_n"], at("mla_n", l))
            pool.dma_start(outs[2][0, l], mla[:, 0, 256:384]).then_inc(s["state_out"], 16)
            pool.dma_start(outs[3][0, l], mla[:, 0, 384:416]).then_inc(s["state_out"], 16)
            pool.wait_ge(s["x1"], at("x1", l))
            row(lnr[:, 0, :], a["ln2_g"][l]).then_inc(s["ln_in"], 16)
            row(lnr[:, 1, :], a["ln2_b"][l]).then_inc(s["ln_in"], 16)
            for c in range(2):
                for i in range(2):
                    mod_row(modr[:, 2 * c + i, :], c, 3 + i).then_inc(s["mod12_in"], 16)
            pool.wait_ge(s["h2"], at("h2", l))
            for c in range(2):
                mod_row(modr[:, c, :], c, 5).then_inc(s["gate_in"], 16)
        for t in range(TT):
            pool.wait_ge(s["x2"], at("x2", DEPTH - 1, t + 1))
            dst = outs[0][0] if t == 0 else outs[1][0, (t - 1) * P:t * P]
            pool.dma_start(dst, x[:, t, :]).then_inc(s["y_out"], 16)
        pool.wait_ge(s["state_out"], 16 * 2 * DEPTH)
        pool.wait_ge(s["y_out"], 16 * TT)

    @block.tensor
    def _(pe):
        pe.wait_ge(s["const_in"], 16)
        pe.wait_ge(s["cT"], 2)
        for l in range(DEPTH):
            for c in range(MOD_CHUNKS):
                n = l * MOD_CHUNKS + c
                pe.wait_ge(ring_full[n % RING], 16 * (n // RING + 1))
                b = n // 8 % 2
                if c % 8 == 0 and n >= 16:
                    pe.wait_ge(s["mod_sum"], n // 8 - 1)
                w = ring[:, n % RING, :].rearrange("p (k n) -> p k n", k=K8)
                for k in range(K8):
                    for j in range(4):
                        mm = pe.matmul(ps[b][32 * j:32 * j + 32, c % 8 * 64:c % 8 * 64 + 64], cT[:, k, :],
                                       w[:, k, j * 64:j * 64 + 64], start=(k == 0), stop=(k == K8 - 1),
                                       tile_position=(0, 32 * j), skip_group_check=True)
                mm.then_inc(s["chunk_done"], 1)

        for l in range(DEPTH):
            n0 = first_chunk(l)

            def loaded(c):
                n = n0 + c
                pe.wait_ge(ring_full[n % RING], 16 * (n // RING + 1))
                return ring[:, n % RING, :]

            pe.wait_ge(s["small_in"], 16 * SMALL_LOADS * (l + 1))
            if l == 0:
                pe.wait_ge(s["dft_in"], 32)
                pe.wait_ge(s["mod_sum"], DEPTH * 3)
            else:
                pe.wait_ge(s["x2"], at("x2", l - 1))
            pe.matmul(ps[0][0:FH, 0:TOK], fw[0:EMB, 0:64], zT, start=True, stop=True).then_inc(s["filt_in"], 1)
            pe.wait_ge(s["hid"], at("hid", l, 1))
            pe.matmul(ps[1][0:FH, 0:TOK], fw[:, 64:128], hid1, start=True, stop=True).then_inc(s["hid_in"], 1)
            pe.wait_ge(s["hid"], at("hid", l, 2))
            for t in range(TT):
                for o in range(2):
                    pe.matmul(ps[2 * t + o][:, :], hid2[:, t * P:(t + 1) * P], w3[:, o * 512:(o + 1) * 512],
                              start=True, stop=True).then_inc(s["filt_raw"], 1)
            pe.wait_ge(s["filt_eo"], at("filt_eo", l))
            for b in range(3):
                tiles = (0,) if b == 0 else (1, 2)
                for part, (m_ctx, m_lat, src) in enumerate(((G_C, F_C, f_sum), (G_S, F_S, f_dif))):
                    for i, t in enumerate(tiles):
                        o = m_ctx if b == 0 else m_lat + i * 256 + (b - 1) * P
                        mm = pe.matmul(ps[2 * b + part][:, :], dft[:, o:o + P], src[:, t, :],
                                       start=(i == 0), stop=(i == len(tiles) - 1))
                mm.then_inc(s["spec_raw"], 1)

            pe.wait_ge(s["h"], at("h", l))
            for k in range(K8):
                if k < 6:
                    pe.wait_ge(s["spec"], at("spec", l, min(k, 5) // 2 + 1))
                else:
                    pe.wait_ge(s["hT"], at("hT", l, k - 5))
                for t in range(TT):
                    mm = pe.transpose(ps[k % 6][:, t * P:(t + 1) * P], h[:, t, k:D:K8], ident)
                mm.then_inc(s["hT_raw"], 1)
            pe.wait_ge(s["hT"], at("hT", l))

            for c in range(2):
                w = loaded(c).rearrange("p (k n) -> p k n", k=K8)
                for t in range(TT):
                    for k in range(K8):
                        mm = pe.matmul(ps[t][:, c * 256:(c + 1) * 256], act_t[:, k, t * P:(t + 1) * P], w[:, k, :],
                                       start=(k == 0), stop=(k == K8 - 1))
                mm.then_inc(s["chunk_done"], 1)
            for c in range(6):
                w = loaded(2 + c // 2).rearrange("p (k n) -> p k n", k=K8)
                if c == 4:
                    pe.wait_ge(s["hy"], at("hy", l, 1))
                for k in range(K8):
                    mm = pe.matmul(ps[3 + c % 4][:, 0:TOK], w[:, k, c % 2 * P:c % 2 * P + P], act_t[:, k, :],
                                   start=(k == 0), stop=(k == K8 - 1))
                if c % 2 == 1:
                    mm.then_inc(s["chunk_done"], 1)
            pe.wait_ge(s["uv"], at("uv", l, 2))
            for c, (c0, n) in enumerate(IN_CHUNKS[5:]):
                w = loaded(5 + c)[:, 0:n * K8].rearrange("p (k n) -> p k n", k=K8)
                for t in range(TT):
                    for k in range(K8):
                        mm = pe.matmul(ps[(7, 0, 1)[t]][:, c0 - 1280:c0 - 1280 + n], act_t[:, k, t * P:(t + 1) * P],
                                       w[:, k, :], start=(k == 0), stop=(k == K8 - 1))
                mm.then_inc(s["chunk_done"], 1)

            pe.wait_ge(s["vh"], at("vh", l))
            pe.wait_ge(s["mla"], at("mla", l))
            for hh in range(4):
                mm = pe.matmul(ps[1 + hh // 2][:, hh % 2 * 192:hh % 2 * 192 + 192].rearrange("p (t n) -> p t n", t=TT), wsT[:, hh, :],
                               vh[:, :, hh * GW:(hh + 1) * GW], start=True, stop=True)
                if hh % 2 == 1:
                    mm.then_inc(s["s_raw"], 1)
            pe.wait_ge(s["a"], at("a", l))
            pe.wait_ge(s["hy"], at("hy", l))
            for c in range(2):
                for t in range(TT):
                    mm = pe.transpose(ps[3 + c][:, t * P:(t + 1) * P], uv[:, t, c * P:(c + 1) * P], ident)
                mm.then_inc(s["aT_raw"], 1)

            pe.wait_ge(s["mla_n"], at("mla_n", l))
            pe.wait_ge(s["cache_in"], 32 * (l + 1))
            for c in range(2):
                for t in range(TT):
                    mm = pe.transpose(ps[6 + c][:, t * P:(t + 1) * P], mla[:, t, c * P:(c + 1) * P], ident)
                mm.then_inc(s["latT_raw"], 1)
            for t in range(4):
                mm = pe.transpose(ps[0][:, t * P:(t + 1) * P], mla[:, t, 256:384] if t < TT else cckv, ident)
            mm.then_inc(s["latT_raw"], 1)
            for t in range(4):
                mm = pe.transpose(ps[5][0:QK, t * P:(t + 1) * P], kpeb[:, t, :], ident)
            mm.then_inc(s["latT_raw"], 1)

            pe.wait_ge(s["zc"], at("zc", l))
            pe.wait_ge(s["aT"], at("aT", l))
            pe.wait_ge(s["latT"], at("latT", l))
            for o in range(2):
                if o == 1:
                    pe.wait_ge(s["yc"], at("yc", l, 2))
                for t in range(TT):
                    for c in range(2):
                        mm = pe.transpose(ps[t // 2][:, t % 2 * 256 + c * P:t % 2 * 256 + c * P + P],
                                          zc[:, 4 + c, t * P:(t + 1) * P], ident)
                    if t > 0:
                        mm.then_inc(s["ut_raw"], 1)
                pe.wait_ge(s["ut"], at("ut", l, 2 * o + 2))
                for b in range(3):
                    tiles = (0,) if b == 0 else (1, 2)
                    for part, (m_ctx, m_lat) in enumerate(((G_C, F_C), (G_S, F_S))):
                        for i, t in enumerate(tiles):
                            q = m_ctx if b == 0 else m_lat + i * 256 + (b - 1) * P
                            mm = pe.matmul(ps[2 + b][:, part * 256:part * 256 + 256], dft[:, q:q + P], utok[:, t, :],
                                           start=(i == 0), stop=(i == len(tiles) - 1))
                    mm.then_inc(s["uf_raw"], 1)
                for c in range(2):
                    pe.wait_ge(s["yf"], at("yf", l, 3 * o + 3))
                    for b in range(3):
                        for part, (m_ctx, m_lat) in enumerate(((G_CT, F_CT), (G_ST, F_ST))):
                            cols = slice(0, P) if b == 0 else slice(P, TOK)
                            q = slice(m_ctx, m_ctx + P) if b == 0 else slice(m_lat + (b - 1) * 256, m_lat + b * 256)
                            mm = pe.matmul(ps[5 + c][:, cols], yfre[:, b, part, c * P:(c + 1) * P], dft[:, q],
                                           start=(b < 2 and part == 0), stop=(b in (0, 2) and part == 1))
                    mm.then_inc(s["yc_raw"], 1)

            pe.wait_ge(s["wuq_sw"], at("wuq_sw", l))
            pe.wait_ge(s["yc"], at("yc", l))
            for hh in range(HEADS):
                b = 2 * (hh % 2)
                if hh >= 2:
                    pe.wait_ge(s["q_pe"], at("q_pe", l, hh - 1))
                    pe.wait_ge(s["q_nope"], at("q_nope", l, hh - 1))
                for c in range(2):
                    pe.matmul(ps[b][0:QK, 0:TOK], wuq[:, c, hh * QK:(hh + 1) * QK], cqT[:, c, :],
                              start=(c == 0), stop=(c == 1))
                for c in range(2):
                    mm = pe.matmul(ps[b + 1][64:96, 0:LAT], wuq_sw[:, c, hh * ROPE:(hh + 1) * ROPE], cqT[:, c, P:TOK],
                                   start=(c == 0), stop=(c == 1))
                mm.then_inc(s["q_raw"], 1)
            for g in range(4):
                if g >= 2:
                    pe.wait_ge(s["kT"], at("kT", l, g - 1))
                for i in range(2):
                    hh = 2 * g + i
                    mm = pe.matmul(ps[4 + 2 * (g % 2) + i][0:64, :], wukv[:, hh * P:hh * P + 64], ckvT,
                                   start=True, stop=True)
                mm.then_inc(s["k_raw"], 1)
            pe.wait_ge(s["q_pe"], at("q_pe", l))
            pe.wait_ge(s["q_nope"], at("q_nope", l))
            wv = wukv[:].rearrange("p (h n) -> p h n", n=P)[:, :, 64:128]
            for t in range(4):
                pe.matmul(ps[t][:, :], ckvT[:, t * P:(t + 1) * P], wv, start=True, stop=True).then_inc(s["v_raw"], 1)

            pe.wait_ge(s["v"], at("v", l))
            pe.wait_ge(s["kT"], at("kT", l))

            def scores(hh):
                b = 2 * (hh % 2)
                if hh >= 2:
                    pe.wait_ge(s["pexp"], at("pexp", l, hh - 1))
                pe.matmul(ps[b][:, 0:384], qT[0:QK, hh, P:2 * P], kT[0:QK, hh, P:KEYS], start=True, stop=True)
                pe.matmul(ps[b][:, 384:512], qT[0:QK, hh, 0:P], kT[0:QK, hh, 0:P], start=True, stop=True)
                pe.matmul(ps[b + 1][:, 0:384], qT[0:QK, hh, 2 * P:3 * P], kT[0:QK, hh, P:KEYS],
                          start=True, stop=True).then_inc(s["sc_raw"], 1)

            scores(0)
            for hh in range(HEADS):
                if hh + 1 < HEADS:
                    scores(hh + 1)
                pe.wait_ge(s["pn"], at("pn", l, hh + 1))
                if hh > 0:
                    pe.wait_ge(s["pT"], at("pT", l, 2 * hh - 1))
                for i, o in enumerate((0, 512, 384)):
                    mm = pe.transpose(ps[4][:, i * P:(i + 1) * P], probs[:, o:o + P], ident)
                mm.then_inc(s["pT_raw"], 1)
                if hh > 0:
                    pe.wait_ge(s["pT"], at("pT", l, 2 * hh))
                for i, o in enumerate((P, 512 + P, 2 * P, 512 + 2 * P)):
                    mm = pe.transpose(ps[5][:, i * P:(i + 1) * P], probs[:, o:o + P], ident)
                mm.then_inc(s["pT_raw"], 1)
                pe.wait_ge(s["pT"], at("pT", l, 2 * hh + 2))
                if hh % 2 == 0 and hh >= 4:
                    pe.wait_ge(s["oT"], at("oT", l, hh // 2 - 1))
                r = slice(64 * (hh % 2), 64 * (hh % 2) + 64)
                ob = ps[6 + hh // 2 % 2]
                pe.matmul(ob[r, 0:P], v_sb[:, 0, hh * GW:(hh + 1) * GW], probsT[:, 2, :], start=True, stop=True)
                for i in range(3):
                    rhs = probsT[:, (0, 3, 5)[i]:(0, 3, 5)[i] + 2, :].rearrange("p b n -> p (b n)")
                    mm = pe.matmul(ob[r, P:TOK], v_sb[:, 1 + i, hh * GW:(hh + 1) * GW], rhs,
                                   start=(i == 0), stop=(i == 2))
                mm.then_inc(s["pv"], 1)

            pe.wait_ge(s["oT"], at("oT", l))
            pe.wait_ge(s["pexp"], at("pexp", l))
            for c in range(4):
                w = loaded(8 + c).rearrange("p (k n) -> p k n", k=2)
                for t in range(TT):
                    for half in range(2):
                        for k in range(2):
                            mm = pe.matmul(ps[2 * t + half][:, :], act_t[:, 2 * c + k, t * P:(t + 1) * P],
                                           w[:, k, half * 512:(half + 1) * 512],
                                           start=(c == 0 and k == 0), stop=(c == 3 and k == 1))
                mm.then_inc(s["chunk_done"], 1)

            pe.wait_ge(s["h2"], at("h2", l))
            for k in range(K8):
                if k >= 6:
                    pe.wait_ge(s["h2T"], at("h2T", l, k - 5))
                for t in range(TT):
                    mm = pe.transpose(ps[k % 6][:, t * P:(t + 1) * P], h[:, t, k:D:K8], ident)
                mm.then_inc(s["h2T_raw"], 1)
            pe.wait_ge(s["h2T"], at("h2T", l))
            for t in range(TT):
                for k in range(K8):
                    mm = pe.matmul(ps[6][:, t * 36:(t + 1) * 36], act_t[:, k, t * P:(t + 1) * P], wr[:, k, :],
                                   start=(k == 0), stop=(k == K8 - 1))
            mm.then_inc(s["lg_raw"], 1)
            pe.wait_ge(s["oh"], at("oh", l))
            oh = rt[:, 0:12].rearrange("p (t g) -> p t g", t=TT)
            for t in range(TT):
                for i in range(t + 1):
                    pe.matmul(ps[7][:, t * 4:t * 4 + 4], tri if i == t else ones, oh[:, i, :],
                              start=(i == 0), stop=(i == t))
            for i in range(TT):
                mm = pe.matmul(ps[7][:, 12:16], ones, oh[:, i, :], start=(i == 0), stop=(i == 2))
            mm.then_inc(s["cum_raw"], 1)
            pe.wait_ge(s["tgt"], at("tgt", l))
            pe.wait_ge(s["regs"], at("regs", l))
            extra = pe.value_load(xi[0:1, 0:1], min_val=0, max_val=EXTRA)

            dw = rt[:, 12:36].rearrange("p (t n) -> p t n", t=TT)

            def visit(slot, e, full, done, n_visit, chunk0):
                pe.wait_ge(e["sel"], n_visit + 1)
                for half in range(2):
                    for k in range(4 * half, 4 * half + 4):
                        for t in range(TT):
                            mm = pe.matmul(ps[2 + half][:, k % 4 * P:k % 4 * P + P], h[:, t, k:D:K8], sel[:, t, :],
                                           start=(t == 0), stop=(t == TT - 1))
                    mm.then_inc(e["xT_raw"], 1)
                if n_visit > 0:
                    pe.wait_ge(e["acc"], TT * n_visit)
                for t in range(TT):
                    pe.matmul(ps[6][:, 384:392], sel[:, t, :], dw[:, t, :], start=(t == 0), stop=(t == TT - 1))
                for t in range(TT):
                    mm = pe.transpose(ps[6][:, t * P:(t + 1) * P], sel[:, t, :], ident)
                mm.then_inc(e["xT_raw"], 1)
                pe.wait_ge(e["xT"], 3 * (n_visit + 1))
                q0 = n_visit * EPG

                def full_at(kind, ex, loop):
                    i = pos(kind, ex)
                    pe.wait_ge(full[i % RING], loop * 16 + 16 * ((chunk0 + i) // RING + 1))
                    return ring[:, i % RING, :]

                def gate_up(ex, loop=0):
                    j = ex % 2
                    if n_visit > 0 or ex >= 2:
                        pe.wait_ge(e["hid_e"], loop * 2 + (q0 + ex - 1))
                    for half, kind in enumerate("GU"):
                        w = full_at(kind, ex, loop).rearrange("p (k n) -> p k n", k=K8)
                        for k in range(K8):
                            mm = pe.matmul(ps[j][:, half * FF:(half + 1) * FF], xT[:, slot, k, :], w[:, k, :],
                                           start=(k == 0), stop=(k == K8 - 1))
                        mm.then_inc(done, 1)

                def down(ex, loop=0, first=False, last=False):
                    j = ex % 2
                    pe.wait_ge(e["hid_e"], loop * 2 + (q0 + ex + 1))
                    if n_visit > 0 or ex >= 1:
                        pe.wait_ge(e["hidT"], loop * 2 + (q0 + ex))
                    for k in range(2):
                        mm = pe.transpose(ps[2][:, k * P:(k + 1) * P], hd[:, j, k:FF:2], ident)
                    mm.then_inc(e["hidT_raw"], 1)
                    w = full_at("D", ex, loop).rearrange("p (k n) -> p k n", k=2)
                    pe.wait_ge(e["hidT"], loop * 2 + (q0 + ex + 1))
                    for k in range(2):
                        for half in range(2):
                            mm = pe.matmul(ps[4 + half][:, :], hdT[:, j, k * P:(k + 1) * P],
                                           w[:, k, half * 512:(half + 1) * 512],
                                           start=(first and k == 0), stop=(last and k == 1), skip_group_check=True)
                    mm.then_inc(done, 1)

                gate_up(0)
                gate_up(1)
                down(0, first=True)
                gate_up(2)
                down(1)
                with pe.Fori(0, 2) as it:
                    gate_up(3, it)
                    down(2, it)
                    gate_up(4, it)
                    down(3, it)
                gate_up(7)
                down(6)
                down(7, last=True)
                pe.wait_ge(e["y"], 2 * (n_visit + 1))
                for t in range(TT):
                    if t > 0 or n_visit > 0:
                        pe.wait_ge(e["acc"], TT * n_visit + t)
                    for half in range(2):
                        mm = pe.matmul(ps[6 + half][:, :], selT[:, slot, t, :], y_sb[:, half * 512:(half + 1) * 512],
                                       start=True, stop=True)
                    mm.then_inc(e["sct"], 1)

            for v in range(GROUPS):
                visit(v, e_main, ring_full, s["chunk_done"], l * GROUPS + v, n0 + MIX_CHUNKS + v * EPG * 3)
            with pe.If(extra >= 1):
                pe.wait_ge(e_main["acc"], TT * GROUPS * (l + 1))
                visit(0, e_extra[l], x_full[l], e_extra[l]["chunk_done"], 0, 0)
                with pe.If(extra >= 2):
                    visit(1, e_extra[l], x_full[l], e_extra[l]["chunk_done"], 1, EPG * 3)

    @block.scalar
    def _(act):
        act.wait_ge(s["cond_in"], 32)
        act.wait_ge(s["cT"], 1)
        act.activation(cT[:, :, 0:2], craw.rearrange("p c k -> p k c"), ACT.Silu).then_inc(s["cT"], 1)
        for t in range(TT):
            act.wait_ge(s["x0_var"], t + 1)
            act.activation(st[:, 64 + t:65 + t], st[:, 60 + t:61 + t], ACT.Sqrt).then_inc(s["x0_std"], 1)
        for l in range(DEPTH):
            for b in range(3):
                act.wait_ge(s["mod_sum"], 3 * l + b + 1)
                for j in range(4):
                    for c in range(2):
                        dst = mod_dram[l, c:c + 1].rearrange("a (b j n) -> a b j n", j=4, n=64)[:, 8 * b:8 * b + 8, j, :]
                        src = region_a[32 * j + c:32 * j + c + 1, l * 1536 + b * 512:l * 1536 + b * 512 + 512]
                        act.dma_start(dst, src.rearrange("p (b n) -> p b n", n=64)).then_inc(s["mod_out"], 16)

        for l in range(DEPTH):
            for i, dst in enumerate((hid1, hid2)):
                act.wait_ge(s["sin_in"], at("sin_in", l, i + 1))
                act.activation(dst, f_arg, ACT.Sin).then_inc(s["hid"], 1)
            for b in range(3):
                act.wait_ge(s["spec_raw"], at("spec_raw", l, b + 1))
                act.activation(spec[:, b, 0, :], ps[2 * b][:, :], ACT.Copy)
                act.activation(spec[:, b, 1, :], ps[2 * b + 1][:, :], ACT.Copy).then_inc(s["spec"], 1)
            for k in range(K8):
                act.wait_ge(s["hT_raw"], at("hT_raw", l, k + 1))
                act.activation(act_t[:, k, :], ps[k % 6][:, 0:TOK], ACT.Copy).then_inc(s["hT"], 1)
            act.wait_ge(s["chunk_done"], first_chunk(l) + 2)
            for t in range(TT):
                act.activation(uv[:, t, :], ps[t][:, :], ACT.Gelu_apprx_tanh).then_inc(s["uv"], 1)
            for c in range(6):
                act.wait_ge(s["chunk_done"], first_chunk(l) + 3 + c // 2)
                bank = ps[3 + c % 4]
                act.activation(hy[:, c, 1:1 + P], bank[:, 0:P], ACT.Copy)
                mm = act.activation(hy[:, c, 2 + P:2 + TOK], bank[:, P:TOK], ACT.Copy)
                if c % 2 == 1:
                    mm.then_inc(s["hy"], 1)
            act.wait_ge(s["chunk_done"], first_chunk(l) + 8)
            for t in range(TT):
                act.activation(mla[:, t, :], ps[(7, 0, 1)[t]][:, 0:MLA_COLS], ACT.Copy).then_inc(s["mla"], 1)
            act.wait_ge(s["mla"], at("mla", l))
            for t in range(TT):
                act.activation(region_k[:, t * 384:t * 384 + 256], mla[:, t, 0:256], ACT.Square, accum_out=st[:, 48 + t:49 + t])
            for t in range(TT):
                mm = act.activation(region_k[:, t * 384 + 256:t * 384 + 384], mla[:, t, 256:384], ACT.Square, accum_out=st[:, 51 + t:52 + t])
            mm.then_inc(s["rms_ss"], 1)
            act.wait_ge(s["gm_var"], at("gm_var", l))
            act.activation(st[:, 12:24], st[:, 0:12], ACT.Sqrt).then_inc(s["gm_std"], 1)
            act.wait_ge(s["rms_var"], at("rms_var", l))
            act.activation(st[:, 54:60], st[:, 48:54], ACT.Sqrt).then_inc(s["rms_std"], 1)
            for c in range(2):
                act.wait_ge(s["aT_raw"], at("aT_raw", l, c + 1))
                act.activation(act_t[:, c, :], ps[3 + c][:, 0:TOK], ACT.Copy).then_inc(s["aT"], 1)
            for c in range(2):
                act.wait_ge(s["latT_raw"], at("latT_raw", l, c + 1))
                act.activation(cqT[:, c, :], ps[6 + c][:, 0:TOK], ACT.Copy).then_inc(s["latT"], 1)
            act.wait_ge(s["latT_raw"], at("latT_raw", l, 3))
            act.activation(ckvT, ps[0][:, :], ACT.Copy).then_inc(s["latT"], 1)
            act.wait_ge(s["latT_raw"], at("latT_raw", l, 4))
            for hh in range(HEADS):
                mm = act.activation(kT[64:96, hh, :], ps[5][64:96, :], ACT.Copy)
            mm.then_inc(s["latT"], 1)
            for o in range(2):
                act.wait_ge(s["ut_raw"], at("ut_raw", l, 2 * o + 1))
                act.activation(utok[:, 0:2, :].rearrange("p t n -> p (t n)"), ps[0][:, :], ACT.Copy).then_inc(s["ut"], 1)
                act.wait_ge(s["ut_raw"], at("ut_raw", l, 2 * o + 2))
                act.activation(utok[:, 2, :], ps[1][:, 0:256], ACT.Copy).then_inc(s["ut"], 1)
            for hh in range(HEADS):
                b = 2 * (hh % 2)
                act.wait_ge(s["q_raw"], at("q_raw", l, hh + 1))
                act.activation(qT[0:QK, hh, 0:P], ps[b][0:QK, 0:P], ACT.Copy)
                act.activation(qT[0:64, hh, P:TOK], ps[b][0:64, P:TOK], ACT.Copy).then_inc(s["q_nope"], 1)
            for g in range(4):
                act.wait_ge(s["k_raw"], at("k_raw", l, g + 1))
                act.activation(kT[0:64, 2 * g, :], ps[4 + 2 * (g % 2)][0:64, :], ACT.Copy)
                act.activation(kT[0:64, 2 * g + 1, :], ps[5 + 2 * (g % 2)][0:64, :], ACT.Copy).then_inc(s["kT"], 1)
            for t in range(4):
                act.wait_ge(s["v_raw"], at("v_raw", l, t + 1))
                act.activation(v_sb[:, t, :], ps[t][:, :], ACT.Copy).then_inc(s["v"], 1)
            for hh in range(HEADS):
                b = 2 * (hh % 2)
                act.wait_ge(s["mx"], at("mx", l, hh + 1))
                if hh > 0:
                    act.wait_ge(s["pT_raw"], at("pT_raw", l, 2 * hh))
                for i, (src, dst) in enumerate(((ps[b][:, 0:384], probs[:, 0:384]),
                                                (ps[b][:, 384:512], probs[:, 384:512]),
                                                (ps[b + 1][:, 0:384], probs[:, 512:896]))):
                    mm = act.activation(dst, src, ACT.Exp, bias=st[:, 36 + i:37 + i], scale=QK_SCALE,
                                        accum_out=st[:, 39 + i:40 + i])
                mm.then_inc(s["pexp"], 1)
                act.wait_ge(s["pT_raw"], at("pT_raw", l, 2 * hh + 1))
                if hh > 0:
                    act.wait_ge(s["pv"], at("pv", l, hh))
                act.activation(probsT[:, 0:3, :], ps[4][:, 0:384].rearrange("p (b n) -> p b n", b=3), ACT.Copy)\
                    .then_inc(s["pT"], 1)
                act.wait_ge(s["pT_raw"], at("pT_raw", l, 2 * hh + 2))
                act.activation(probsT[:, 3:7, :], ps[5][:, :].rearrange("p (b n) -> p b n", b=4), ACT.Copy)\
                    .then_inc(s["pT"], 1)
                if hh % 2 == 1:
                    act.wait_ge(s["pv"], at("pv", l, hh + 1))
                    act.activation(act_t[:, 4 + hh // 2, :], ps[6 + hh // 2 % 2][:, 0:TOK], ACT.Copy)\
                        .then_inc(s["oT"], 1)
            for t in range(TT):
                act.wait_ge(s["ln1_var"], at("ln1_var", l, t + 1))
                act.activation(st[:, 64 + t:65 + t], st[:, 60 + t:61 + t], ACT.Sqrt).then_inc(s["ln1_std"], 1)
            for k in range(K8):
                act.wait_ge(s["h2T_raw"], at("h2T_raw", l, k + 1))
                act.activation(act_t[:, k, :], ps[k % 6][:, 0:TOK], ACT.Copy).then_inc(s["h2T"], 1)
            act.wait_ge(s["lg_sh"], at("lg_sh", l))
            act.activation(rt[:, 300:315], rt[:, 280:295], ACT.Exp).then_inc(s["lg_exp"], 1)
            act.wait_ge(s["regs"], at("regs", l))
            extra = act.value_load(xi[0:1, 0:1], min_val=0, max_val=EXTRA)

            def visit(v, slot, e, done, n_visit, chunk0):
                for half in range(2):
                    act.wait_ge(e["xT_raw"], 3 * n_visit + half + 1)
                    act.activation(xT[:, slot, 4 * half:4 * half + 4, :],
                                   ps[2 + half][:, :].rearrange("p (k n) -> p k n", k=4), ACT.Copy).then_inc(e["xT"], 1)
                act.wait_ge(e["xT_raw"], 3 * n_visit + 3)
                act.activation(selT[:, slot, :, :], ps[6][:, 0:384].rearrange("p (t n) -> p t n", t=TT), ACT.Copy)
                act.activation(wslot[:, v, :], ps[6][:, 384:392], ACT.Copy).then_inc(e["xT"], 1)
                q0 = n_visit * EPG

                def silu(ex, loop=0):
                    act.wait_ge(done, loop * 6 + (chunk0 + pos("U", ex) + 1))
                    if n_visit > 0 or ex >= 2:
                        act.wait_ge(e["hid_e"], loop * 2 + (q0 + ex - 1))
                    act.activation(sg[:, ex % 2, :], ps[ex % 2][:, 0:FF], ACT.Silu).then_inc(e["silu"], 1)

                def turned(ex, loop=0):
                    act.wait_ge(e["hidT_raw"], loop * 2 + (q0 + ex + 1))
                    act.activation(hdT[:, ex % 2, :], ps[2][:, 0:FF], ACT.Copy).then_inc(e["hidT"], 1)

                silu(0)
                with act.Fori(0, 3) as it:
                    silu(1, it)
                    turned(0, it)
                    silu(2, it)
                    turned(1, it)
                silu(7)
                turned(6)
                turned(7)
                act.wait_ge(done, chunk0 + EPG * 3)
                for half in range(2):
                    act.activation(y_sb[:, half * 512:(half + 1) * 512], ps[4 + half][:, :], ACT.Copy)\
                        .then_inc(e["y"], 1)

            for v in range(GROUPS):
                visit(v, v, e_main, s["chunk_done"], l * GROUPS + v, first_chunk(l) + MIX_CHUNKS + v * EPG * 3)
            with act.If(extra >= 1):
                visit(4, 0, e_extra[l], e_extra[l]["chunk_done"], 0, 0)
                with act.If(extra >= 2):
                    visit(5, 1, e_extra[l], e_extra[l]["chunk_done"], 1, EPG * 3)
            for t in range(TT):
                act.wait_ge(s["ln2_var"], at("ln2_var", l, t + 1))
                act.activation(st[:, 64 + t:65 + t], st[:, 60 + t:61 + t], ACT.Sqrt).then_inc(s["ln2_std"], 1)

    @block.vector
    def _(dve):
        steps = [0]

        def link(ins):
            steps[0] += 1
            ins.then_inc(s["dve_step"], 1)
            dve.wait_ge(s["dve_step"], steps[0])

        lnst = st[:, 80:94]

        def layer_norm(t, var, std, done, base):
            xt = x[:, t, :]
            dve.bn_stats(lnst[:, 0:6], xt[:, 0:512])
            link(dve.bn_stats(lnst[:, 6:12], xt[:, 512:1024]))
            link(dve.bn_aggr(lnst[:, 12:14], lnst[:, 0:12]))
            dve.tensor_scalar(st[:, 60 + t:61 + t], lnst[:, 13:14], LN_EPS, None, ALU.add).then_inc(s[var], 1)
            dve.wait_ge(s[std], base + t + 1)
            link(dve.reciprocal(st[:, 68:69], st[:, 64 + t:65 + t]))
            link(dve.tensor_scalar(xt, xt, lnst[:, 12:13], st[:, 68:69], ALU.subtract, ALU.mult))
            link(dve.tensor_tensor(xt, xt, lnr[:, 0, :], ALU.mult))
            dve.tensor_tensor(xt, xt, lnr[:, 1, :], ALU.add).then_inc(s[done], 1)

        def modulate(l, n_loads, done):
            dve.wait_ge(s["mod12_in"], 64 * n_loads)
            for t in range(TT):
                c = min(t, 1)
                link(dve.scalar_tensor_tensor(h[:, t, :], modr[:, 2 * c + 1, :], 1.0, x[:, t, :], ALU.add, ALU.mult))
                dve.tensor_tensor(h[:, t, :], h[:, t, :], modr[:, 2 * c, :], ALU.add).then_inc(s[done], 1)

        def wide(ap, shape):
            return ap.to_broadcast(shape)

        dve.memset(cT, 0.0).then_inc(s["cT"], 1)
        dve.memset(region_a[:, 0:3072], 0.0).then_inc(s["mod_zero"], 1)
        link(dve.memset(xi[:], 0))
        dve.wait_ge(s["x_in"], 16 * TT)
        dve.wait_ge(s["ln_in"], 32)
        for t in range(TT):
            layer_norm(t, "x0_var", "x0_std", "x0", 0)
        dve.wait_ge(s["bmod_in"], 16 * 8 * DEPTH)
        dve.wait_ge(s["mod_zero"], 1)
        for i in range(3 * DEPTH):
            dve.wait_ge(s["chunk_done"], 8 * (i + 1))
            sums = region_a[:, i * 512:(i + 1) * 512]
            dve.tensor_tensor(sums, sums, ps[i % 2][:, :], ALU.add).then_inc(s["mod_sum"], 1)

        for l in range(DEPTH):
            dve.wait_ge(s["small_in"], 16 * SMALL_LOADS * (l + 1))
            for i in range(2):
                if i == 0:
                    dve.wait_ge(s["filt_in"], at("filt_in", l))
                else:
                    dve.wait_ge(s["hid_in"], at("hid_in", l))
                link(dve.tensor_scalar(f_arg, ps[i][0:FH, 0:TOK], fw[:, 128 + i:129 + i], fw[:, 130 + i:131 + i],
                                       ALU.add, ALU.mult))
                link(dve.tensor_scalar(f_n, f_arg, 0.5 / math.pi, MAGIC, ALU.mult, ALU.add))
                link(dve.tensor_scalar(f_n, f_n, MAGIC, None, ALU.subtract))
                link(dve.scalar_tensor_tensor(f_arg, f_n, -TWO_PI_HI, f_arg, ALU.mult, ALU.add))
                link(dve.scalar_tensor_tensor(f_arg, f_n, -TWO_PI_LO, f_arg, ALU.mult, ALU.add))
                dve.tensor_scalar(f_arg, f_arg, PI_SAFE, -PI_SAFE, ALU.min, ALU.max).then_inc(s["sin_in"], 1)
            for t in range(TT):
                for o in range(2):
                    dve.wait_ge(s["filt_raw"], at("filt_raw", l, 2 * t + o + 1))
                    raw = ps[2 * t + o]
                    dve.tensor_tensor(f_tmp[:, 0:CH], raw[:, 0:CH], decay[:, t, :], ALU.mult)
                    link(dve.scalar_tensor_tensor(f_tmp[:, CH:2 * CH], raw[:, CH:2 * CH], cst[:, C_MASK + t:C_MASK + t + 1],
                                                  decay[:, t, :], ALU.mult, ALU.mult))
                    dve.tensor_tensor(f_sum[:, t, o * CH:(o + 1) * CH], f_tmp[:, 0:CH], f_tmp[:, CH:2 * CH], ALU.add)
                    last = dve.tensor_tensor(f_dif[:, t, o * CH:(o + 1) * CH], f_tmp[:, 0:CH], f_tmp[:, CH:2 * CH],
                                             ALU.subtract)
                    if o == 0:
                        link(last)
                    else:
                        last.then_inc(s["filt_eo"], 1)
                        dve.wait_ge(s["filt_eo"], at("filt_eo", l, t + 1))
            for c in range(2):
                pe_cols = wuq[:, c, :].rearrange("p (h n) -> p h n", n=QK)
                sw = wuq_sw[:, c, :].rearrange("p (h n) -> p h n", n=ROPE)
                dve.tensor_copy(sw[:, :, 0:ROPE:2], pe_cols[:, :, 65:QK:2])
                last = dve.tensor_copy(sw[:, :, 1:ROPE:2], pe_cols[:, :, 64:QK:2])
            last.then_inc(s["wuq_sw"], 1)
            for col in (0, 1 + P, 2 + TOK):
                link(dve.memset(hy[:, :, col:col + 1], 0.0))

            if l > 0:
                dve.wait_ge(s["x2"], at("x2", l - 1))
            else:
                dve.wait_ge(s["x0"], TT)
            modulate(l, 2 * l + 1, "h")
            dve.wait_ge(s["h"], at("h", l))
            link(dve.memset(kpeb[:, :, 0:64], 0.0))

            v4 = uv[:, :, CH:2 * CH].rearrange("p t (h d) -> p t h d", h=4)
            vh4 = vh.rearrange("p t (h d) -> p t h d", h=4)
            sq4 = utok[:].rearrange("p t (h d) -> p t h d", h=4)

            def per_head(c):
                return st[:, c:c + 12].rearrange("p (t h) -> p t h", t=TT)

            dve.wait_ge(s["uv"], at("uv", l))
            link(dve.tensor_reduce(per_head(0), v4, AX.X, ALU.add))
            link(dve.tensor_scalar(st[:, 0:12], st[:, 0:12], 1.0 / GW, None, ALU.mult))
            link(dve.tensor_tensor(vh4, v4, per_head(0).unsqueeze(3).to_broadcast([P, TT, 4, GW]), ALU.subtract))
            link(dve.tensor_tensor(sq4, vh4, vh4, ALU.mult))
            link(dve.tensor_reduce(per_head(0), sq4, AX.X, ALU.add))
            dve.tensor_scalar(st[:, 0:12], st[:, 0:12], 1.0 / GW, LN_EPS, ALU.mult, ALU.add).then_inc(s["gm_var"], 1)

            dve.wait_ge(s["rms_ss"], at("rms_ss", l))
            dve.tensor_scalar(st[:, 48:51], st[:, 48:51], 1.0 / 256, RMS_EPS, ALU.mult, ALU.add)
            dve.tensor_scalar(st[:, 51:54], st[:, 51:54], 1.0 / 128, RMS_EPS, ALU.mult, ALU.add).then_inc(s["rms_var"], 1)

            dve.wait_ge(s["gm_std"], at("gm_std", l))
            link(dve.reciprocal(st[:, 24:36], st[:, 12:24]))
            link(dve.tensor_tensor(vh4, vh4, per_head(24).unsqueeze(3).to_broadcast([P, TT, 4, GW]), ALU.mult))
            link(dve.tensor_tensor(vh, vh, rows[:, 0:256].unsqueeze(1).to_broadcast([P, TT, 256]), ALU.mult))
            dve.tensor_tensor(vh, vh, rows[:, 256:512].unsqueeze(1).to_broadcast([P, TT, 256]), ALU.add)\
                .then_inc(s["vh"], 1)

            dve.wait_ge(s["rms_std"], at("rms_std", l))
            dve.wait_ge(s["mla"], at("mla", l))
            link(dve.reciprocal(st[:, 70:76], st[:, 54:60]))
            for t in range(TT):
                cq, ckv = mla[:, t, 0:256], mla[:, t, 256:384]
                dve.scalar_tensor_tensor(cq, cq, st[:, 70 + t:71 + t], rows[:, 512:768], ALU.mult, ALU.mult)
                dve.scalar_tensor_tensor(ckv, ckv, st[:, 73 + t:74 + t], rows[:, 768:896], ALU.mult, ALU.mult)
            pe2 = mla[:, 1:3, 384:416]
            cos = cst[:, C_COS:C_COS + 64].rearrange("p (t n) -> p t n", t=2)
            sin = cst[:, C_SIN:C_SIN + 64].rearrange("p (t n) -> p t n", t=2)
            turn = rt[:, 200:264].rearrange("p (t n) -> p t n", t=2)
            dve.tensor_copy(kpeb[:, 0, 64:96], mla[:, 0, 384:416])
            dve.tensor_tensor(kpeb[:, 1:3, 64:96], pe2, cos, ALU.mult)
            dve.tensor_tensor(turn[:, :, 0:ROPE:2], pe2[:, :, 1:ROPE:2], sin[:, :, 0:ROPE:2], ALU.mult)
            link(dve.tensor_tensor(turn[:, :, 1:ROPE:2], pe2[:, :, 0:ROPE:2], sin[:, :, 1:ROPE:2], ALU.mult))
            dve.tensor_tensor(kpeb[:, 1:3, 64:96], kpeb[:, 1:3, 64:96], turn, ALU.add).then_inc(s["mla_n"], 1)

            for hh in range(4):
                if hh % 2 == 0:
                    dve.wait_ge(s["s_raw"], at("s_raw", l, hh // 2 + 1))
                mixed = ps[1 + hh // 2][:, hh % 2 * 192:hh % 2 * 192 + 192].rearrange("p (t n) -> p t n", t=TT)
                u = uv[:, :, hh * GW:(hh + 1) * GW]
                last = dve.scalar_tensor_tensor(u, mixed, bs_c[:, hh:hh + 1], u, ALU.add, ALU.mult)
            last.then_inc(s["a"], 1)

            dve.wait_ge(s["hT_raw"], at("hT_raw", l))
            for c in range(6):
                dve.wait_ge(s["hy"], at("hy", l, c // 2 + 1))
                for o, i, n in ((0, 0, P), (P, P + 1, LAT)):
                    link(dve.tensor_scalar(zc[:, c, o:o + n], hy[:, c, i + 1:i + 1 + n], cw[:, 1, c:c + 1],
                                           cw[:, 3, c:c + 1], ALU.mult, ALU.add))
                    link(dve.scalar_tensor_tensor(zc[:, c, o:o + n], hy[:, c, i:i + n], cw[:, 0, c:c + 1],
                                                  zc[:, c, o:o + n], ALU.mult, ALU.add))
                    last = dve.scalar_tensor_tensor(zc[:, c, o:o + n], hy[:, c, i + 2:i + 2 + n], cw[:, 2, c:c + 1],
                                                    zc[:, c, o:o + n], ALU.mult, ALU.add)
                last.then_inc(s["zc"], 1)
            dve.wait_ge(s["zc"], at("zc", l))
            for o in range(2):
                for b in range(3):
                    dve.wait_ge(s["uf_raw"], at("uf_raw", l, 3 * o + b + 1))
                    uc, us = ps[2 + b][:, 0:CH], ps[2 + b][:, CH:2 * CH]
                    hc, hs = spec[:, b, 0, o * CH:(o + 1) * CH], spec[:, b, 1, o * CH:(o + 1) * CH]
                    for part, (f, g, op) in enumerate(((hc, hs, ALU.subtract), (hs, hc, ALU.add))):
                        dve.tensor_tensor(ytmp[:, 0:CH], uc, f, ALU.mult)
                        link(dve.tensor_tensor(ytmp[:, CH:2 * CH], us, g, ALU.mult))
                        last = dve.tensor_tensor(yfre[:, b, part, :], ytmp[:, 0:CH], ytmp[:, CH:2 * CH], op)
                        if part == 0:
                            link(last)
                    last.then_inc(s["yf"], 1)
                    dve.wait_ge(s["yf"], at("yf", l, 3 * o + b + 1))
                for c in range(2):
                    dve.wait_ge(s["yc_raw"], at("yc_raw", l, 2 * o + c + 1))
                    cur = zc[:, 4 + c, :]
                    link(dve.scalar_tensor_tensor(cur, cur, hyb[:, o, c:c + 1], ps[5 + c][:, 0:TOK], ALU.mult, ALU.add))
                    dst = cur if o == 0 else act_t[:, 2 + c, :]
                    dve.tensor_tensor(dst, cur, zc[:, 2 * o + c, :], ALU.mult).then_inc(s["yc"], 1)
                dve.wait_ge(s["yc"], at("yc", l, 2 * o + 2))

            for hh in range(HEADS):
                b = 2 * (hh % 2)
                dve.wait_ge(s["q_raw"], at("q_raw", l, hh + 1))
                dve.wait_ge(s["q_nope"], at("q_nope", l, hh + 1))
                dst = qT[64:96, hh, P:TOK]
                dve.tensor_tensor(qtmp[64:96, :], ps[b][64:96, P:TOK], ropeT[64:96, 0, :], ALU.mult)
                link(dve.tensor_tensor(dst, ps[b + 1][64:96, 0:LAT], ropeT[64:96, 1, :], ALU.mult))
                dve.tensor_tensor(dst, dst, qtmp[64:96, :], ALU.add).then_inc(s["q_pe"], 1)
                dve.wait_ge(s["q_pe"], at("q_pe", l, hh + 1))
            for hh in range(HEADS):
                b = 2 * (hh % 2)
                dve.wait_ge(s["sc_raw"], at("sc_raw", l, hh + 1))
                dve.reduce_max(st[:, 45:46], ps[b][:, 0:384], AX.X)
                dve.reduce_max(st[:, 46:47], ps[b][:, 384:512], AX.X)
                link(dve.reduce_max(st[:, 47:48], ps[b + 1][:, 0:384], AX.X))
                dve.tensor_scalar(st[:, 36:39], st[:, 45:48], -QK_SCALE, None, ALU.mult).then_inc(s["mx"], 1)
                dve.wait_ge(s["pexp"], at("pexp", l, hh + 1))
                link(dve.reciprocal(st[:, 42:45], st[:, 39:42]))
                for i, (o, n) in enumerate(((0, 384), (384, P), (512, 384))):
                    last = dve.tensor_scalar(probs[:, o:o + n], probs[:, o:o + n], st[:, 42 + i:43 + i], None, ALU.mult)
                last.then_inc(s["pn"], 1)

            dve.wait_ge(s["chunk_done"], first_chunk(l) + MIX_CHUNKS)
            dve.wait_ge(s["gate_in"], 32 * (2 * l + 1))
            dve.wait_ge(s["ln_in"], 32 * (2 * l + 2))
            for t in range(TT):
                for half in range(2):
                    cols = slice(half * 512, (half + 1) * 512)
                    last = dve.tensor_tensor(h[:, t, cols], ps[2 * t + half][:, :], modr[:, min(t, 1), cols], ALU.mult)
                link(last)
                link(dve.scalar_tensor_tensor(x[:, t, :], x[:, t, :], ALPHA, h[:, t, :], ALU.mult, ALU.add))
                layer_norm(t, "ln1_var", "ln1_std", "x1", l * 3)
            dve.wait_ge(s["x1"], at("x1", l))
            modulate(l, 2 * l + 2, "h2")

            logits = rt[:, 40:148].rearrange("p (t n) -> p t n", t=TT)

            def col3(c, n=1):
                return rt[:, c:c + 3 * n].rearrange("p (t n) -> p t n", t=TT)

            def const(c, n):
                return cst[:, c:c + n].unsqueeze(1).to_broadcast([P, TT, n])

            def first_max(values, n, c_max, c_eq, c_pri, c_pm, rank, out):
                link(dve.tensor_reduce(rt[:, c_max:c_max + 3], values, AX.X, ALU.max))
                link(dve.tensor_tensor(col3(c_eq, n), values, col3(c_max).to_broadcast([P, TT, n]), ALU.is_ge))
                link(dve.tensor_tensor(col3(c_pri, n), col3(c_eq, n), const(rank, n), ALU.mult))
                link(dve.tensor_reduce(rt[:, c_pm:c_pm + 3], col3(c_pri, n), AX.X, ALU.max))
                return dve.tensor_tensor(out, col3(c_pri, n), col3(c_pm).to_broadcast([P, TT, n]), ALU.is_equal)

            dve.wait_ge(s["lg_raw"], at("lg_raw", l))
            link(dve.tensor_tensor(logits, ps[6][:, 0:108].rearrange("p (t n) -> p t n", t=TT),
                                   rows[:, 896:932].unsqueeze(1).to_broadcast([P, TT, 36]), ALU.add))
            oh = col3(0, 4)
            first_max(logits[:, :, 0:4], 4, 150, 156, 168, 153, C_RANK, oh).then_inc(s["oh"], 1)
            dve.wait_ge(s["oh"], at("oh", l))
            dve.tensor_tensor(col3(280, 4), logits[:, :, 0:4], col3(150).to_broadcast([P, TT, 4]), ALU.subtract)
            prod = rt[:, 184:280].rearrange("p (t g e) -> p t g e", t=TT, g=4)
            for t in range(TT):
                last = dve.tensor_tensor(prod[:, t], logits[:, t, 4:36].rearrange("p (g e) -> p g e", g=4),
                                         oh[:, t, :].unsqueeze(2).to_broadcast([P, 4, 8]), ALU.mult)
            link(last)
            e_in = col3(316, 8)
            link(dve.tensor_reduce(e_in, prod.rearrange("p t g e -> p t e g"), AX.X, ALU.add))
            oh1, oh2, e_2nd = col3(344, 8), col3(392, 8), col3(368, 8)
            link(first_max(e_in, 8, 340, 184, 208, 232, C_GE, oh1))
            link(dve.scalar_tensor_tensor(e_2nd, oh1, -BIG, e_in, ALU.mult, ALU.add))
            link(first_max(e_2nd, 8, 416, 184, 208, 232, C_GE, oh2))
            dve.tensor_tensor(rt[:, 292:295], rt[:, 416:419], rt[:, 340:343], ALU.subtract).then_inc(s["lg_sh"], 1)
            dve.wait_ge(s["lg_exp"], at("lg_exp", l))
            link(dve.tensor_reduce(rt[:, 419:422], col3(300, 4), AX.X, ALU.add))
            link(dve.scalar_tensor_tensor(rt[:, 422:425], rt[:, 312:315], 1.0, rt[:, 419:422], ALU.add, ALU.mult))
            link(dve.reciprocal(rt[:, 425:428], rt[:, 422:425]))
            link(dve.tensor_tensor(rt[:, 428:431], rt[:, 425:428], rt[:, 312:315], ALU.mult))
            link(dve.tensor_tensor(oh1, oh1, col3(425).to_broadcast([P, TT, 8]), ALU.mult))
            link(dve.tensor_tensor(oh2, oh2, col3(428).to_broadcast([P, TT, 8]), ALU.mult))
            link(dve.tensor_tensor(col3(12, 8), oh1, oh2, ALU.add))
            dve.wait_ge(s["cum_raw"], at("cum_raw", l))
            link(dve.tensor_tensor(col3(432, 4), oh, ps[7][:, 0:12].rearrange("p (t n) -> p t n", t=TT), ALU.mult))
            link(dve.tensor_reduce(rt[:, 444:447], col3(432, 4), AX.X, ALU.add))
            link(dve.tensor_scalar(rt[:, 448:451], rt[:, 444:447], float(P), None, ALU.is_ge))
            link(dve.scalar_tensor_tensor(rt[:, 451:454], rt[:, 444:447], 2.0 * P, rt[:, 448:451], ALU.is_ge, ALU.add))
            link(dve.scalar_tensor_tensor(rt[:, 454:457], rt[:, 451:454], -float(P), rt[:, 444:447], ALU.mult, ALU.add))
            link(dve.tensor_scalar(rt[:, 457:461], ps[7][:, 12:16], P + 1.0, None, ALU.is_ge))
            link(dve.scalar_tensor_tensor(rt[:, 457:461], ps[7][:, 12:16], 2.0 * P + 1, rt[:, 457:461], ALU.is_ge, ALU.add))
            link(dve.memset(rt[:, 461:462], 0.0))
            for g in range(GROUPS):
                link(dve.tensor_tensor(rt[:, 462 + g:463 + g], rt[:, 461 + g:462 + g], rt[:, 457 + g:458 + g], ALU.add))
            link(dve.tensor_tensor(col3(432, 4), oh, const(C_GI, 4), ALU.mult))
            link(dve.tensor_reduce(rt[:, 466:469], col3(432, 4), AX.X, ALU.add))
            link(dve.tensor_tensor(col3(432, 4), oh, rt[:, 461:465].unsqueeze(1).to_broadcast([P, TT, 4]), ALU.mult))
            link(dve.tensor_reduce(rt[:, 469:472], col3(432, 4), AX.X, ALU.add))
            link(dve.scalar_tensor_tensor(rt[:, 469:472], rt[:, 469:472], GROUPS - 1.0, rt[:, 451:454], ALU.add, ALU.add))
            link(dve.tensor_tensor(rt[:, 469:472], rt[:, 469:472], rt[:, 466:469], ALU.subtract))
            link(dve.tensor_tensor(rt[:, 469:472], rt[:, 469:472], rt[:, 448:451], ALU.mult))
            link(dve.tensor_tensor(rt[:, 469:472], rt[:, 469:472], rt[:, 466:469], ALU.add))
            n_v = GROUPS + EXTRA
            tgt = col3(474, n_v)
            link(dve.tensor_tensor(tgt, col3(469).to_broadcast([P, TT, n_v]), const(C_VI, n_v), ALU.is_equal))
            link(dve.tensor_scalar(rt[:, 454:457], rt[:, 454:457], 1.0, None, ALU.add))
            dve.tensor_tensor(tgt, tgt, col3(454).to_broadcast([P, TT, n_v]), ALU.mult).then_inc(s["tgt"], 1)
            dve.wait_ge(s["tgt"], at("tgt", l))
            for i in range(EXTRA):
                link(dve.tensor_scalar(rt[:, 432:435], rt[:, 462:465], float(i), None, ALU.is_le))
                link(dve.tensor_reduce(rt[:, 496 + i:497 + i], rt[:, 432:435], AX.X, ALU.add))
            link(dve.tensor_copy(xi[:, 1:3], rt[:, 496:498]))
            dve.tensor_copy(xi[:, 0:1], rt[:, 465:466]).then_inc(s["regs"], 1)
            dve.wait_ge(s["regs"], at("regs", l))
            extra = dve.value_load(xi[0:1, 0:1], min_val=0, max_val=EXTRA)

            def pick(v, e):
                for t in range(TT):
                    last = dve.tensor_scalar(sel[:, t, :], iota, tgt[:, t, v:v + 1], None, ALU.is_equal)
                last.then_inc(e["sel"], 1)

            def visit(v, e, done, n_visit, chunk0, following):
                q0 = n_visit * EPG
                dve.wait_ge(e["xT_raw"], 3 * (n_visit + 1))
                dve.wait_ge(e["xT"], 3 * (n_visit + 1))
                if following is not None:
                    pick(following, e)
                for ex in range(EPG):
                    dve.wait_ge(done, chunk0 + pos("U", ex) + 1)
                    dve.wait_ge(e["silu"], q0 + ex + 1)
                    if n_visit > 0 or ex >= 2:
                        dve.wait_ge(e["hidT_raw"], q0 + ex - 1)
                    dve.scalar_tensor_tensor(hd[:, ex % 2, :], ps[ex % 2][:, FF:2 * FF], wslot[:, v, ex:ex + 1],
                                             sg[:, ex % 2, :], ALU.mult, ALU.mult).then_inc(e["hid_e"], 1)
                for t in range(TT):
                    dve.wait_ge(e["sct"], TT * n_visit + t + 1)
                    for half in range(2):
                        dst = moe[:, t, half * 512:(half + 1) * 512]
                        if v == 0:
                            last = dve.tensor_copy(dst, ps[6 + half][:, :])
                        else:
                            last = dve.tensor_tensor(dst, dst, ps[6 + half][:, :], ALU.add)
                    last.then_inc(e["acc"], 1)
                dve.wait_ge(e["acc"], TT * (n_visit + 1))

            pick(0, e_main)
            for v in range(GROUPS):
                visit(v, e_main, s["chunk_done"], l * GROUPS + v, first_chunk(l) + MIX_CHUNKS + v * EPG * 3,
                      v + 1 if v + 1 < GROUPS else None)
            with dve.If(extra >= 1):
                pick(4, e_extra[l])
                visit(4, e_extra[l], e_extra[l]["chunk_done"], 0, 0, None)
                with dve.If(extra >= 2):
                    pick(5, e_extra[l])
                    visit(5, e_extra[l], e_extra[l]["chunk_done"], 1, EPG * 3, None)

            dve.wait_ge(s["gate_in"], 32 * (2 * l + 2))
            dve.wait_ge(s["ln_in"], 32 * (2 * l + 3))
            for t in range(TT):
                link(dve.tensor_tensor(moe[:, t, :], moe[:, t, :], modr[:, min(t, 1), :], ALU.mult))
                link(dve.scalar_tensor_tensor(x[:, t, :], x[:, t, :], ALPHA, moe[:, t, :], ALU.mult, ALU.add))
                layer_norm(t, "ln2_var", "ln2_std", "x2", l * 3)

    ctx.close()


def packed(w):
    def flat(name):
        return np.asarray(w[name]).reshape(DEPTH, -1)

    def by_partition(name, outer):
        v = np.asarray(w[name]).reshape(DEPTH, outer, -1, P)
        return v.transpose(0, 3, 1, 2).reshape(DEPTH, P, -1)

    router = np.concatenate([np.asarray(w["moe_w_gr"]), np.asarray(w["moe_w_er"]).reshape(DEPTH, D, -1)], 2)
    columns = [by_partition("gm_bs", 4), by_partition("hy_conv_w", 3), by_partition("hy_conv_b", 1),
               by_partition("hy_bias", 2)]
    w1 = np.zeros((DEPTH, FH, FH), np.float32)
    w1[:, :EMB] = np.asarray(w["hy_f_w1"])
    return dict(
        rows=np.concatenate([flat(n) for n in ("gm_ln_g", "gm_ln_b", "mla_gq", "mla_gkv", "moe_b_gr", "moe_b_er")], 1),
        cols=np.concatenate(columns, 2),
        fw=np.concatenate([w1, np.asarray(w["hy_f_w2"]), np.asarray(w["hy_f_b1"])[:, :, None],
                           np.asarray(w["hy_f_b2"])[:, :, None], np.asarray(w["hy_f_freq"]).transpose(0, 2, 1)], 2),
        gm_ws_t=np.asarray(w["gm_ws"]).transpose(0, 3, 1, 2).reshape(DEPTH, P, -1),
        w_router=router.reshape(DEPTH, P, -1),
    )


def tables():
    f8 = np.float64
    cst = np.zeros((P, C_END))
    cst[:, C_ID:C_ID + P] = np.eye(P)
    cst[:, C_TRI:C_TRI + P] = np.triu(np.ones((P, P)), 1)
    cst[:, C_ONE:C_ONE + P] = 1.0
    cst[:, C_IOTA:C_IOTA + P] = np.arange(1, P + 1)
    cst[:, C_RANK:C_RANK + 4] = np.arange(4, 0, -1)
    cst[:, C_GE:C_GE + 8] = np.arange(8, 0, -1)
    cst[:, C_GI:C_GI + 4] = np.arange(4)
    cst[:, C_VI:C_VI + 6] = np.arange(6)
    cst[:, C_MASK:C_MASK + 3] = 1.0
    cst[0, C_MASK:C_MASK + 2] = 0.0
    n = ROPE // 4
    inv = (np.float32(10000.0) ** (-np.arange(n, dtype=np.float32) / np.float32(n))).astype(np.float32)
    p = np.arange(LAT)
    ang = np.concatenate([(p // 64)[:, None].astype(np.float32) * inv, (p % 64)[:, None].astype(np.float32) * inv], 1)
    cos = np.repeat(np.cos(ang.astype(f8)), 2, axis=1)
    sin = np.repeat(np.sin(ang.astype(f8)), 2, axis=1)
    sin[:, 0::2] *= -1.0
    cst[:, C_COS:C_COS + 64] = cos.reshape(2, P, ROPE).transpose(1, 0, 2).reshape(P, 64)
    cst[:, C_SIN:C_SIN + 64] = sin.reshape(2, P, ROPE).transpose(1, 0, 2).reshape(P, 64)
    rope_t = np.stack([cos.T, sin.T], 1)
    dft = np.zeros((P, DFT_COLS))
    for L, oc, osn, oct_, ost in ((P, G_C, G_S, G_CT, G_ST), (LAT, F_C, F_S, F_CT, F_ST)):
        arg = np.pi * np.outer(np.arange(L), 2 * np.arange(L) + 1) / (2 * L)
        for o, m in ((oc, np.cos(arg)), (osn, np.sin(arg)), (oct_, np.cos(arg).T / L), (ost, np.sin(arg).T / L)):
            dft[:, o:o + L * L // P] = m.reshape(L // P, P, L).transpose(1, 0, 2).reshape(P, -1)
    feats, decays = [], []
    deltas = np.abs(np.linspace(math.log(1e-2) / 1.5, math.log(1e-2) / 0.3, CH))
    for L in (P, LAT):
        t = np.linspace(0.0, 1.0, L)[:, None]
        bands = (EMB - 1) // 2
        w = 2.0 * math.pi * np.arange(L)[:, None] / L
        f = np.linspace(1e-4, bands - 1, bands)[None]
        feats.append(np.concatenate([t, np.cos(f * w), -np.sin(f * w)], -1))
        decays.append(np.exp(-t * deltas))
    z_t = np.concatenate(feats, 0).T
    decay = np.concatenate(decays, 0).reshape(TT, P, CH).transpose(1, 0, 2)
    out = dict(consts=cst, rope_t=rope_t, dft=dft, z_t=z_t, decay=decay)
    return {k: np.ascontiguousarray(v, dtype=np.float32) for k, v in out.items()}


_INS = ("x_prompt", "x_sample", "c", "cache_ckv", "cache_kpe", "c_ctx", "ln_in_g", "ln_in_b", "w_mod", "b_mod", "w_in",
        "hy_f_w3", "mla_wuq", "mla_wukv", "w_out", "ln1_g", "ln1_b", "ln2_g", "ln2_b",
        "moe_w_gate", "moe_w_up", "moe_w_down")
_OUTS = ((1, P, D), (1, LAT, D), (1, DEPTH, P, P), (1, DEPTH, P, ROPE))


def kernel(**inputs):
    import concourse.bacc as _bacc
    from concourse.bass_utils import run_bass_kernel_spmd as _run

    nc = _bacc.Bacc("TRN2", target_bir_lowering=False, num_devices=1)
    arrays, aps = {}, {}
    for name, value in [(n, inputs[n]) for n in _INS] + list(packed(inputs).items()) + list(tables().items()):
        arr = np.ascontiguousarray(value)
        arrays[f"in_{name}"] = arr
        aps[name] = nc.dram_tensor(f"in_{name}", arr.shape, mybir.dt.from_np(arr.dtype), kind="ExternalInput").ap()
    outs = [nc.dram_tensor(f"out_{i}", shape, F32, kind="ExternalOutput").ap() for i, shape in enumerate(_OUTS)]
    build(nc, aps, outs)
    r = _run(nc, [arrays], core_ids=[0])
    return tuple(r.results[0][f"out_{i}"] for i in range(len(_OUTS)))
```

```python
from contextlib import ExitStack
import math

import numpy as np
import concourse.bass as bass
from concourse import mybir

F32 = mybir.dt.float32
F32R = mybir.dt.float32r
I32 = mybir.dt.int32
ACT = mybir.ActivationFunctionType
ALU = mybir.AluOpType
AX = mybir.AxisListType

P = 128
D = 1024
K8 = D // P
DEPTH = 2
TT = 3
TOK = TT * P
LAT = 2 * P
KEYS = 4 * P
GW = 64
HEADS = 8
QK = 96
ROPE = 32
CH = 256
FH = 64
EMB = 33
MLA_COLS = 416
GROUPS = 4
EPG = 8
FF = 256
EXTRA = 2
RING = 4
SPLIT = 3
CHUNK = 2048
MOD_CHUNKS = 6 * D // 256
IN_CHUNKS = ((0, 256), (256, 256), (512, 256), (768, 256), (1024, 256), (1280, 144), (1424, 136), (1560, 136))
MIX_CHUNKS = len(IN_CHUNKS) + 4
MOE_CHUNKS = GROUPS * EPG * 3
ALPHA = (2.0 * DEPTH) ** 0.25
LN_EPS = 1e-5
RMS_EPS = 1e-6
QK_SCALE = 1.0 / math.sqrt(QK)
SMALL_LOADS = 11
MAGIC = 1.5 * 2.0 ** 23
TWO_PI_HI = 6.28125
TWO_PI_LO = 2.0 * math.pi - 6.28125
PI_SAFE = 3.1415925
BIG = 1.0e30

C_ID, C_TRI, C_ONE, C_IOTA = 0, 128, 256, 384
C_RANK, C_GE, C_COS, C_SIN = 512, 516, 524, 588
C_GI, C_VI, C_MASK = 652, 656, 662
C_END = 665
F_C, F_S, F_CT, F_ST = 128, 640, 1280, 1792
G_C, G_S, G_CT, G_ST = 0, 1152, 2304, 2432
DFT_COLS = 2560

A_U = 4 * D
A_MLA = A_U + 2304
A_UTOK = A_MLA + TT * MLA_COLS
A_DFT = A_UTOK + TT * CH
ARENA = 2 * D + 2 * SPLIT * CHUNK
assert A_DFT + DFT_COLS <= ARENA

PER = dict(
    filt_in=1, hid_in=1, sin_in=2, hid=2, filt_raw=6, filt_eo=3, spec_raw=3, spec=3, 
    h=3, hT_raw=8, hT=8, uv=3, hy=3, mla=3,
    zc=6, gm_var=1, gm_std=1, vh=1, s_raw=2, a=1, aT_raw=2, aT=2,
    rms_ss=1, rms_var=1, rms_std=1, mla_n=1, wuq_sw=1, latT_raw=4, latT=4,
    ut_raw=4, ut=4, uf_raw=6, yf=6, yc_raw=4, yc=4,
    q_raw=8, q_nope=8, q_pe=8, k_raw=4, kT=4, v_raw=4, v=4,
    sc_raw=8, mx=8, pexp=8, pn=8, pT_raw=16, pT=16, pv=8, oT=4, out_raw=2,
    ln1_var=3, ln1_std=3, x1=3, h2=3, h2T_raw=6, h2T=6, lg_raw=1, oh=1, lg_sh=1, lg_exp=1, cum_raw=1, tgt=1, regs=1,
    ln2_var=3, ln2_std=3, x2=3,
)


def pos(kind, e, experts):
    if kind == "D":
        return 3 * e + 4 if e < experts - 1 else 3 * e + 2
    return (0 if e == 0 else 3 * e - 1) + (kind == "U")


def order(experts):
    return [(k, e) for _, k, e in sorted((pos(k, e, experts), k, e) for k in "GUD" for e in range(experts))]


PAIR = 2 * EPG
GATHERS = GROUPS + 1
GATHER = {3: (0, 0), 4: (0, 1), 5: (0, 2), 12: (1, 0), 13: (1, 1), 14: (1, 2)}
SCATTER = {9: 0, 10: 1, 11: 2}


def build(nc, a, outs):
    ctx = ExitStack()

    def sb(name, shape, dt=F32):
        return ctx.enter_context(nc.sbuf_tensor(name, shape, dt))

    def sem(name):
        return ctx.enter_context(nc.semaphore(name))

    ps = [ctx.enter_context(nc.psum_tensor(f"bank{i}", [P, 512], F32)) for i in range(8)]
    ring = sb("ring", [P, RING, CHUNK])
    x = sb("x", [P, TT, D])
    region_a = sb("region_a", [P, TT * D])
    act_t = sb("act_t", [P, K8, TOK])
    arena = sb("arena", [P, ARENA])
    arena_at = nc.sbuf_base - 4 * ARENA
    modr = arena[:, 0:4 * D].rearrange("p (a d) -> p a d", a=4)
    lnr = sb("lnr", [P, 2, D])
    region_k = sb("region_k", [P, 4096])
    region_k_at = nc.sbuf_base - 4 * 4096
    region_s = sb("region_s", [P, TT * D])
    region_q = sb("region_q", [P, HEADS * TOK])
    region_q_at = nc.sbuf_base - 4 * HEADS * TOK
    region_v = sb("region_v", [P, 2048])
    region_v_at = nc.sbuf_base - 4 * 2048
    region_u = arena[:, A_U:A_U + 2304]
    mla = arena[:, A_MLA:A_MLA + TT * MLA_COLS].rearrange("p (t n) -> p t n", t=TT)
    utok = arena[:, A_UTOK:A_UTOK + TT * CH].rearrange("p (t n) -> p t n", t=TT)
    dft = arena[:, A_DFT:A_DFT + DFT_COLS]
    cst = sb("cst", [P, C_END])
    ropeT = sb("ropeT", [QK, 2, LAT])
    wuq = sb("wuq", [P, 2, HEADS * QK])
    wuq_sw = sb("wuq_sw", [P, 2, HEADS * ROPE])
    wukv = sb("wukv", [P, HEADS * 128])
    wsT = sb("wsT", [P, 4, P])
    wr = sb("wr", [P, K8, 36])
    rows = sb("rows", [P, 932])
    cols = sb("cols", [P, 32])
    fw = sb("fw", [FH, 132])
    st = sb("st", [P, 96])
    xi = sb("xi", [P, 4], I32)

    bs_c = cols[:, 0:4]
    cw = cols[:, 4:28].rearrange("p (j c) -> p j c", j=4)
    hyb = cols[:, 28:32].rearrange("p (o c) -> p o c", o=2)
    w_hi = nc.alloc_sbuf_tensor_at("w_hi", [P, SPLIT, CHUNK], F32R, offset=arena_at + 4 * 2 * D)
    w_lo = nc.alloc_sbuf_tensor_at("w_lo", [P, SPLIT, CHUNK], F32R, offset=arena_at + 4 * (2 * D + SPLIT * CHUNK))
    x_hi = nc.alloc_sbuf_tensor_at("x_hi", [P, 2, K8, P], F32R, offset=region_k_at)
    x_lo = nc.alloc_sbuf_tensor_at("x_lo", [P, 2, K8, P], F32R, offset=region_k_at + 4 * 2 * K8 * P)
    hd_hi = nc.alloc_sbuf_tensor_at("hd_hi", [P, 2, FF], F32R, offset=region_v_at + 4 * 768)
    hd_lo = nc.alloc_sbuf_tensor_at("hd_lo", [P, 2, FF], F32R, offset=region_q_at + 4 * 2432)
    cT = utok[:, 0, :].rearrange("p (k n) -> p k n", k=K8)
    craw = utok[:, 1, 0:2 * K8].rearrange("p (c k) -> p c k", c=2)
    h = region_a[:].rearrange("p (t d) -> p t d", t=TT)
    zc = region_a[:, 0:6 * TOK].rearrange("p (c t) -> p c t", c=6)
    kT = region_k[:].rearrange("p (h t) -> p h t", h=HEADS)
    v_sb = region_v[:].rearrange("p (k n) -> p k n", k=4)
    spec = region_s[:].rearrange("p (b c n) -> p b c n", b=3, c=2)
    hy = region_q[:, 0:6 * 387].rearrange("p (c t) -> p c t", c=6)
    qT = region_q[:].rearrange("p (h t) -> p h t", h=HEADS)
    uv = region_u[:, 0:1536].rearrange("p (t n) -> p t n", t=TT)
    vh = region_u[:, 1536:2304].rearrange("p (t n) -> p t n", t=TT)
    probs = region_u[:, 0:896]
    probsT = region_u[:, 896:1792].rearrange("p (b n) -> p b n", n=128)
    yfre = region_v[:, 0:1536].rearrange("p (b c n) -> p b c n", b=3, c=2)
    ytmp = region_v[:, 1536:2048]
    f_sum = region_k[:, 0:1536].rearrange("p (t n) -> p t n", t=TT)
    f_dif = region_k[:, 1536:3072].rearrange("p (t n) -> p t n", t=TT)
    w3 = region_k[0:FH, 3072:4096]
    decay = region_v[:, 0:768].rearrange("p (t n) -> p t n", t=TT)
    f_tmp = region_v[:, 768:1280]
    f_arg = region_u[0:FH, 0:384]
    f_n = region_u[0:FH, 384:768]
    hid1 = region_u[0:FH, 768:1152]
    hid2 = region_u[0:FH, 1152:1536]
    zT = region_u[0:EMB, 1536:1920]
    spare = arena[:, 0:4 * D]
    cqT = spare[:, 2048:2816].rearrange("p (c t) -> p c t", c=2)
    ckvT = spare[:, 2816:3328]
    kpeb = spare[:, 3328:3712].rearrange("p (t n) -> p t n", t=4)
    cckv = spare[:, 3712:3840]
    qtmp = spare[:, 3840:4096]
    moe = region_s[:].rearrange("p (t d) -> p t d", t=TT)
    selT = region_v[:, 0:768].rearrange("p (v t n) -> p v t n", v=2, t=TT)
    sel = region_q[:, 0:384].rearrange("p (t n) -> p t n", t=TT)
    y_sb = region_q[:, 384:1408]
    sg = region_q[:, 1408:1920].rearrange("p (b n) -> p b n", b=2)
    hd = region_q[:, 1920:2432].rearrange("p (b n) -> p b n", b=2)
    rt = region_v[:, 1536:2048]
    wslot = region_q[:, 2944:2960].rearrange("p (v n) -> p v n", n=8)

    ident = cst[:, C_ID:C_ID + P]
    tri = cst[:, C_TRI:C_TRI + P]
    ones = cst[:, C_ONE:C_ONE + P]
    iota = cst[:, C_IOTA:C_IOTA + P]

    s = {name: sem(name) for name in PER}
    for name in ("const_in", "dft_in", "x_in", "cond_in", "cT", "mod_zero", "bmod_in", "mod_sum", "mod_out",
                 "x0_var", "x0_std", "x0", "chunk_done", "small_in", "cache_in",
                 "mod12_in", "moe_zero", "gate_in", "ln_in", "dve_step", "state_out", "y_out"):
        s[name] = sem(name)
    ring_full = [sem(f"ring_full{i}") for i in range(RING)]
    MOE_NAMES = ("hi", "lo", "done", "sel", "x_raw", "x_hi", "x_lo", "picked", "rest", "silu", "hid", "hd_raw", "hd_hi", "hd_lo",
                 "y", "sct", "acc")
    e_main = {n: sem("e_" + n) for n in MOE_NAMES}
    e_extra = [{n: sem(f"x{l}_" + n) for n in MOE_NAMES} for l in range(DEPTH)]
    moe_full = [sem(f"moe_full{i}") for i in range(RING)]
    x_full = [[sem(f"x{l}_full{i}") for i in range(RING)] for l in range(DEPTH)]

    def at(name, l, i=None):
        return l * PER[name] + (PER[name] if i is None else i)

    mod_dram = nc.dram_tensor("mod_rows", (DEPTH, 2, 6 * D), F32, kind="Internal").ap()

    MOD_ALL = DEPTH * MOD_CHUNKS

    def first_chunk(l):
        return MOD_ALL + l * MIX_CHUNKS

    block = ctx.enter_context(nc.Block())

    @block.sync
    def _(sp):
        sp.dma_start(cst[:], a["consts"]).then_inc(s["const_in"], 16)
        sp.dma_start(craw[:, 0, :], a["c_ctx"].rearrange("(p k) -> p k", k=K8)).then_inc(s["cond_in"], 16)
        sp.dma_start(craw[:, 1, :], a["c"].rearrange("a (p k) -> p (a k)", k=K8)).then_inc(s["cond_in"], 16)

        def chunk(n, dst, src, first=0):
            if n >= RING and n - RING >= first:
                sp.wait_ge(s["chunk_done"], n - RING + 1)
            sp.dma_start(dst, src).then_inc(ring_full[n % RING], 16)

        def slot(n, cols, k):
            return ring[:, n % RING, 0:cols * k].rearrange("p (k n) -> p k n", k=k)

        for l in range(DEPTH):
            wm = a["w_mod"][l].rearrange("(p k) n -> p k n", k=K8)
            for c in range(MOD_CHUNKS):
                n = l * MOD_CHUNKS + c
                chunk(n, slot(n, 256, K8), wm[:, :, c * 256:(c + 1) * 256])

        for l in range(DEPTH):
            n0 = first_chunk(l)
            wi = a["w_in"][l].rearrange("(p k) n -> p k n", k=K8)
            wo = a["w_out"][l].rearrange("(k p) n -> p k n", p=P)
            for c, (c0, n) in enumerate(IN_CHUNKS):
                chunk(n0 + c, slot(n0 + c, n, K8), wi[:, :, c0:c0 + n], n0 if l > 0 else 0)
            for c in range(4):
                chunk(n0 + 8 + c, slot(n0 + 8 + c, D, 2), wo[:, 2 * c:2 * c + 2, :])
            n1 = n0 + MIX_CHUNKS
            w_of = {"G": a["moe_w_gate"][l], "U": a["moe_w_up"][l], "D": a["moe_w_down"][l]}

            def expert(kind, e):
                return w_of[kind][bass.ds(e, 1)].rearrange("a (p k) n -> p (a k n)", k=2 if kind == "D" else K8)

            sp.wait_ge(s["chunk_done"], n1)
            with sp.Fori(0, GROUPS // 2) as it:
                for i, (kind, e) in enumerate(order(PAIR)):
                    sp.wait_ge(e_main["lo"], it * (3 * PAIR) + (l * MOE_CHUNKS + i + 1))
                    sp.dma_start(ring[:, i % RING, :], expert(kind, it * PAIR + e)).then_inc(moe_full[i % RING], 16)
            sp.wait_ge(s["regs"], at("regs", l))
            extra = sp.value_load(xi[0:1, 0:1], min_val=0, max_val=EXTRA)

            def extra_loads(i):
                g = sp.value_load(xi[0:1, 1 + i:2 + i], min_val=0, max_val=GROUPS - 1)
                for j, (kind, e) in enumerate(order(EPG)):
                    if i == 0 and j < RING:
                        sp.wait_ge(e_main["lo"], (l + 1) * MOE_CHUNKS + j + 1)
                    sp.wait_ge(e_extra[l]["lo"], i * EPG * 3 + j + 1)
                    sp.dma_start(ring[:, j % RING, :], expert(kind, g * EPG + e)).then_inc(x_full[l][j % RING], 16)

            with sp.If(extra >= 1):
                extra_loads(0)
                with sp.If(extra >= 2):
                    extra_loads(1)
                    sp.wait_ge(e_extra[l]["lo"], RING + 2 * EPG * 3)
                sp.wait_ge(e_extra[l]["lo"], RING + EPG * 3)
            if l + 1 < DEPTH:
                sp.wait_ge(e_main["lo"], RING + (l + 1) * MOE_CHUNKS)

    @block.gpsimd
    def _(pool):
        pool.dma_start(x[:, 0, :], a["x_prompt"][0]).then_inc(s["x_in"], 16)
        for t in range(2):
            pool.dma_start(x[:, 1 + t, :], a["x_sample"][0, t * P:(t + 1) * P]).then_inc(s["x_in"], 16)

        def row(dst, src):
            return pool.dma_start(dst, src.rearrange("(a n) -> a n", a=1).to_broadcast([P, src.shape[0]]))

        row(lnr[:, 0, :], a["ln_in_g"]).then_inc(s["ln_in"], 16)
        row(lnr[:, 1, :], a["ln_in_b"]).then_inc(s["ln_in"], 16)
        pool.dma_start(ropeT[64:96], a["rope_t"]).then_inc(s["dft_in"], 16)
        pool.wait_ge(s["mod_zero"], 1)
        for l in range(DEPTH):
            bview = a["b_mod"][l].rearrange("(a b j n) -> a b j n", a=1, j=4, n=64)
            for j in range(4):
                for c in range(2):
                    pool.dma_start(region_a[32 * j + c:32 * j + c + 1, l * 1536:(l + 1) * 1536].rearrange(
                        "p (b n) -> p b n", n=64), bview[:, :, j, :]).then_inc(s["bmod_in"], 16)

        for l in range(DEPTH):
            if l > 0:
                pool.wait_ge(s["lg_exp"], at("lg_exp", l - 1))
                pool.wait_ge(s["lg_raw"], at("lg_raw", l - 1))
                pool.wait_ge(s["v_raw"], at("v_raw", l - 1))
                pool.wait_ge(s["x2"], at("x2", l - 1))
            small = s["small_in"]
            row(rows[:], a["rows"][l]).then_inc(small, 16)
            pool.dma_start(cols[:], a["cols"][l]).then_inc(small, 16)
            pool.dma_start(fw[:], a["fw"][l]).then_inc(small, 16)
            pool.dma_start(dft, a["dft"]).then_inc(small, 16)
            pool.dma_start(w3, a["hy_f_w3"][l]).then_inc(small, 16)
            pool.dma_start(decay, a["decay"]).then_inc(small, 16)
            pool.dma_start(zT, a["z_t"]).then_inc(small, 16)
            pool.dma_start(wsT[:].rearrange("p h q -> p (h q)"), a["gm_ws_t"][l]).then_inc(small, 16)
            pool.dma_start(wuq[:], a["mla_wuq"][l].rearrange("(c p) n -> p c n", p=P)).then_inc(small, 16)
            pool.dma_start(wukv[:], a["mla_wukv"][l]).then_inc(small, 16)
            pool.dma_start(wr[:].rearrange("p k n -> p (k n)"), a["w_router"][l]).then_inc(small, 16)

            def mod_row(dst, c, i):
                src = mod_dram[l, c:c + 1, i * D:(i + 1) * D]
                return pool.dma_start(dst, src.to_broadcast([P, D]))

            pool.wait_ge(s["mod_out"], 16 * 24 * DEPTH)
            for c in range(2):
                for i in range(2):
                    mod_row(modr[:, 2 * c + i, :], c, i).then_inc(s["mod12_in"], 16)
            pool.wait_ge(s["h"], at("h", l))
            for c in range(2):
                mod_row(modr[:, c, :], c, 2).then_inc(s["gate_in"], 16)
            pool.dma_start(cckv, a["cache_ckv"][0, l]).then_inc(s["cache_in"], 16)
            if l == 0:
                pool.wait_ge(s["x0"], TT)
            else:
                pool.wait_ge(s["x2"], at("x2", l - 1))
            row(lnr[:, 0, :], a["ln1_g"][l]).then_inc(s["ln_in"], 16)
            row(lnr[:, 1, :], a["ln1_b"][l]).then_inc(s["ln_in"], 16)
            pool.dma_start(kpeb[:, 3, 64:96], a["cache_kpe"][0, l]).then_inc(s["cache_in"], 16)
            pool.wait_ge(s["mla_n"], at("mla_n", l))
            pool.dma_start(outs[2][0, l], mla[:, 0, 256:384]).then_inc(s["state_out"], 16)
            pool.dma_start(outs[3][0, l], mla[:, 0, 384:416]).then_inc(s["state_out"], 16)
            pool.wait_ge(s["yc"], at("yc", l))
            pool.memset(region_s[:], 0.0).then_inc(s["moe_zero"], 1)
            pool.wait_ge(s["x1"], at("x1", l))
            row(lnr[:, 0, :], a["ln2_g"][l]).then_inc(s["ln_in"], 16)
            row(lnr[:, 1, :], a["ln2_b"][l]).then_inc(s["ln_in"], 16)
            for c in range(2):
                for i in range(2):
                    mod_row(modr[:, 2 * c + i, :], c, 3 + i).then_inc(s["mod12_in"], 16)
            pool.wait_ge(s["h2"], at("h2", l))
            for c in range(2):
                mod_row(modr[:, c, :], c, 5).then_inc(s["gate_in"], 16)
        for t in range(TT):
            pool.wait_ge(s["x2"], at("x2", DEPTH - 1, t + 1))
            dst = outs[0][0] if t == 0 else outs[1][0, (t - 1) * P:t * P]
            pool.dma_start(dst, x[:, t, :]).then_inc(s["y_out"], 16)
        pool.wait_ge(s["state_out"], 16 * 2 * DEPTH)
        pool.wait_ge(s["y_out"], 16 * TT)

    @block.tensor
    def _(pe):
        pe.wait_ge(s["const_in"], 16)
        pe.wait_ge(s["dft_in"], 16)

        def filters(l):
            pe.wait_ge(s["small_in"], 16 * SMALL_LOADS * (l + 1))
            if l > 0:
                pe.wait_ge(s["x2"], at("x2", l - 1))
            pe.matmul(ps[0][0:FH, 0:TOK], fw[0:EMB, 0:64], zT, start=True, stop=True).then_inc(s["filt_in"], 1)
            pe.wait_ge(s["hid"], at("hid", l, 1))
            pe.matmul(ps[1][0:FH, 0:TOK], fw[:, 64:128], hid1, start=True, stop=True).then_inc(s["hid_in"], 1)
            pe.wait_ge(s["hid"], at("hid", l, 2))
            for t in range(TT):
                for o in range(2):
                    pe.matmul(ps[2 * t + o][:, :], hid2[:, t * P:(t + 1) * P], w3[:, o * 512:(o + 1) * 512],
                              start=True, stop=True).then_inc(s["filt_raw"], 1)
            pe.wait_ge(s["filt_eo"], at("filt_eo", l))
            for b in range(3):
                tiles = (0,) if b == 0 else (1, 2)
                for part, (m_ctx, m_lat, src) in enumerate(((G_C, F_C, f_sum), (G_S, F_S, f_dif))):
                    for i, t in enumerate(tiles):
                        o = m_ctx if b == 0 else m_lat + i * 256 + (b - 1) * P
                        mm = pe.matmul(ps[2 * b + part][:, :], dft[:, o:o + P], src[:, t, :],
                                       start=(i == 0), stop=(i == len(tiles) - 1))
                mm.then_inc(s["spec_raw"], 1)

        filters(0)
        pe.wait_ge(s["cT"], 2)
        pe.wait_ge(s["spec"], at("spec", 0))
        for l in range(DEPTH):
            for c in range(MOD_CHUNKS):
                n = l * MOD_CHUNKS + c
                pe.wait_ge(ring_full[n % RING], 16 * (n // RING + 1))
                b = n // 8 % 2
                if c % 8 == 0 and n >= 16:
                    pe.wait_ge(s["mod_sum"], n // 8 - 1)
                w = ring[:, n % RING, :].rearrange("p (k n) -> p k n", k=K8)
                for k in range(K8):
                    for j in range(4):
                        mm = pe.matmul(ps[b][32 * j:32 * j + 32, c % 8 * 64:c % 8 * 64 + 64], cT[:, k, :],
                                       w[:, k, j * 64:j * 64 + 64], start=(k == 0), stop=(k == K8 - 1),
                                       tile_position=(0, 32 * j), skip_group_check=True)
                mm.then_inc(s["chunk_done"], 1)

        for l in range(DEPTH):
            n0 = first_chunk(l)

            def loaded(c):
                n = n0 + c
                pe.wait_ge(ring_full[n % RING], 16 * (n // RING + 1))
                return ring[:, n % RING, :]

            if l > 0:
                filters(l)

            pe.wait_ge(s["h"], at("h", l))
            if l == 0:
                pe.wait_ge(s["mod_sum"], DEPTH * 3)
            for k in range(K8):
                if k < 6:
                    pe.wait_ge(s["spec"], at("spec", l, min(k, 5) // 2 + 1))
                else:
                    pe.wait_ge(s["hT"], at("hT", l, k - 5))
                for t in range(TT):
                    mm = pe.transpose(ps[k % 6][:, t * P:(t + 1) * P], h[:, t, k:D:K8], ident)
                mm.then_inc(s["hT_raw"], 1)
            pe.wait_ge(s["hT"], at("hT", l))

            for c in range(2):
                w = loaded(c).rearrange("p (k n) -> p k n", k=K8)
                for t in range(TT):
                    for k in range(K8):
                        mm = pe.matmul(ps[t][:, c * 256:(c + 1) * 256], act_t[:, k, t * P:(t + 1) * P], w[:, k, :],
                                       start=(k == 0), stop=(k == K8 - 1))
                mm.then_inc(s["chunk_done"], 1)
            for c in range(6):
                w = loaded(2 + c // 2).rearrange("p (k n) -> p k n", k=K8)
                if c == 4:
                    pe.wait_ge(s["hy"], at("hy", l, 1))
                for k in range(K8):
                    mm = pe.matmul(ps[3 + c % 4][:, 0:TOK], w[:, k, c % 2 * P:c % 2 * P + P], act_t[:, k, :],
                                   start=(k == 0), stop=(k == K8 - 1))
                if c % 2 == 1:
                    mm.then_inc(s["chunk_done"], 1)
            pe.wait_ge(s["uv"], at("uv", l, 2))
            for c, (c0, n) in enumerate(IN_CHUNKS[5:]):
                w = loaded(5 + c)[:, 0:n * K8].rearrange("p (k n) -> p k n", k=K8)
                for t in range(TT):
                    for k in range(K8):
                        mm = pe.matmul(ps[(7, 0, 1)[t]][:, c0 - 1280:c0 - 1280 + n], act_t[:, k, t * P:(t + 1) * P],
                                       w[:, k, :], start=(k == 0), stop=(k == K8 - 1))
                mm.then_inc(s["chunk_done"], 1)

            pe.wait_ge(s["vh"], at("vh", l))
            pe.wait_ge(s["mla"], at("mla", l))
            for hh in range(4):
                mm = pe.matmul(ps[1 + hh // 2][:, hh % 2 * 192:hh % 2 * 192 + 192].rearrange("p (t n) -> p t n", t=TT), wsT[:, hh, :],
                               vh[:, :, hh * GW:(hh + 1) * GW], start=True, stop=True)
                if hh % 2 == 1:
                    mm.then_inc(s["s_raw"], 1)
            pe.wait_ge(s["a"], at("a", l))
            pe.wait_ge(s["hy"], at("hy", l))
            for c in range(2):
                for t in range(TT):
                    mm = pe.transpose(ps[3 + c][:, t * P:(t + 1) * P], uv[:, t, c * P:(c + 1) * P], ident)
                mm.then_inc(s["aT_raw"], 1)

            pe.wait_ge(s["mla_n"], at("mla_n", l))
            pe.wait_ge(s["cache_in"], 32 * (l + 1))
            for c in range(2):
                for t in range(TT):
                    mm = pe.transpose(ps[6 + c][:, t * P:(t + 1) * P], mla[:, t, c * P:(c + 1) * P], ident)
                mm.then_inc(s["latT_raw"], 1)
            for t in range(4):
                mm = pe.transpose(ps[0][:, t * P:(t + 1) * P], mla[:, t, 256:384] if t < TT else cckv, ident)
            mm.then_inc(s["latT_raw"], 1)
            for t in range(4):
                mm = pe.transpose(ps[5][0:QK, t * P:(t + 1) * P], kpeb[:, t, :], ident)
            mm.then_inc(s["latT_raw"], 1)

            pe.wait_ge(s["zc"], at("zc", l))
            pe.wait_ge(s["aT"], at("aT", l))
            pe.wait_ge(s["latT"], at("latT", l))
            for o in range(2):
                if o == 1:
                    pe.wait_ge(s["yc"], at("yc", l, 2))
                for t in range(TT):
                    for c in range(2):
                        mm = pe.transpose(ps[t // 2][:, t % 2 * 256 + c * P:t % 2 * 256 + c * P + P],
                                          zc[:, 4 + c, t * P:(t + 1) * P], ident)
                    if t > 0:
                        mm.then_inc(s["ut_raw"], 1)
                pe.wait_ge(s["ut"], at("ut", l, 2 * o + 2))
                for b in range(3):
                    tiles = (0,) if b == 0 else (1, 2)
                    for part, (m_ctx, m_lat) in enumerate(((G_C, F_C), (G_S, F_S))):
                        for i, t in enumerate(tiles):
                            q = m_ctx if b == 0 else m_lat + i * 256 + (b - 1) * P
                            mm = pe.matmul(ps[2 + b][:, part * 256:part * 256 + 256], dft[:, q:q + P], utok[:, t, :],
                                           start=(i == 0), stop=(i == len(tiles) - 1))
                    mm.then_inc(s["uf_raw"], 1)
                for c in range(2):
                    pe.wait_ge(s["yf"], at("yf", l, 3 * o + 3))
                    for b in range(3):
                        for part, (m_ctx, m_lat) in enumerate(((G_CT, F_CT), (G_ST, F_ST))):
                            cols = slice(0, P) if b == 0 else slice(P, TOK)
                            q = slice(m_ctx, m_ctx + P) if b == 0 else slice(m_lat + (b - 1) * 256, m_lat + b * 256)
                            mm = pe.matmul(ps[5 + c][:, cols], yfre[:, b, part, c * P:(c + 1) * P], dft[:, q],
                                           start=(b < 2 and part == 0), stop=(b in (0, 2) and part == 1))
                    mm.then_inc(s["yc_raw"], 1)

            pe.wait_ge(s["wuq_sw"], at("wuq_sw", l))
            pe.wait_ge(s["yc"], at("yc", l))
            for hh in range(HEADS):
                b = 2 * (hh % 2)
                if hh >= 2:
                    pe.wait_ge(s["q_pe"], at("q_pe", l, hh - 1))
                    pe.wait_ge(s["q_nope"], at("q_nope", l, hh - 1))
                for c in range(2):
                    pe.matmul(ps[b][0:QK, 0:TOK], wuq[:, c, hh * QK:(hh + 1) * QK], cqT[:, c, :],
                              start=(c == 0), stop=(c == 1))
                for c in range(2):
                    mm = pe.matmul(ps[b + 1][64:96, 0:LAT], wuq_sw[:, c, hh * ROPE:(hh + 1) * ROPE], cqT[:, c, P:TOK],
                                   start=(c == 0), stop=(c == 1))
                mm.then_inc(s["q_raw"], 1)
            for g in range(4):
                if g >= 2:
                    pe.wait_ge(s["kT"], at("kT", l, g - 1))
                for i in range(2):
                    hh = 2 * g + i
                    mm = pe.matmul(ps[4 + 2 * (g % 2) + i][0:64, :], wukv[:, hh * P:hh * P + 64], ckvT,
                                   start=True, stop=True)
                mm.then_inc(s["k_raw"], 1)
            pe.wait_ge(s["q_pe"], at("q_pe", l))
            pe.wait_ge(s["q_nope"], at("q_nope", l))
            wv = wukv[:].rearrange("p (h n) -> p h n", n=P)[:, :, 64:128]
            for t in range(4):
                pe.matmul(ps[t][:, :], ckvT[:, t * P:(t + 1) * P], wv, start=True, stop=True).then_inc(s["v_raw"], 1)

            pe.wait_ge(s["v"], at("v", l))
            pe.wait_ge(s["kT"], at("kT", l))

            def scores(hh):
                b = 2 * (hh % 2)
                if hh >= 2:
                    pe.wait_ge(s["pexp"], at("pexp", l, hh - 1))
                pe.matmul(ps[b][:, 0:384], qT[0:QK, hh, P:2 * P], kT[0:QK, hh, P:KEYS], start=True, stop=True)
                pe.matmul(ps[b][:, 384:512], qT[0:QK, hh, 0:P], kT[0:QK, hh, 0:P], start=True, stop=True)
                pe.matmul(ps[b + 1][:, 0:384], qT[0:QK, hh, 2 * P:3 * P], kT[0:QK, hh, P:KEYS],
                          start=True, stop=True).then_inc(s["sc_raw"], 1)

            scores(0)
            for hh in range(HEADS):
                if hh + 1 < HEADS:
                    scores(hh + 1)
                pe.wait_ge(s["pn"], at("pn", l, hh + 1))
                if hh > 0:
                    pe.wait_ge(s["pT"], at("pT", l, 2 * hh - 1))
                for i, o in enumerate((0, 512, 384)):
                    mm = pe.transpose(ps[4][:, i * P:(i + 1) * P], probs[:, o:o + P], ident)
                mm.then_inc(s["pT_raw"], 1)
                if hh > 0:
                    pe.wait_ge(s["pT"], at("pT", l, 2 * hh))
                for i, o in enumerate((P, 512 + P, 2 * P, 512 + 2 * P)):
                    mm = pe.transpose(ps[5][:, i * P:(i + 1) * P], probs[:, o:o + P], ident)
                mm.then_inc(s["pT_raw"], 1)
                pe.wait_ge(s["pT"], at("pT", l, 2 * hh + 2))
                if hh % 2 == 0 and hh >= 4:
                    pe.wait_ge(s["oT"], at("oT", l, hh // 2 - 1))
                r = slice(64 * (hh % 2), 64 * (hh % 2) + 64)
                ob = ps[6 + hh // 2 % 2]
                pe.matmul(ob[r, 0:P], v_sb[:, 0, hh * GW:(hh + 1) * GW], probsT[:, 2, :], start=True, stop=True)
                for i in range(3):
                    rhs = probsT[:, (0, 3, 5)[i]:(0, 3, 5)[i] + 2, :].rearrange("p b n -> p (b n)")
                    mm = pe.matmul(ob[r, P:TOK], v_sb[:, 1 + i, hh * GW:(hh + 1) * GW], rhs,
                                   start=(i == 0), stop=(i == 2))
                mm.then_inc(s["pv"], 1)

            pe.wait_ge(s["oT"], at("oT", l))
            pe.wait_ge(s["pexp"], at("pexp", l))
            for t in range(TT):
                for c in range(4):
                    w = loaded(8 + c).rearrange("p (k n) -> p k n", k=2)
                    for half in range(2):
                        for k in range(2):
                            mm = pe.matmul(ps[2 * t + half][:, :], act_t[:, 2 * c + k, t * P:(t + 1) * P],
                                           w[:, k, half * 512:(half + 1) * 512],
                                           start=(c == 0 and k == 0), stop=(c == 3 and k == 1))
                    if t == TT - 1:
                        mm.then_inc(s["chunk_done"], 1)
                if t < TT - 1:
                    mm.then_inc(s["out_raw"], 1)

            for t in range(TT):
                pe.wait_ge(s["h2"], at("h2", l, t + 1))
                for half in range(2):
                    for k in range(4):
                        mm = pe.transpose(ps[2 * t + half][:, k * P:(k + 1) * P], h[:, t, 4 * half + k:D:K8], ident)
                    mm.then_inc(s["h2T_raw"], 1)
                pe.wait_ge(s["h2T"], at("h2T", l, 2 * t + 2))
                for k in range(K8):
                    mm = pe.matmul(ps[6][:, t * 36:(t + 1) * 36], act_t[:, k, t * P:(t + 1) * P], wr[:, k, :],
                                   start=(k == 0), stop=(k == K8 - 1))
            mm.then_inc(s["lg_raw"], 1)
            pe.wait_ge(s["oh"], at("oh", l))
            oh = rt[:, 0:12].rearrange("p (t g) -> p t g", t=TT)
            for t in range(TT):
                for i in range(t + 1):
                    pe.matmul(ps[7][:, t * 4:t * 4 + 4], tri if i == t else ones, oh[:, i, :],
                              start=(i == 0), stop=(i == t))
            for i in range(TT):
                mm = pe.matmul(ps[7][:, 12:16], ones, oh[:, i, :], start=(i == 0), stop=(i == 2))
            mm.then_inc(s["cum_raw"], 1)
            pe.wait_ge(s["tgt"], at("tgt", l))
            dw = rt[:, 12:36].rearrange("p (t n) -> p t n", t=TT)

            def gather_half(e, half, g, loop=0):
                pe.wait_ge(e["sel"], loop * 2 + (g + 1))
                if half > 0 or g > 0:
                    pe.wait_ge(e["x_lo"], loop * 4 + (2 * g + half))
                for k in range(4 * half, 4 * half + 4):
                    for t in range(TT):
                        mm = pe.matmul(ps[3][:, k % 4 * P:k % 4 * P + P], h[:, t, k:D:K8], sel[:, t, :],
                                       start=(t == 0), stop=(t == TT - 1))
                mm.then_inc(e["x_raw"], 1)

            def gather_rest(e, scattered, loop=0):
                if scattered > 0:
                    pe.wait_ge(e_main["acc"], loop * 2 * TT + TT * scattered)
                for t in range(TT):
                    pe.matmul(ps[7][:, 384:392], sel[:, t, :], dw[:, t, :], start=(t == 0), stop=(t == TT - 1))
                for t in range(TT):
                    mm = pe.transpose(ps[7][:, t * P:(t + 1) * P], sel[:, t, :], ident)
                mm.then_inc(e["picked"], 1)

            def run(experts, slot0, e, chunk0, v0, loop, tokens_in, g0=None):
                q0 = v0 * EPG
                ex_by, v_by = loop * PAIR, loop * 2

                def weights(kind, ex):
                    i = pos(kind, ex, experts)
                    pe.wait_ge(e["lo"], loop * (3 * PAIR) + (RING + chunk0 + i + 1))
                    return [w[:, i % SPLIT, :].rearrange("p (k n) -> p k n", k=2 if kind == "D" else K8)
                            for w in (w_hi, w_lo)]

                def gate_up(ex, kind):
                    j = ex % 2
                    if kind == "G":
                        if q0 > 0 or ex >= 2:
                            pe.wait_ge(e["hid"], ex_by + (q0 + ex - 1))
                        if ex % EPG == 0:
                            sem_in, value, by = tokens_in(ex // EPG)
                            pe.wait_ge(sem_in, loop * by + value)
                    hi, lo = weights(kind, ex)
                    sl = (slot0 + ex // EPG) % 2
                    cols = slice(0, FF) if kind == "G" else slice(FF, 2 * FF)
                    for k in range(K8):
                        for i, (xs, ws) in enumerate(((x_hi, hi), (x_hi, lo), (x_lo, hi))):
                            mm = pe.matmul(ps[j][:, cols], xs[:, sl, k, :], ws[:, k, :],
                                           start=(k == 0 and i == 0), stop=(k == K8 - 1 and i == 2))
                    mm.then_inc(e["done"], 1)

                def turn(ex):
                    pe.wait_ge(e["hid"], ex_by + (q0 + ex + 1))
                    if q0 > 0 or ex >= 1:
                        pe.wait_ge(e["hd_lo"], ex_by + (q0 + ex))
                    for k in range(2):
                        mm = pe.transpose(ps[2][:, k * P:(k + 1) * P], hd[:, ex % 2, k:FF:2], ident)
                    mm.then_inc(e["hd_raw"], 1)

                def down(ex):
                    first, last = ex % EPG == 0, ex % EPG == EPG - 1
                    hi, lo = weights("D", ex)
                    pe.wait_ge(e["hd_lo"], ex_by + (q0 + ex + 1))
                    if first and v0 + ex > 0:
                        pe.wait_ge(e["y"], v_by * 2 + 2 * (v0 + ex // EPG))
                    for k in range(2):
                        for i, (hs, ws) in enumerate(((hd_hi, hi), (hd_hi, lo), (hd_lo, hi))):
                            for half in range(2):
                                mm = pe.matmul(ps[4 + half][:, :], hs[:, ex % 2, k * P:(k + 1) * P],
                                               ws[:, k, half * 512:(half + 1) * 512],
                                               start=(first and k == 0 and i == 0), stop=(last and k == 1 and i == 2),
                                               skip_group_check=True)
                    mm.then_inc(e["done"], 1)

                def scatter(visit, t):
                    pe.wait_ge(e["y"], v_by * 2 + 2 * (v0 + visit + 1))
                    if v0 + visit > 0 or t > 0:
                        pe.wait_ge(e["acc"], v_by * TT + (TT * (v0 + visit) + t))
                    for half in range(2):
                        mm = pe.matmul(ps[6 + half][:, :], selT[:, (slot0 + visit) % 2, t, :],
                                       y_sb[:, half * 512:(half + 1) * 512], start=True, stop=True)
                    mm.then_inc(e["sct"], 1)

                gate_up(0, "G")
                gate_up(0, "U")
                for ex in range(1, experts):
                    gate_up(ex, "G")
                    turn(ex - 1)
                    gate_up(ex, "U")
                    if experts == PAIR:
                        if ex in GATHER:
                            nth, step = GATHER[ex]
                            if step < 2:
                                gather_half(e, step, g0 + 1 + nth, loop)
                            else:
                                gather_rest(e, v0 + nth, loop)
                        if ex in SCATTER:
                            if ex == min(SCATTER):
                                pe.wait_ge(e["rest"], loop * 2 + (g0 + 2))
                            scatter(0, SCATTER[ex])
                    down(ex - 1)
                turn(experts - 1)
                down(experts - 1)
                if experts == PAIR:
                    pe.wait_ge(e["rest"], loop * 2 + (g0 + 3))
                for t in range(TT):
                    scatter(experts // EPG - 1, t)

            g0 = l * GATHERS
            for half in range(2):
                gather_half(e_main, half, g0)
            gather_rest(e_main, l * GROUPS)
            with pe.Fori(0, GROUPS // 2) as it:
                run(PAIR, 0, e_main, l * MOE_CHUNKS, l * GROUPS, it,
                    lambda visit: (e_main["x_lo"], 2 * (g0 + visit + 1), 4), g0)
            pe.wait_ge(s["regs"], at("regs", l))
            extra = pe.value_load(xi[0:1, 0:1], min_val=0, max_val=EXTRA)
            xe = e_extra[l]
            with pe.If(extra >= 1):
                pe.wait_ge(e_main["acc"], TT * GROUPS * (l + 1))
                run(EPG, 0, xe, 0, 0, 0, lambda visit: (e_main["x_lo"], 2 * (g0 + GATHERS), 0))
                with pe.If(extra >= 2):
                    pe.wait_ge(xe["acc"], TT)
                    for half in range(2):
                        gather_half(xe, half, 0)
                    gather_rest(xe, 0)
                    pe.wait_ge(xe["rest"], 1)
                    run(EPG, 1, xe, EPG * 3, 1, 0, lambda visit: (xe["x_lo"], 2, 0))

    @block.scalar
    def _(act):
        act.wait_ge(s["cond_in"], 32)
        act.wait_ge(s["cT"], 1)
        act.activation(cT[:, :, 0:2], craw.rearrange("p c k -> p k c"), ACT.Silu).then_inc(s["cT"], 1)
        for t in range(TT):
            act.wait_ge(s["x0_var"], t + 1)
            act.activation(st[:, 64 + t:65 + t], st[:, 60 + t:61 + t], ACT.Sqrt).then_inc(s["x0_std"], 1)
        def filters(l):
            for i, dst in enumerate((hid1, hid2)):
                act.wait_ge(s["sin_in"], at("sin_in", l, i + 1))
                act.activation(dst, f_arg, ACT.Sin).then_inc(s["hid"], 1)
            for b in range(3):
                act.wait_ge(s["spec_raw"], at("spec_raw", l, b + 1))
                act.activation(spec[:, b, 0, :], ps[2 * b][:, :], ACT.Copy)
                act.activation(spec[:, b, 1, :], ps[2 * b + 1][:, :], ACT.Copy).then_inc(s["spec"], 1)

        filters(0)
        for l in range(DEPTH):
            for b in range(3):
                act.wait_ge(s["mod_sum"], 3 * l + b + 1)
                for j in range(4):
                    for c in range(2):
                        dst = mod_dram[l, c:c + 1].rearrange("a (b j n) -> a b j n", j=4, n=64)[:, 8 * b:8 * b + 8, j, :]
                        src = region_a[32 * j + c:32 * j + c + 1, l * 1536 + b * 512:l * 1536 + b * 512 + 512]
                        act.dma_start(dst, src.rearrange("p (b n) -> p b n", n=64)).then_inc(s["mod_out"], 16)

        for l in range(DEPTH):
            if l > 0:
                filters(l)
            for k in range(K8):
                act.wait_ge(s["hT_raw"], at("hT_raw", l, k + 1))
                act.activation(act_t[:, k, :], ps[k % 6][:, 0:TOK], ACT.Copy).then_inc(s["hT"], 1)
            act.wait_ge(s["chunk_done"], first_chunk(l) + 2)
            for t in range(TT):
                act.activation(uv[:, t, :], ps[t][:, :], ACT.Gelu_apprx_tanh).then_inc(s["uv"], 1)
            for c in range(6):
                act.wait_ge(s["chunk_done"], first_chunk(l) + 3 + c // 2)
                bank = ps[3 + c % 4]
                act.activation(hy[:, c, 1:1 + P], bank[:, 0:P], ACT.Copy)
                mm = act.activation(hy[:, c, 2 + P:2 + TOK], bank[:, P:TOK], ACT.Copy)
                if c % 2 == 1:
                    mm.then_inc(s["hy"], 1)
            act.wait_ge(s["chunk_done"], first_chunk(l) + 8)
            for t in range(TT):
                act.activation(mla[:, t, :], ps[(7, 0, 1)[t]][:, 0:MLA_COLS], ACT.Copy).then_inc(s["mla"], 1)
            act.wait_ge(s["mla"], at("mla", l))
            for t in range(TT):
                act.activation(region_k[:, t * 384:t * 384 + 256], mla[:, t, 0:256], ACT.Square, accum_out=st[:, 48 + t:49 + t])
            for t in range(TT):
                mm = act.activation(region_k[:, t * 384 + 256:t * 384 + 384], mla[:, t, 256:384], ACT.Square, accum_out=st[:, 51 + t:52 + t])
            mm.then_inc(s["rms_ss"], 1)
            act.wait_ge(s["gm_var"], at("gm_var", l))
            act.activation(st[:, 12:24], st[:, 0:12], ACT.Sqrt).then_inc(s["gm_std"], 1)
            act.wait_ge(s["rms_var"], at("rms_var", l))
            act.activation(st[:, 54:60], st[:, 48:54], ACT.Sqrt).then_inc(s["rms_std"], 1)
            for c in range(2):
                act.wait_ge(s["aT_raw"], at("aT_raw", l, c + 1))
                act.activation(act_t[:, c, :], ps[3 + c][:, 0:TOK], ACT.Copy).then_inc(s["aT"], 1)
            for c in range(2):
                act.wait_ge(s["latT_raw"], at("latT_raw", l, c + 1))
                act.activation(cqT[:, c, :], ps[6 + c][:, 0:TOK], ACT.Copy).then_inc(s["latT"], 1)
            act.wait_ge(s["latT_raw"], at("latT_raw", l, 3))
            act.activation(ckvT, ps[0][:, :], ACT.Copy).then_inc(s["latT"], 1)
            act.wait_ge(s["latT_raw"], at("latT_raw", l, 4))
            for hh in range(HEADS):
                mm = act.activation(kT[64:96, hh, :], ps[5][64:96, :], ACT.Copy)
            mm.then_inc(s["latT"], 1)
            for o in range(2):
                act.wait_ge(s["ut_raw"], at("ut_raw", l, 2 * o + 1))
                act.activation(utok[:, 0:2, :].rearrange("p t n -> p (t n)"), ps[0][:, :], ACT.Copy).then_inc(s["ut"], 1)
                act.wait_ge(s["ut_raw"], at("ut_raw", l, 2 * o + 2))
                act.activation(utok[:, 2, :], ps[1][:, 0:256], ACT.Copy).then_inc(s["ut"], 1)
            for hh in range(HEADS):
                b = 2 * (hh % 2)
                act.wait_ge(s["q_raw"], at("q_raw", l, hh + 1))
                act.activation(qT[0:QK, hh, 0:P], ps[b][0:QK, 0:P], ACT.Copy)
                act.activation(qT[0:64, hh, P:TOK], ps[b][0:64, P:TOK], ACT.Copy).then_inc(s["q_nope"], 1)
            for g in range(4):
                act.wait_ge(s["k_raw"], at("k_raw", l, g + 1))
                act.activation(kT[0:64, 2 * g, :], ps[4 + 2 * (g % 2)][0:64, :], ACT.Copy)
                act.activation(kT[0:64, 2 * g + 1, :], ps[5 + 2 * (g % 2)][0:64, :], ACT.Copy).then_inc(s["kT"], 1)
            for t in range(4):
                act.wait_ge(s["v_raw"], at("v_raw", l, t + 1))
                act.activation(v_sb[:, t, :], ps[t][:, :], ACT.Copy).then_inc(s["v"], 1)
            for hh in range(HEADS):
                b = 2 * (hh % 2)
                act.wait_ge(s["mx"], at("mx", l, hh + 1))
                if hh > 0:
                    act.wait_ge(s["pT_raw"], at("pT_raw", l, 2 * hh))
                for i, (src, dst) in enumerate(((ps[b][:, 0:384], probs[:, 0:384]),
                                                (ps[b][:, 384:512], probs[:, 384:512]),
                                                (ps[b + 1][:, 0:384], probs[:, 512:896]))):
                    mm = act.activation(dst, src, ACT.Exp, bias=st[:, 36 + i:37 + i], scale=QK_SCALE,
                                        accum_out=st[:, 39 + i:40 + i])
                mm.then_inc(s["pexp"], 1)
                act.wait_ge(s["pT_raw"], at("pT_raw", l, 2 * hh + 1))
                if hh > 0:
                    act.wait_ge(s["pv"], at("pv", l, hh))
                act.activation(probsT[:, 0:3, :], ps[4][:, 0:384].rearrange("p (b n) -> p b n", b=3), ACT.Copy)\
                    .then_inc(s["pT"], 1)
                act.wait_ge(s["pT_raw"], at("pT_raw", l, 2 * hh + 2))
                act.activation(probsT[:, 3:7, :], ps[5][:, :].rearrange("p (b n) -> p b n", b=4), ACT.Copy)\
                    .then_inc(s["pT"], 1)
                if hh % 2 == 1:
                    act.wait_ge(s["pv"], at("pv", l, hh + 1))
                    act.activation(act_t[:, 4 + hh // 2, :], ps[6 + hh // 2 % 2][:, 0:TOK], ACT.Copy)\
                        .then_inc(s["oT"], 1)
            for t in range(TT):
                act.wait_ge(s["ln1_var"], at("ln1_var", l, t + 1))
                act.activation(st[:, 64 + t:65 + t], st[:, 60 + t:61 + t], ACT.Sqrt).then_inc(s["ln1_std"], 1)
            for t in range(TT):
                for half in range(2):
                    act.wait_ge(s["h2T_raw"], at("h2T_raw", l, 2 * t + half + 1))
                    act.activation(act_t[:, 4 * half:4 * half + 4, t * P:(t + 1) * P],
                                   ps[2 * t + half][:, :].rearrange("p (k n) -> p k n", k=4), ACT.Copy)\
                        .then_inc(s["h2T"], 1)
            act.wait_ge(s["lg_sh"], at("lg_sh", l))
            act.activation(rt[:, 300:315], rt[:, 280:295], ACT.Exp).then_inc(s["lg_exp"], 1)

            def gathered(e, half, slot, g, loop=0):
                act.wait_ge(e["x_raw"], loop * 4 + (2 * g + half + 1))
                act.activation(x_hi[:, slot, 4 * half:4 * half + 4, :],
                               ps[3][:, :].rearrange("p (k n) -> p k n", k=4), ACT.Copy).then_inc(e["x_hi"], 1)

            def picked(e, slot, g, loop=0):
                act.wait_ge(e["picked"], loop * 2 + (g + 1))
                act.activation(selT[:, slot, :, :], ps[7][:, 0:384].rearrange("p (t n) -> p t n", t=TT), ACT.Copy)
                act.activation(wslot[:, slot, :], ps[7][:, 384:392], ACT.Copy).then_inc(e["rest"], 1)

            def run(experts, e, full, full0, chunk0, v0, loop, g0=None):
                q0 = v0 * EPG
                ex_by, v_by, c_by = loop * PAIR, loop * 2, loop * (3 * PAIR)

                def high(c):
                    act.wait_ge(full[c % RING], loop * (16 * 3 * PAIR // RING) + 16 * (full0 + c // RING + 1))
                    act.wait_ge(e["done"], c_by + (chunk0 + c + 1))
                    act.activation(w_hi[:, c % SPLIT, :], ring[:, c % RING, :], ACT.Copy).then_inc(e["hi"], 1)

                for c in range(SPLIT):
                    high(c)
                for c, (kind, ex) in enumerate(order(experts)):
                    if kind == "G" and ex > 0 or (kind, ex) == ("D", experts - 1):
                        turned = ex - 1 if kind == "G" else ex
                        act.wait_ge(e["hd_raw"], ex_by + (q0 + turned + 1))
                        act.activation(hd_hi[:, turned % 2, :], ps[2][:, 0:FF], ACT.Copy).then_inc(e["hd_hi"], 1)
                    if kind == "U":
                        act.wait_ge(e["done"], c_by + (SPLIT + chunk0 + c + 1))
                        if q0 > 0 or ex >= 2:
                            act.wait_ge(e["hid"], ex_by + (q0 + ex - 1))
                        act.activation(sg[:, ex % 2, :], ps[ex % 2][:, 0:FF], ACT.Silu).then_inc(e["silu"], 1)
                        if experts == PAIR and ex in GATHER:
                            nth, step = GATHER[ex]
                            if step < 2:
                                gathered(e, step, 1 - nth, g0 + 1 + nth, loop)
                            else:
                                picked(e, 1 - nth, g0 + 1 + nth, loop)
                    if kind == "D" and ex % EPG == EPG - 1:
                        act.wait_ge(e["done"], c_by + (SPLIT + chunk0 + c + 1))
                        if v0 + ex // EPG > 0:
                            act.wait_ge(e["sct"], v_by * TT + TT * (v0 + ex // EPG))
                        for half in range(2):
                            act.activation(y_sb[:, half * 512:(half + 1) * 512], ps[4 + half][:, :], ACT.Copy)\
                                .then_inc(e["y"], 1)
                    if c + SPLIT < 3 * experts:
                        high(c + SPLIT)

            g0 = l * GATHERS
            for half in range(2):
                gathered(e_main, half, 0, g0)
            picked(e_main, 0, g0)
            with act.Fori(0, GROUPS // 2) as it:
                run(PAIR, e_main, moe_full, l * MOE_CHUNKS // RING, l * MOE_CHUNKS, l * GROUPS, it, g0)
            act.wait_ge(s["regs"], at("regs", l))
            extra = act.value_load(xi[0:1, 0:1], min_val=0, max_val=EXTRA)
            xe = e_extra[l]
            with act.If(extra >= 1):
                act.wait_ge(e_main["done"], SPLIT + (l + 1) * MOE_CHUNKS)
                act.wait_ge(e_main["sct"], TT * GROUPS * (l + 1))
                run(EPG, xe, x_full[l], 0, 0, 0, 0)
                with act.If(extra >= 2):
                    for half in range(2):
                        gathered(xe, half, 1, 0)
                    picked(xe, 1, 0)
                    run(EPG, xe, x_full[l], EPG * 3 // RING, EPG * 3, 1, 0)
            for t in range(TT):
                act.wait_ge(s["ln2_var"], at("ln2_var", l, t + 1))
                act.activation(st[:, 64 + t:65 + t], st[:, 60 + t:61 + t], ACT.Sqrt).then_inc(s["ln2_std"], 1)

    @block.vector
    def _(dve):
        steps = [0]

        def link(ins):
            steps[0] += 1
            ins.then_inc(s["dve_step"], 1)
            dve.wait_ge(s["dve_step"], steps[0])

        lnst = st[:, 80:94]

        def layer_norm(t, var, std, done, base):
            xt = x[:, t, :]
            dve.bn_stats(lnst[:, 0:6], xt[:, 0:512])
            link(dve.bn_stats(lnst[:, 6:12], xt[:, 512:1024]))
            link(dve.bn_aggr(lnst[:, 12:14], lnst[:, 0:12]))
            dve.tensor_scalar(st[:, 60 + t:61 + t], lnst[:, 13:14], LN_EPS, None, ALU.add).then_inc(s[var], 1)
            dve.wait_ge(s[std], base + t + 1)
            link(dve.reciprocal(st[:, 68:69], st[:, 64 + t:65 + t]))
            link(dve.tensor_scalar(xt, xt, lnst[:, 12:13], st[:, 68:69], ALU.subtract, ALU.mult))
            link(dve.tensor_tensor(xt, xt, lnr[:, 0, :], ALU.mult))
            dve.tensor_tensor(xt, xt, lnr[:, 1, :], ALU.add).then_inc(s[done], 1)

        def modulate(l, n_loads, done):
            dve.wait_ge(s["mod12_in"], 64 * n_loads)
            for t in range(TT):
                c = min(t, 1)
                link(dve.scalar_tensor_tensor(h[:, t, :], modr[:, 2 * c + 1, :], 1.0, x[:, t, :], ALU.add, ALU.mult))
                dve.tensor_tensor(h[:, t, :], h[:, t, :], modr[:, 2 * c, :], ALU.add).then_inc(s[done], 1)

        def wide(ap, shape):
            return ap.to_broadcast(shape)

        dve.memset(cT, 0.0).then_inc(s["cT"], 1)
        dve.memset(region_a[:, 0:3072], 0.0).then_inc(s["mod_zero"], 1)
        link(dve.memset(xi[:], 0))
        for e in [e_main] + e_extra:
            dve.memset(st[:, 95:96], 0.0).then_inc(e["lo"], RING)
            link(dve.memset(st[:, 94:95], 0.0))
            dve.memset(st[:, 94:95], 0.0).then_inc(e["done"], SPLIT)
            link(dve.memset(st[:, 95:96], 0.0))
        dve.wait_ge(s["x_in"], 16 * TT)
        dve.wait_ge(s["ln_in"], 32)
        for t in range(TT):
            layer_norm(t, "x0_var", "x0_std", "x0", 0)
        def filters(l):
            dve.wait_ge(s["small_in"], 16 * SMALL_LOADS * (l + 1))
            for i in range(2):
                if i == 0:
                    dve.wait_ge(s["filt_in"], at("filt_in", l))
                else:
                    dve.wait_ge(s["hid_in"], at("hid_in", l))
                link(dve.tensor_scalar(f_arg, ps[i][0:FH, 0:TOK], fw[:, 128 + i:129 + i], fw[:, 130 + i:131 + i],
                                       ALU.add, ALU.mult))
                link(dve.tensor_scalar(f_n, f_arg, 0.5 / math.pi, MAGIC, ALU.mult, ALU.add))
                link(dve.tensor_scalar(f_n, f_n, MAGIC, None, ALU.subtract))
                link(dve.scalar_tensor_tensor(f_arg, f_n, -TWO_PI_HI, f_arg, ALU.mult, ALU.add))
                link(dve.scalar_tensor_tensor(f_arg, f_n, -TWO_PI_LO, f_arg, ALU.mult, ALU.add))
                dve.tensor_scalar(f_arg, f_arg, PI_SAFE, -PI_SAFE, ALU.min, ALU.max).then_inc(s["sin_in"], 1)
            for t in range(TT):
                for o in range(2):
                    dve.wait_ge(s["filt_raw"], at("filt_raw", l, 2 * t + o + 1))
                    raw = ps[2 * t + o]
                    dve.tensor_tensor(f_tmp[:, 0:CH], raw[:, 0:CH], decay[:, t, :], ALU.mult)
                    link(dve.scalar_tensor_tensor(f_tmp[:, CH:2 * CH], raw[:, CH:2 * CH], cst[:, C_MASK + t:C_MASK + t + 1],
                                                  decay[:, t, :], ALU.mult, ALU.mult))
                    dve.tensor_tensor(f_sum[:, t, o * CH:(o + 1) * CH], f_tmp[:, 0:CH], f_tmp[:, CH:2 * CH], ALU.add)
                    last = dve.tensor_tensor(f_dif[:, t, o * CH:(o + 1) * CH], f_tmp[:, 0:CH], f_tmp[:, CH:2 * CH],
                                             ALU.subtract)
                    if o == 0:
                        link(last)
                    else:
                        last.then_inc(s["filt_eo"], 1)
                        dve.wait_ge(s["filt_eo"], at("filt_eo", l, t + 1))
            for c in range(2):
                pe_cols = wuq[:, c, :].rearrange("p (h n) -> p h n", n=QK)
                sw = wuq_sw[:, c, :].rearrange("p (h n) -> p h n", n=ROPE)
                dve.tensor_copy(sw[:, :, 0:ROPE:2], pe_cols[:, :, 65:QK:2])
                last = dve.tensor_copy(sw[:, :, 1:ROPE:2], pe_cols[:, :, 64:QK:2])
            last.then_inc(s["wuq_sw"], 1)
            for col in (0, 1 + P, 2 + TOK):
                link(dve.memset(hy[:, :, col:col + 1], 0.0))

        filters(0)
        dve.wait_ge(s["bmod_in"], 16 * 8 * DEPTH)
        dve.wait_ge(s["mod_zero"], 1)
        for i in range(3 * DEPTH):
            dve.wait_ge(s["chunk_done"], 8 * (i + 1))
            sums = region_a[:, i * 512:(i + 1) * 512]
            dve.tensor_tensor(sums, sums, ps[i % 2][:, :], ALU.add).then_inc(s["mod_sum"], 1)

        for l in range(DEPTH):
            if l > 0:
                filters(l)

            if l > 0:
                dve.wait_ge(s["x2"], at("x2", l - 1))
            else:
                dve.wait_ge(s["x0"], TT)
            modulate(l, 2 * l + 1, "h")
            dve.wait_ge(s["h"], at("h", l))
            link(dve.memset(kpeb[:, :, 0:64], 0.0))

            v4 = uv[:, :, CH:2 * CH].rearrange("p t (h d) -> p t h d", h=4)
            vh4 = vh.rearrange("p t (h d) -> p t h d", h=4)
            sq4 = utok.rearrange("p t (h d) -> p t h d", h=4)

            def per_head(c):
                return st[:, c:c + 12].rearrange("p (t h) -> p t h", t=TT)

            dve.wait_ge(s["uv"], at("uv", l))
            link(dve.tensor_reduce(per_head(0), v4, AX.X, ALU.add))
            link(dve.tensor_scalar(st[:, 0:12], st[:, 0:12], 1.0 / GW, None, ALU.mult))
            link(dve.tensor_tensor(vh4, v4, per_head(0).unsqueeze(3).to_broadcast([P, TT, 4, GW]), ALU.subtract))
            link(dve.tensor_tensor(sq4, vh4, vh4, ALU.mult))
            link(dve.tensor_reduce(per_head(0), sq4, AX.X, ALU.add))
            dve.tensor_scalar(st[:, 0:12], st[:, 0:12], 1.0 / GW, LN_EPS, ALU.mult, ALU.add).then_inc(s["gm_var"], 1)

            dve.wait_ge(s["rms_ss"], at("rms_ss", l))
            dve.tensor_scalar(st[:, 48:51], st[:, 48:51], 1.0 / 256, RMS_EPS, ALU.mult, ALU.add)
            dve.tensor_scalar(st[:, 51:54], st[:, 51:54], 1.0 / 128, RMS_EPS, ALU.mult, ALU.add).then_inc(s["rms_var"], 1)

            dve.wait_ge(s["gm_std"], at("gm_std", l))
            link(dve.reciprocal(st[:, 24:36], st[:, 12:24]))
            link(dve.tensor_tensor(vh4, vh4, per_head(24).unsqueeze(3).to_broadcast([P, TT, 4, GW]), ALU.mult))
            link(dve.tensor_tensor(vh, vh, rows[:, 0:256].unsqueeze(1).to_broadcast([P, TT, 256]), ALU.mult))
            dve.tensor_tensor(vh, vh, rows[:, 256:512].unsqueeze(1).to_broadcast([P, TT, 256]), ALU.add)\
                .then_inc(s["vh"], 1)

            dve.wait_ge(s["rms_std"], at("rms_std", l))
            dve.wait_ge(s["mla"], at("mla", l))
            link(dve.reciprocal(st[:, 70:76], st[:, 54:60]))
            for t in range(TT):
                cq, ckv = mla[:, t, 0:256], mla[:, t, 256:384]
                dve.scalar_tensor_tensor(cq, cq, st[:, 70 + t:71 + t], rows[:, 512:768], ALU.mult, ALU.mult)
                dve.scalar_tensor_tensor(ckv, ckv, st[:, 73 + t:74 + t], rows[:, 768:896], ALU.mult, ALU.mult)
            pe2 = mla[:, 1:3, 384:416]
            cos = cst[:, C_COS:C_COS + 64].rearrange("p (t n) -> p t n", t=2)
            sin = cst[:, C_SIN:C_SIN + 64].rearrange("p (t n) -> p t n", t=2)
            turn = rt[:, 200:264].rearrange("p (t n) -> p t n", t=2)
            dve.tensor_copy(kpeb[:, 0, 64:96], mla[:, 0, 384:416])
            dve.tensor_tensor(kpeb[:, 1:3, 64:96], pe2, cos, ALU.mult)
            dve.tensor_tensor(turn[:, :, 0:ROPE:2], pe2[:, :, 1:ROPE:2], sin[:, :, 0:ROPE:2], ALU.mult)
            link(dve.tensor_tensor(turn[:, :, 1:ROPE:2], pe2[:, :, 0:ROPE:2], sin[:, :, 1:ROPE:2], ALU.mult))
            dve.tensor_tensor(kpeb[:, 1:3, 64:96], kpeb[:, 1:3, 64:96], turn, ALU.add).then_inc(s["mla_n"], 1)

            for hh in range(4):
                if hh % 2 == 0:
                    dve.wait_ge(s["s_raw"], at("s_raw", l, hh // 2 + 1))
                mixed = ps[1 + hh // 2][:, hh % 2 * 192:hh % 2 * 192 + 192].rearrange("p (t n) -> p t n", t=TT)
                u = uv[:, :, hh * GW:(hh + 1) * GW]
                last = dve.scalar_tensor_tensor(u, mixed, bs_c[:, hh:hh + 1], u, ALU.add, ALU.mult)
            last.then_inc(s["a"], 1)

            dve.wait_ge(s["hT_raw"], at("hT_raw", l))
            for c in range(6):
                dve.wait_ge(s["hy"], at("hy", l, c // 2 + 1))
                for o, i, n in ((0, 0, P), (P, P + 1, LAT)):
                    link(dve.tensor_scalar(zc[:, c, o:o + n], hy[:, c, i + 1:i + 1 + n], cw[:, 1, c:c + 1],
                                           cw[:, 3, c:c + 1], ALU.mult, ALU.add))
                    link(dve.scalar_tensor_tensor(zc[:, c, o:o + n], hy[:, c, i:i + n], cw[:, 0, c:c + 1],
                                                  zc[:, c, o:o + n], ALU.mult, ALU.add))
                    last = dve.scalar_tensor_tensor(zc[:, c, o:o + n], hy[:, c, i + 2:i + 2 + n], cw[:, 2, c:c + 1],
                                                    zc[:, c, o:o + n], ALU.mult, ALU.add)
                last.then_inc(s["zc"], 1)
            dve.wait_ge(s["zc"], at("zc", l))
            for o in range(2):
                for b in range(3):
                    dve.wait_ge(s["uf_raw"], at("uf_raw", l, 3 * o + b + 1))
                    uc, us = ps[2 + b][:, 0:CH], ps[2 + b][:, CH:2 * CH]
                    hc, hs = spec[:, b, 0, o * CH:(o + 1) * CH], spec[:, b, 1, o * CH:(o + 1) * CH]
                    for part, (f, g, op) in enumerate(((hc, hs, ALU.subtract), (hs, hc, ALU.add))):
                        dve.tensor_tensor(ytmp[:, 0:CH], uc, f, ALU.mult)
                        link(dve.tensor_tensor(ytmp[:, CH:2 * CH], us, g, ALU.mult))
                        last = dve.tensor_tensor(yfre[:, b, part, :], ytmp[:, 0:CH], ytmp[:, CH:2 * CH], op)
                        if part == 0:
                            link(last)
                    last.then_inc(s["yf"], 1)
                    dve.wait_ge(s["yf"], at("yf", l, 3 * o + b + 1))
                for c in range(2):
                    dve.wait_ge(s["yc_raw"], at("yc_raw", l, 2 * o + c + 1))
                    cur = zc[:, 4 + c, :]
                    link(dve.scalar_tensor_tensor(cur, cur, hyb[:, o, c:c + 1], ps[5 + c][:, 0:TOK], ALU.mult, ALU.add))
                    dst = cur if o == 0 else act_t[:, 2 + c, :]
                    dve.tensor_tensor(dst, cur, zc[:, 2 * o + c, :], ALU.mult).then_inc(s["yc"], 1)
                dve.wait_ge(s["yc"], at("yc", l, 2 * o + 2))

            for hh in range(HEADS):
                b = 2 * (hh % 2)
                dve.wait_ge(s["q_raw"], at("q_raw", l, hh + 1))
                dve.wait_ge(s["q_nope"], at("q_nope", l, hh + 1))
                dst = qT[64:96, hh, P:TOK]
                dve.tensor_tensor(qtmp[64:96, :], ps[b][64:96, P:TOK], ropeT[64:96, 0, :], ALU.mult)
                link(dve.tensor_tensor(dst, ps[b + 1][64:96, 0:LAT], ropeT[64:96, 1, :], ALU.mult))
                dve.tensor_tensor(dst, dst, qtmp[64:96, :], ALU.add).then_inc(s["q_pe"], 1)
                dve.wait_ge(s["q_pe"], at("q_pe", l, hh + 1))
            for hh in range(HEADS):
                b = 2 * (hh % 2)
                dve.wait_ge(s["sc_raw"], at("sc_raw", l, hh + 1))
                dve.reduce_max(st[:, 45:46], ps[b][:, 0:384], AX.X)
                dve.reduce_max(st[:, 46:47], ps[b][:, 384:512], AX.X)
                link(dve.reduce_max(st[:, 47:48], ps[b + 1][:, 0:384], AX.X))
                dve.tensor_scalar(st[:, 36:39], st[:, 45:48], -QK_SCALE, None, ALU.mult).then_inc(s["mx"], 1)
                dve.wait_ge(s["pexp"], at("pexp", l, hh + 1))
                link(dve.reciprocal(st[:, 42:45], st[:, 39:42]))
                for i, (o, n) in enumerate(((0, 384), (384, P), (512, 384))):
                    last = dve.tensor_scalar(probs[:, o:o + n], probs[:, o:o + n], st[:, 42 + i:43 + i], None, ALU.mult)
                last.then_inc(s["pn"], 1)

            dve.wait_ge(s["gate_in"], 32 * (2 * l + 1))
            dve.wait_ge(s["ln_in"], 32 * (2 * l + 2))
            for t in range(TT):
                if t < TT - 1:
                    dve.wait_ge(s["out_raw"], at("out_raw", l, t + 1))
                else:
                    dve.wait_ge(s["chunk_done"], first_chunk(l) + MIX_CHUNKS)
                for half in range(2):
                    cols = slice(half * 512, (half + 1) * 512)
                    last = dve.tensor_tensor(h[:, t, cols], ps[2 * t + half][:, :], modr[:, min(t, 1), cols], ALU.mult)
                link(last)
                link(dve.scalar_tensor_tensor(x[:, t, :], x[:, t, :], ALPHA, h[:, t, :], ALU.mult, ALU.add))
                layer_norm(t, "ln1_var", "ln1_std", "x1", l * 3)
            dve.wait_ge(s["x1"], at("x1", l))
            modulate(l, 2 * l + 2, "h2")

            logits = rt[:, 40:148].rearrange("p (t n) -> p t n", t=TT)

            def col3(c, n=1):
                return rt[:, c:c + 3 * n].rearrange("p (t n) -> p t n", t=TT)

            def const(c, n):
                return cst[:, c:c + n].unsqueeze(1).to_broadcast([P, TT, n])

            def first_max(values, n, c_max, c_eq, c_pri, c_pm, rank, out):
                link(dve.tensor_reduce(rt[:, c_max:c_max + 3], values, AX.X, ALU.max))
                link(dve.tensor_tensor(col3(c_eq, n), values, col3(c_max).to_broadcast([P, TT, n]), ALU.is_ge))
                link(dve.tensor_tensor(col3(c_pri, n), col3(c_eq, n), const(rank, n), ALU.mult))
                link(dve.tensor_reduce(rt[:, c_pm:c_pm + 3], col3(c_pri, n), AX.X, ALU.max))
                return dve.tensor_tensor(out, col3(c_pri, n), col3(c_pm).to_broadcast([P, TT, n]), ALU.is_equal)

            dve.wait_ge(s["lg_raw"], at("lg_raw", l))
            link(dve.tensor_tensor(logits, ps[6][:, 0:108].rearrange("p (t n) -> p t n", t=TT),
                                   rows[:, 896:932].unsqueeze(1).to_broadcast([P, TT, 36]), ALU.add))
            oh = col3(0, 4)
            first_max(logits[:, :, 0:4], 4, 150, 156, 168, 153, C_RANK, oh).then_inc(s["oh"], 1)
            dve.wait_ge(s["oh"], at("oh", l))
            dve.tensor_tensor(col3(280, 4), logits[:, :, 0:4], col3(150).to_broadcast([P, TT, 4]), ALU.subtract)
            prod = rt[:, 184:280].rearrange("p (t g e) -> p t g e", t=TT, g=4)
            for t in range(TT):
                last = dve.tensor_tensor(prod[:, t], logits[:, t, 4:36].rearrange("p (g e) -> p g e", g=4),
                                         oh[:, t, :].unsqueeze(2).to_broadcast([P, 4, 8]), ALU.mult)
            link(last)
            e_in = col3(316, 8)
            link(dve.tensor_reduce(e_in, prod.rearrange("p t g e -> p t e g"), AX.X, ALU.add))
            oh1, oh2, e_2nd = col3(344, 8), col3(392, 8), col3(368, 8)
            link(first_max(e_in, 8, 340, 184, 208, 232, C_GE, oh1))
            link(dve.scalar_tensor_tensor(e_2nd, oh1, -BIG, e_in, ALU.mult, ALU.add))
            link(first_max(e_2nd, 8, 416, 184, 208, 232, C_GE, oh2))
            dve.tensor_tensor(rt[:, 292:295], rt[:, 416:419], rt[:, 340:343], ALU.subtract).then_inc(s["lg_sh"], 1)
            dve.wait_ge(s["lg_exp"], at("lg_exp", l))
            link(dve.tensor_reduce(rt[:, 419:422], col3(300, 4), AX.X, ALU.add))
            link(dve.scalar_tensor_tensor(rt[:, 422:425], rt[:, 312:315], 1.0, rt[:, 419:422], ALU.add, ALU.mult))
            link(dve.reciprocal(rt[:, 425:428], rt[:, 422:425]))
            link(dve.tensor_tensor(rt[:, 428:431], rt[:, 425:428], rt[:, 312:315], ALU.mult))
            link(dve.tensor_tensor(oh1, oh1, col3(425).to_broadcast([P, TT, 8]), ALU.mult))
            link(dve.tensor_tensor(oh2, oh2, col3(428).to_broadcast([P, TT, 8]), ALU.mult))
            link(dve.tensor_tensor(col3(12, 8), oh1, oh2, ALU.add))
            dve.wait_ge(s["cum_raw"], at("cum_raw", l))
            link(dve.tensor_tensor(col3(432, 4), oh, ps[7][:, 0:12].rearrange("p (t n) -> p t n", t=TT), ALU.mult))
            link(dve.tensor_reduce(rt[:, 444:447], col3(432, 4), AX.X, ALU.add))
            link(dve.tensor_scalar(rt[:, 448:451], rt[:, 444:447], float(P), None, ALU.is_ge))
            link(dve.scalar_tensor_tensor(rt[:, 451:454], rt[:, 444:447], 2.0 * P, rt[:, 448:451], ALU.is_ge, ALU.add))
            link(dve.scalar_tensor_tensor(rt[:, 454:457], rt[:, 451:454], -float(P), rt[:, 444:447], ALU.mult, ALU.add))
            link(dve.tensor_scalar(rt[:, 457:461], ps[7][:, 12:16], P + 1.0, None, ALU.is_ge))
            link(dve.scalar_tensor_tensor(rt[:, 457:461], ps[7][:, 12:16], 2.0 * P + 1, rt[:, 457:461], ALU.is_ge, ALU.add))
            link(dve.memset(rt[:, 461:462], 0.0))
            for g in range(GROUPS):
                link(dve.tensor_tensor(rt[:, 462 + g:463 + g], rt[:, 461 + g:462 + g], rt[:, 457 + g:458 + g], ALU.add))
            link(dve.tensor_tensor(col3(432, 4), oh, const(C_GI, 4), ALU.mult))
            link(dve.tensor_reduce(rt[:, 466:469], col3(432, 4), AX.X, ALU.add))
            link(dve.tensor_tensor(col3(432, 4), oh, rt[:, 461:465].unsqueeze(1).to_broadcast([P, TT, 4]), ALU.mult))
            link(dve.tensor_reduce(rt[:, 469:472], col3(432, 4), AX.X, ALU.add))
            link(dve.scalar_tensor_tensor(rt[:, 469:472], rt[:, 469:472], GROUPS - 1.0, rt[:, 451:454], ALU.add, ALU.add))
            link(dve.tensor_tensor(rt[:, 469:472], rt[:, 469:472], rt[:, 466:469], ALU.subtract))
            link(dve.tensor_tensor(rt[:, 469:472], rt[:, 469:472], rt[:, 448:451], ALU.mult))
            link(dve.tensor_tensor(rt[:, 469:472], rt[:, 469:472], rt[:, 466:469], ALU.add))
            n_v = GROUPS + EXTRA
            tgt = col3(474, n_v)
            link(dve.tensor_tensor(tgt, col3(469).to_broadcast([P, TT, n_v]), const(C_VI, n_v), ALU.is_equal))
            link(dve.tensor_scalar(rt[:, 454:457], rt[:, 454:457], 1.0, None, ALU.add))
            dve.tensor_tensor(tgt, tgt, col3(454).to_broadcast([P, TT, n_v]), ALU.mult).then_inc(s["tgt"], 1)
            dve.wait_ge(s["tgt"], at("tgt", l))
            for i in range(EXTRA):
                link(dve.tensor_scalar(rt[:, 432:435], rt[:, 462:465], float(i), None, ALU.is_le))
                link(dve.tensor_reduce(rt[:, 496 + i:497 + i], rt[:, 432:435], AX.X, ALU.add))
            link(dve.tensor_copy(xi[:, 1:3], rt[:, 496:498]))
            dve.tensor_copy(xi[:, 0:1], rt[:, 465:466]).then_inc(s["regs"], 1)
            dve.wait_ge(s["moe_zero"], l + 1)

            def pick(v, e, loop=0):
                for t in range(TT):
                    who = tgt[:, t, bass.ds(loop * 2 + v, 1)]
                    last = dve.tensor_scalar(sel[:, t, :], iota, who, None, ALU.is_equal)
                last.then_inc(e["sel"], 1)

            def gathered(e, half, slot, g, loop=0):
                dve.wait_ge(e["x_hi"], loop * 4 + (2 * g + half + 1))
                tokens = ps[3][:, :].rearrange("p (k n) -> p k n", k=4)
                dve.tensor_tensor(x_lo[:, slot, 4 * half:4 * half + 4, :], tokens,
                                  x_hi[:, slot, 4 * half:4 * half + 4, :].bitcast(F32), ALU.subtract)\
                    .then_inc(e["x_lo"], 1)

            def run(experts, slot0, e, chunk0, v0, loop, rest_in, g0=None):
                q0 = v0 * EPG
                ex_by, v_by, c_by = loop * PAIR, loop * 2, loop * (3 * PAIR)

                def low(c):
                    dve.wait_ge(e["hi"], c_by + (chunk0 + c + 1))
                    dve.tensor_tensor(w_lo[:, c % SPLIT, :], ring[:, c % RING, :], w_hi[:, c % SPLIT, :].bitcast(F32),
                                      ALU.subtract).then_inc(e["lo"], 1)

                def summed(visit, t):
                    dve.wait_ge(e["sct"], v_by * TT + (TT * (v0 + visit) + t + 1))
                    for half in range(2):
                        dst = moe[:, t, half * 512:(half + 1) * 512]
                        last = dve.tensor_tensor(dst, dst, ps[6 + half][:, :], ALU.add)
                    last.then_inc(e["acc"], 1)

                for c in range(SPLIT):
                    low(c)
                for c, (kind, ex) in enumerate(order(experts)):
                    if kind == "G" and ex > 0 or (kind, ex) == ("D", experts - 1):
                        turned = ex - 1 if kind == "G" else ex
                        dve.wait_ge(e["hd_hi"], ex_by + (q0 + turned + 1))
                        dve.tensor_tensor(hd_lo[:, turned % 2, :], ps[2][:, 0:FF],
                                          hd_hi[:, turned % 2, :].bitcast(F32), ALU.subtract).then_inc(e["hd_lo"], 1)
                    if kind == "U":
                        if ex % EPG == 0:
                            sem_in, value, by = rest_in(ex // EPG)
                            dve.wait_ge(sem_in, loop * by + value)
                        dve.wait_ge(e["silu"], ex_by + (q0 + ex + 1))
                        if q0 > 0 or ex >= 2:
                            dve.wait_ge(e["hd_raw"], ex_by + (q0 + ex - 1))
                        sl = (slot0 + ex // EPG) % 2
                        dve.scalar_tensor_tensor(hd[:, ex % 2, :], ps[ex % 2][:, FF:2 * FF],
                                                 wslot[:, sl, ex % EPG:ex % EPG + 1], sg[:, ex % 2, :],
                                                 ALU.mult, ALU.mult).then_inc(e["hid"], 1)
                        if experts == PAIR:
                            if ex in GATHER and GATHER[ex][1] < 2:
                                nth, step = GATHER[ex]
                                gathered(e, step, 1 - nth, g0 + 1 + nth, loop)
                            if ex in SCATTER:
                                summed(0, SCATTER[ex])
                            if ex in (1, 8):
                                nth = ex // 8
                                dve.wait_ge(e["picked"], loop * 2 + (g0 + 1 + nth))
                                pick(1 + nth, e, loop)
                    if c + SPLIT < 3 * experts:
                        low(c + SPLIT)
                for t in range(TT):
                    summed(experts // EPG - 1, t)

            g0 = l * GATHERS
            pick(0, e_main)
            for half in range(2):
                gathered(e_main, half, 0, g0)
            with dve.Fori(0, GROUPS // 2) as it:
                run(PAIR, 0, e_main, l * MOE_CHUNKS, l * GROUPS, it, lambda visit: (e_main["rest"], g0 + visit + 1, 2), g0)
            dve.wait_ge(e_main["acc"], TT * GROUPS * (l + 1))
            extra = dve.value_load(xi[0:1, 0:1], min_val=0, max_val=EXTRA)
            xe = e_extra[l]
            with dve.If(extra >= 1):
                run(EPG, 0, xe, 0, 0, 0, lambda visit: (e_main["rest"], g0 + GATHERS, 0))
                dve.wait_ge(xe["acc"], TT)
                with dve.If(extra >= 2):
                    dve.wait_ge(e_main["picked"], g0 + GATHERS)
                    pick(5, xe)
                    for half in range(2):
                        gathered(xe, half, 1, 0)
                    run(EPG, 1, xe, EPG * 3, 1, 0, lambda visit: (xe["rest"], 1, 0))
                    dve.wait_ge(xe["acc"], 2 * TT)

            dve.wait_ge(s["gate_in"], 32 * (2 * l + 2))
            dve.wait_ge(s["ln_in"], 32 * (2 * l + 3))
            for t in range(TT):
                link(dve.tensor_tensor(moe[:, t, :], moe[:, t, :], modr[:, min(t, 1), :], ALU.mult))
                link(dve.scalar_tensor_tensor(x[:, t, :], x[:, t, :], ALPHA, moe[:, t, :], ALU.mult, ALU.add))
                layer_norm(t, "ln2_var", "ln2_std", "x2", l * 3)

    ctx.close()


def packed(w):
    def flat(name):
        return np.asarray(w[name]).reshape(DEPTH, -1)

    def by_partition(name, outer):
        v = np.asarray(w[name]).reshape(DEPTH, outer, -1, P)
        return v.transpose(0, 3, 1, 2).reshape(DEPTH, P, -1)

    router = np.concatenate([np.asarray(w["moe_w_gr"]), np.asarray(w["moe_w_er"]).reshape(DEPTH, D, -1)], 2)
    columns = [by_partition("gm_bs", 4), by_partition("hy_conv_w", 3), by_partition("hy_conv_b", 1),
               by_partition("hy_bias", 2)]
    w1 = np.zeros((DEPTH, FH, FH), np.float32)
    w1[:, :EMB] = np.asarray(w["hy_f_w1"])
    return dict(
        rows=np.concatenate([flat(n) for n in ("gm_ln_g", "gm_ln_b", "mla_gq", "mla_gkv", "moe_b_gr", "moe_b_er")], 1),
        cols=np.concatenate(columns, 2),
        fw=np.concatenate([w1, np.asarray(w["hy_f_w2"]), np.asarray(w["hy_f_b1"])[:, :, None],
                           np.asarray(w["hy_f_b2"])[:, :, None], np.asarray(w["hy_f_freq"]).transpose(0, 2, 1)], 2),
        gm_ws_t=np.asarray(w["gm_ws"]).transpose(0, 3, 1, 2).reshape(DEPTH, P, -1),
        w_router=router.reshape(DEPTH, P, -1),
    )


def tables():
    f8 = np.float64
    cst = np.zeros((P, C_END))
    cst[:, C_ID:C_ID + P] = np.eye(P)
    cst[:, C_TRI:C_TRI + P] = np.triu(np.ones((P, P)), 1)
    cst[:, C_ONE:C_ONE + P] = 1.0
    cst[:, C_IOTA:C_IOTA + P] = np.arange(1, P + 1)
    cst[:, C_RANK:C_RANK + 4] = np.arange(4, 0, -1)
    cst[:, C_GE:C_GE + 8] = np.arange(8, 0, -1)
    cst[:, C_GI:C_GI + 4] = np.arange(4)
    cst[:, C_VI:C_VI + 6] = np.arange(6)
    cst[:, C_MASK:C_MASK + 3] = 1.0
    cst[0, C_MASK:C_MASK + 2] = 0.0
    n = ROPE // 4
    inv = (np.float32(10000.0) ** (-np.arange(n, dtype=np.float32) / np.float32(n))).astype(np.float32)
    p = np.arange(LAT)
    ang = np.concatenate([(p // 64)[:, None].astype(np.float32) * inv, (p % 64)[:, None].astype(np.float32) * inv], 1)
    cos = np.repeat(np.cos(ang.astype(f8)), 2, axis=1)
    sin = np.repeat(np.sin(ang.astype(f8)), 2, axis=1)
    sin[:, 0::2] *= -1.0
    cst[:, C_COS:C_COS + 64] = cos.reshape(2, P, ROPE).transpose(1, 0, 2).reshape(P, 64)
    cst[:, C_SIN:C_SIN + 64] = sin.reshape(2, P, ROPE).transpose(1, 0, 2).reshape(P, 64)
    rope_t = np.stack([cos.T, sin.T], 1)
    dft = np.zeros((P, DFT_COLS))
    for L, oc, osn, oct_, ost in ((P, G_C, G_S, G_CT, G_ST), (LAT, F_C, F_S, F_CT, F_ST)):
        arg = np.pi * np.outer(np.arange(L), 2 * np.arange(L) + 1) / (2 * L)
        for o, m in ((oc, np.cos(arg)), (osn, np.sin(arg)), (oct_, np.cos(arg).T / L), (ost, np.sin(arg).T / L)):
            dft[:, o:o + L * L // P] = m.reshape(L // P, P, L).transpose(1, 0, 2).reshape(P, -1)
    feats, decays = [], []
    deltas = np.abs(np.linspace(math.log(1e-2) / 1.5, math.log(1e-2) / 0.3, CH))
    for L in (P, LAT):
        t = np.linspace(0.0, 1.0, L)[:, None]
        bands = (EMB - 1) // 2
        w = 2.0 * math.pi * np.arange(L)[:, None] / L
        f = np.linspace(1e-4, bands - 1, bands)[None]
        feats.append(np.concatenate([t, np.cos(f * w), -np.sin(f * w)], -1))
        decays.append(np.exp(-t * deltas))
    z_t = np.concatenate(feats, 0).T
    decay = np.concatenate(decays, 0).reshape(TT, P, CH).transpose(1, 0, 2)
    out = dict(consts=cst, rope_t=rope_t, dft=dft, z_t=z_t, decay=decay)
    return {k: np.ascontiguousarray(v, dtype=np.float32) for k, v in out.items()}


_INS = ("x_prompt", "x_sample", "c", "cache_ckv", "cache_kpe", "c_ctx", "ln_in_g", "ln_in_b", "w_mod", "b_mod", "w_in",
        "hy_f_w3", "mla_wuq", "mla_wukv", "w_out", "ln1_g", "ln1_b", "ln2_g", "ln2_b",
        "moe_w_gate", "moe_w_up", "moe_w_down")
_OUTS = ((1, P, D), (1, LAT, D), (1, DEPTH, P, P), (1, DEPTH, P, ROPE))


def kernel(**inputs):
    import concourse.bacc as _bacc
    from concourse.bass_utils import run_bass_kernel_spmd as _run

    nc = _bacc.Bacc("TRN2", target_bir_lowering=False, num_devices=1)
    arrays, aps = {}, {}
    for name, value in [(n, inputs[n]) for n in _INS] + list(packed(inputs).items()) + list(tables().items()):
        arr = np.ascontiguousarray(value)
        arrays[f"in_{name}"] = arr
        aps[name] = nc.dram_tensor(f"in_{name}", arr.shape, mybir.dt.from_np(arr.dtype), kind="ExternalInput").ap()
    outs = [nc.dram_tensor(f"out_{i}", shape, F32, kind="ExternalOutput").ap() for i, shape in enumerate(_OUTS)]
    build(nc, aps, outs)
    r = _run(nc, [arrays], core_ids=[0])
    return tuple(r.results[0][f"out_{i}"] for i in range(len(_OUTS)))
```

```python
from contextlib import ExitStack
import math

import numpy as np
import concourse.bass as bass
from concourse import mybir

F32 = mybir.dt.float32
F32R = mybir.dt.float32r
I32 = mybir.dt.int32
ACT = mybir.ActivationFunctionType
ALU = mybir.AluOpType
AX = mybir.AxisListType

P = 128
D = 1024
K8 = D // P
DEPTH = 2
TT = 3
TOK = TT * P
LAT = 2 * P
KEYS = 4 * P
GW = 64
HEADS = 8
QK = 96
ROPE = 32
CH = 256
FH = 64
EMB = 33
MLA_COLS = 416
GROUPS = 4
EPG = 8
FF = 256
EXTRA = 2
RING = 4
SPLIT = 3
CHUNK = 2048
MOD_CHUNKS = 6 * D // 256
MOD_GROUP = 8
MOD_GROUPS = DEPTH * MOD_CHUNKS // MOD_GROUP
IN_CHUNKS = ((0, 256), (256, 256), (512, 256), (768, 256), (1024, 256), (1280, 144), (1424, 136), (1560, 136))
OUT_CHUNKS = 4
MOE_CHUNKS = GROUPS * EPG * 3
ALPHA = (2.0 * DEPTH) ** 0.25
LN_EPS = 1e-5
RMS_EPS = 1e-6
QK_SCALE = 1.0 / math.sqrt(QK)
SMALL_LOADS = 4
MAGIC = 1.5 * 2.0 ** 23
TWO_PI_HI = 6.28125
TWO_PI_LO = 2.0 * math.pi - 6.28125
PI_SAFE = 3.1415925
BIG = 1.0e30

C_ID, C_TRI, C_ONE, C_IOTA = 0, 128, 256, 384
C_RANK, C_GE, C_COS, C_SIN = 512, 516, 524, 588
C_GI, C_VI, C_MASK = 652, 656, 662
C_END = 665
F_C, F_S, F_CT, F_ST = 128, 640, 1280, 1792
G_C, G_S, G_CT, G_ST = 0, 1152, 2304, 2432
DFT_COLS = 2560

A_U = 4 * D
A_MLA = A_U + 2304
A_UTOK = A_MLA + TT * MLA_COLS
A_DFT = A_UTOK + TT * CH
ARENA = 2 * D + 2 * SPLIT * CHUNK
A_CT = A_DFT + DFT_COLS
assert A_CT + 34 * K8 <= ARENA - MOD_GROUPS * 512

MOD_START = [(0, i) for i in range(MOD_GROUP)] + [(1, i) for i in range(4)]
MOD_REST = [(1, i) for i in range(4, MOD_GROUP)] + [(g, i) for g in range(2, 6) for i in range(MOD_GROUP)]
AFTER_IN = (3, 3, 4, 4, 4, 3, 3, 3)
FILL = [MOD_REST[sum(AFTER_IN[:c]):sum(AFTER_IN[:c + 1])] for c in range(len(IN_CHUNKS))]
MOD_LATE = MOD_REST[sum(AFTER_IN):]
LATE_STEPS = 5


def stream():
    out = [("mod", *m) for m in MOD_START]
    for l in range(DEPTH):
        for c in range(len(IN_CHUNKS)):
            out += [("in", l, c)] + ([("mod", *m) for m in FILL[c]] if l == 0 else [])
        if l == 0:
            out += [("mod", *m) for m in MOD_LATE]
        out += [("out", l, c) for c in range(OUT_CHUNKS)]
    return out


STREAM = stream()
PLACE = {chunk: n for n, chunk in enumerate(STREAM)}
SPEC_BANKS = (((0, 1), (2, 3), (4, 5)), ((6, 7), (4, 5), (6, 7)))
HT_BANKS = ((6, 0, 1, 2, 3, 4, 5, 6), (6, 7, 6, 7, 0, 6, 1, 7))
MOD_BANK = (6, 7, 7, 7, 7, 7)
MOD_OUTS = 2

SOFT_COLS = (36, 0)

PER = dict(
    filt_in=1, hid_in=1, sin_in=2, hid=2, filt_raw=6, filt_eo=3, spec_raw=3, spec=3, 
    h=3, hT_raw=8, hT=8, uv=3, hy=3, mla=3,
    zc=6, gm_var=1, gm_std=1, vh=1, s_raw=2, a=1, aT_raw=2, aT=2,
    rms_ss=1, rms_var=1, rms_std=1, mla_n=1, wuq_sw=1, latT_raw=4, latT=4,
    ut_raw=4, ut=4, uf_raw=6, yf=6, yc_raw=4, yc=4,
    q_raw=8, q_nope=8, q_pe=8, k_raw=4, kT=4, v_raw=4, v=4,
    sc_raw=8, mx=8, pexp=8, pn=8, pT_raw=16, pT=16, pv=8, oT=4, out_raw=2,
    x1=3, h2=3, h2T_raw=6, h2T=6, lg_raw=1, oh=1, lg_sh=1, lg_exp=1, cum_raw=1, tgt=1, regs=1,
    x2=3,
)


def pos(kind, e, experts):
    if kind == "D":
        return 3 * e + 4 if e < experts - 1 else 3 * e + 2
    return (0 if e == 0 else 3 * e - 1) + (kind == "U")


def order(experts):
    return [(k, e) for _, k, e in sorted((pos(k, e, experts), k, e) for k in "GUD" for e in range(experts))]


PAIR = 2 * EPG
LAST_BANKS = (6, 4, 6)
GATHERS = GROUPS + 1
GATHER = {3: (0, 0), 4: (0, 1), 5: (0, 2), 12: (1, 0), 13: (1, 1), 14: (1, 2)}
SCATTER = {9: 0, 10: 1, 11: 2}


def build(nc, a, outs):
    ctx = ExitStack()

    def sb(name, shape, dt=F32):
        return ctx.enter_context(nc.sbuf_tensor(name, shape, dt))

    def sem(name):
        return ctx.enter_context(nc.semaphore(name))

    ps = [ctx.enter_context(nc.psum_tensor(f"bank{i}", [P, 512], F32)) for i in range(8)]
    ring = sb("ring", [P, RING, CHUNK])
    x = sb("x", [P, TT, D])
    region_a = sb("region_a", [P, TT * D])
    act_t = sb("act_t", [P, K8, TOK])
    arena = sb("arena", [P, ARENA])
    arena_at = nc.sbuf_base - 4 * ARENA
    gates = arena[:, 0:2 * D].rearrange("p (a d) -> p a d", a=2)
    lat_shift = arena[:, 2 * D:3 * D]
    lnr = sb("lnr", [P, 2, D])
    region_k = sb("region_k", [P, 4096])
    region_k_at = nc.sbuf_base - 4 * 4096
    region_s = sb("region_s", [P, TT * D])
    region_q = sb("region_q", [P, HEADS * TOK])
    region_q_at = nc.sbuf_base - 4 * HEADS * TOK
    region_v = sb("region_v", [P, 2048])
    region_v_at = nc.sbuf_base - 4 * 2048
    region_u = arena[:, A_U:A_U + 2304]
    mla = arena[:, A_MLA:A_MLA + TT * MLA_COLS].rearrange("p (t n) -> p t n", t=TT)
    utok = arena[:, A_UTOK:A_UTOK + TT * CH].rearrange("p (t n) -> p t n", t=TT)
    dft = arena[:, A_DFT:A_DFT + DFT_COLS]
    cst = sb("cst", [P, C_END])
    ropeT = sb("ropeT", [QK, 2, LAT])
    region_w = sb("region_w", [P, 2048])
    region_w_at = nc.sbuf_base - 4 * 2048
    wuq = region_w[:, 0:2 * HEADS * QK].rearrange("p (c n) -> p c n", c=2)
    wuq_sw = region_w[:, 2 * HEADS * QK:2048].rearrange("p (c n) -> p c n", c=2)
    wukv = sb("wukv", [P, HEADS * 128])
    wsT = sb("wsT", [P, 4, P])
    wr = sb("wr", [P, K8, 36])
    rows = sb("rows", [P, 932])
    cols = sb("cols", [P, 32])
    fw = sb("fw", [FH, DEPTH, 132])
    st = sb("st", [P, 128])
    xi = sb("xi", [P, 4], I32)

    bs_c = cols[:, 0:4]
    cw = cols[:, 4:28].rearrange("p (j c) -> p j c", j=4)
    hyb = cols[:, 28:32].rearrange("p (o c) -> p o c", o=2)
    w_hi = nc.alloc_sbuf_tensor_at("w_hi", [P, SPLIT, CHUNK], F32R, offset=arena_at + 4 * 2 * D)
    w_lo = nc.alloc_sbuf_tensor_at("w_lo", [P, SPLIT, CHUNK], F32R, offset=arena_at + 4 * (2 * D + SPLIT * CHUNK))
    x_hi = nc.alloc_sbuf_tensor_at("x_hi", [P, 2, K8, P], F32R, offset=region_k_at)
    x_lo = nc.alloc_sbuf_tensor_at("x_lo", [P, 2, K8, P], F32R, offset=region_k_at + 4 * 2 * K8 * P)
    hd_hi = nc.alloc_sbuf_tensor_at("hd_hi", [P, 2, FF], F32R, offset=region_v_at + 4 * 768)
    hd_lo = nc.alloc_sbuf_tensor_at("hd_lo", [P, 2, FF], F32R, offset=region_q_at + 4 * 2432)
    mod_sums = arena[:, ARENA - MOD_GROUPS * 512:ARENA]
    y_hi = nc.alloc_sbuf_tensor_at("y_hi", [P, D], F32R, offset=region_q_at + 4 * 384)
    y_lo = nc.alloc_sbuf_tensor_at("y_lo", [P, D], F32R, offset=region_w_at + 4 * D)
    selT = nc.alloc_sbuf_tensor_at("selT", [P, 2, TT, P], F32R, offset=region_v_at)
    cT = arena[:, A_CT:A_CT + 32 * K8].rearrange("p (k n) -> p k n", k=K8)
    craw = arena[:, A_CT + 32 * K8:A_CT + 34 * K8].rearrange("p (c k) -> p c k", c=2)
    h = region_a[:].rearrange("p (t d) -> p t d", t=TT)
    zc = region_a[:, 0:6 * TOK].rearrange("p (c t) -> p c t", c=6)
    kT = region_k[:].rearrange("p (h t) -> p h t", h=HEADS)
    v_sb = region_v[:].rearrange("p (k n) -> p k n", k=4)
    spec = region_s[:].rearrange("p (b c n) -> p b c n", b=3, c=2)
    hy = region_q[:, 0:6 * 387].rearrange("p (c t) -> p c t", c=6)
    qT = region_q[:].rearrange("p (h t) -> p h t", h=HEADS)
    uv = region_u[:, 0:1536].rearrange("p (t n) -> p t n", t=TT)
    vh = region_u[:, 1536:2304].rearrange("p (t n) -> p t n", t=TT)
    probs = (region_u[:, 0:896], dft[:, 0:896])
    probsT = region_u[:, 896:1792].rearrange("p (b n) -> p b n", n=128)
    yfre = region_v[:, 0:1536].rearrange("p (b c n) -> p b c n", b=3, c=2)
    ytmp = region_v[:, 1536:2048]
    f_sum = region_k[:, 0:1536].rearrange("p (t n) -> p t n", t=TT)
    f_dif = region_k[:, 1536:3072].rearrange("p (t n) -> p t n", t=TT)
    w3 = region_k[0:FH, 3072:4096]
    decay = region_v[:, 0:768].rearrange("p (t n) -> p t n", t=TT)
    f_tmp = region_v[:, 768:1280]
    f_arg = region_u[0:FH, 0:384]
    f_n = region_u[0:FH, 384:768]
    hid1 = region_u[0:FH, 768:1152]
    hid2 = (region_u[0:FH, 1152:1536], ropeT[0:FH].rearrange("p c n -> p (c n)")[:, 0:TOK])
    zT = region_u[0:EMB, 1536:1920]
    rows_by_half = [r.rearrange("p (a d) -> p a d", a=3) for r in (act_t[:].rearrange("p k t -> p (k t)"), region_s[:])]
    next_lat_shift = wukv[:]
    spare = arena[:, 0:4 * D]
    cqT = spare[:, 2048:2816].rearrange("p (c t) -> p c t", c=2)
    ckvT = spare[:, 2816:3328]
    kpeb = spare[:, 3328:3712].rearrange("p (t n) -> p t n", t=4)
    cckv = spare[:, 3712:3840]
    qtmp = spare[:, 3840:4096]
    moe = region_s[:].rearrange("p (t d) -> p t d", t=TT)
    sel = region_q[:, 0:384].rearrange("p (t n) -> p t n", t=TT)
    sg = region_q[:, 1408:1920].rearrange("p (b n) -> p b n", b=2)
    hd = region_q[:, 1920:2432].rearrange("p (b n) -> p b n", b=2)
    rt = region_v[:, 1536:2048]
    wslot = region_q[:, 2944:2960].rearrange("p (v n) -> p v n", n=8)

    ident = cst[:, C_ID:C_ID + P]
    tri = cst[:, C_TRI:C_TRI + P]
    ones = cst[:, C_ONE:C_ONE + P]
    iota = cst[:, C_IOTA:C_IOTA + P]

    s = {name: sem(name) for name in PER}
    for name in ("x_in", "cond_in", "mlp_in", "taps_in", "cT", "mod_zero", "bmod_in", "mod_sum", "mod_out", "mod0_out",
                 "ln_var", "ln_std", "ln_scale", "normed", "pool_step", "x0", "chunk_done", "small_in", "cache_in",
                 "mod12_in", "moe_zero", "gate_in", "ln_in", "dve_step", "state_out", "y_out"):
        s[name] = sem(name)
    ring_full = [sem(f"ring_full{i}") for i in range(RING)]
    MOE_NAMES = ("hi", "lo", "done", "sel", "x_raw", "x_hi", "x_lo", "picked", "rest", "silu", "hid", "hd_raw",
                 "hd_hi", "hd_lo", "y", "sct", "acc")
    e_main = {n: sem("e_" + n) for n in MOE_NAMES}
    e_extra = [{n: sem(f"x{l}_" + n) for n in MOE_NAMES} for l in range(DEPTH)]
    moe_full = [sem(f"moe_full{i}") for i in range(RING)]
    x_full = [[sem(f"x{l}_full{i}") for i in range(RING)] for l in range(DEPTH)]

    def at(name, l, i=None):
        return l * PER[name] + (PER[name] if i is None else i)

    mod_dram = nc.dram_tensor("mod_rows", (DEPTH, 2, 6 * D), F32, kind="Internal").ap()

    def last_chunk(kind, l, c):
        return PLACE[kind, l, c] + 1

    def mod_rows(l, c, i0, n):
        return mod_dram[l, c:c + 1, i0 * D:(i0 + n) * D].rearrange("a (b j n) -> a b j n", j=4, n=64)

    def store_group(engine, g, done="mod_out"):
        engine.wait_ge(s["mod_sum"], g + 1)
        for c in range(2):
            dst = mod_rows(g // 3, c, g % 3 * 2, 2).rearrange("a b j n -> (a j) b n")
            src = mod_sums[c:P:32, g * 512:(g + 1) * 512]
            engine.dma_start(dst, src.rearrange("p (b n) -> p b n", n=64)).then_inc(s[done], 16)

    def norms(l, which, i=TT):
        return (0 if l < 0 else TT * (2 * l + which)) + i

    def fused_steps(l):
        return (l - 1) * (2 * TT + 8) + TT + 8

    def fuse_rows(engine, link, three, shift_lat, tmp):
        for scale, shift in ((three[:, 1, :], three[:, 0, :]), (three[:, 2, :], shift_lat)):
            link(engine.tensor_scalar(scale, scale, 1.0, None, ALU.add))
            link(engine.tensor_tensor(tmp, scale, lnr[:, 1, :], ALU.mult))
            link(engine.tensor_tensor(shift, shift, tmp, ALU.add))
            link(engine.tensor_tensor(scale, scale, lnr[:, 0, :], ALU.mult))

    block = ctx.enter_context(nc.Block())

    @block.sync
    def _(sp):
        sp.dma_start(fw[:], a["fw"].rearrange("l p n -> p l n")).then_inc(s["mlp_in"], 16)
        sp.dma_start(zT, a["z_t"]).then_inc(s["mlp_in"], 16)
        sp.dma_start(craw[:, 0, :], a["c_ctx"].rearrange("(p k) -> p k", k=K8)).then_inc(s["cond_in"], 16)
        sp.dma_start(craw[:, 1, :], a["c"].rearrange("a (p k) -> p (a k)", k=K8)).then_inc(s["cond_in"], 16)

        def slot(n, cols, k):
            return ring[:, n % RING, 0:cols * k].rearrange("p (k n) -> p k n", k=k)

        for l in range(DEPTH):
            first = 0 if l == 0 else PLACE["in", l, 0]
            n1 = last_chunk("out", l, OUT_CHUNKS - 1)
            wi = a["w_in"][l].rearrange("(p k) n -> p k n", k=K8)
            wo = a["w_out"][l].rearrange("(k p) n -> p k n", p=P)
            for n in range(first, n1):
                kind, g, c = STREAM[n]
                if kind == "mod":
                    i = g * MOD_GROUP + c
                    wm = a["w_mod"][i // MOD_CHUNKS].rearrange("(p k) n -> p k n", k=K8)
                    dst, src = slot(n, 256, K8), wm[:, :, i % MOD_CHUNKS * 256:(i % MOD_CHUNKS + 1) * 256]
                elif kind == "in":
                    c0, width = IN_CHUNKS[c]
                    dst, src = slot(n, width, K8), wi[:, :, c0:c0 + width]
                else:
                    dst, src = slot(n, D, 2), wo[:, 2 * c:2 * c + 2, :]
                if n - RING >= first:
                    sp.wait_ge(s["chunk_done"], n - RING + 1)
                sp.dma_start(dst, src).then_inc(ring_full[n % RING], 16)
            w_of = {"G": a["moe_w_gate"][l], "U": a["moe_w_up"][l], "D": a["moe_w_down"][l]}

            def expert(kind, e):
                return w_of[kind][bass.ds(e, 1)].rearrange("a (p k) n -> p (a k n)", k=2 if kind == "D" else K8)

            sp.wait_ge(s["chunk_done"], n1)
            with sp.Fori(0, GROUPS // 2) as it:
                for i, (kind, e) in enumerate(order(PAIR)):
                    sp.wait_ge(e_main["lo"], it * (3 * PAIR) + (l * MOE_CHUNKS + i + 1))
                    sp.dma_start(ring[:, i % RING, :], expert(kind, it * PAIR + e)).then_inc(moe_full[i % RING], 16)
            sp.wait_ge(s["regs"], at("regs", l))
            extra = sp.value_load(xi[0:1, 0:1], min_val=0, max_val=EXTRA)

            def extra_loads(i):
                g = sp.value_load(xi[0:1, 1 + i:2 + i], min_val=0, max_val=GROUPS - 1)
                for j, (kind, e) in enumerate(order(EPG)):
                    if i == 0 and j < RING:
                        sp.wait_ge(e_main["lo"], (l + 1) * MOE_CHUNKS + j + 1)
                    sp.wait_ge(e_extra[l]["lo"], i * EPG * 3 + j + 1)
                    sp.dma_start(ring[:, j % RING, :], expert(kind, g * EPG + e)).then_inc(x_full[l][j % RING], 16)

            with sp.If(extra >= 1):
                extra_loads(0)
                with sp.If(extra >= 2):
                    extra_loads(1)
                    sp.wait_ge(e_extra[l]["lo"], RING + 2 * EPG * 3)
                sp.wait_ge(e_extra[l]["lo"], RING + EPG * 3)
            if l + 1 < DEPTH:
                sp.wait_ge(e_main["lo"], RING + (l + 1) * MOE_CHUNKS)

    @block.gpsimd
    def _(pool):
        def row(dst, src):
            return pool.dma_start(dst, src.rearrange("(a n) -> a n", a=1).to_broadcast([P, src.shape[0]]))

        row(lnr[:, 0, :], a["ln_in_g"]).then_inc(s["ln_in"], 16)
        row(lnr[:, 1, :], a["ln_in_b"]).then_inc(s["ln_in"], 16)
        steps = [0]

        def link(ins):
            steps[0] += 1
            ins.then_inc(s["pool_step"], 1)
            pool.wait_ge(s["pool_step"], steps[0])

        def affine(t, done):
            link(pool.tensor_tensor(x[:, t, :], x[:, t, :], lnr[:, 0, :], ALU.mult))
            pool.tensor_tensor(x[:, t, :], x[:, t, :], lnr[:, 1, :], ALU.add).then_inc(s[done], 1)

        def mod_row(dst, l, c, i):
            src = mod_dram[l, c:c + 1, i * D:(i + 1) * D]
            return pool.dma_start(dst, src.to_broadcast([P, D]))

        def half_rows(l, half):
            for i, (c, what) in enumerate(((0, 0), (0, 1), (1, 1))):
                mod_row(rows_by_half[half][:, i, :], l, c, 3 * half + what).then_inc(s["mod12_in"], 16)

        for l in range(DEPTH):
            if l > 0:
                pool.wait_ge(s["lg_exp"], at("lg_exp", l - 1))
                pool.wait_ge(s["lg_raw"], at("lg_raw", l - 1))
                pool.wait_ge(s["v_raw"], at("v_raw", l - 1))

            def load_taps():
                pool.dma_start(w3, a["hy_f_w3"][l]).then_inc(s["taps_in"], 16)
                pool.dma_start(decay, a["decay"]).then_inc(s["taps_in"], 16)
                pool.dma_start(dft, a["dft"]).then_inc(s["taps_in"], 16)

            if l == 0:
                pool.wait_ge(s["chunk_done"], 3)
                load_taps()
                pool.wait_ge(s["mod0_out"], 16 * MOD_OUTS)
                mod_row(next_lat_shift, l, 1, 0).then_inc(s["mod12_in"], 16)
                half_rows(l, 0)
            small = s["small_in"]
            row(rows[:], a["rows"][l]).then_inc(small, 16)
            pool.dma_start(cols[:], a["cols"][l]).then_inc(small, 16)
            pool.dma_start(wsT[:].rearrange("p h q -> p (h q)"), a["gm_ws_t"][l]).then_inc(small, 16)
            pool.dma_start(wr[:].rearrange("p k n -> p (k n)"), a["w_router"][l]).then_inc(small, 16)

            if l > 0:
                pool.wait_ge(s["ln_var"], norms(l - 1, 2, 1))
                load_taps()
                for t in range(TT):
                    pool.wait_ge(s["h"], at("h", l, t + 1))
                    affine(t, "x2")
            pool.wait_ge(s["h"], at("h", l))
            pool.dma_start(wuq, a["mla_wuq"][l].rearrange("(c p) n -> p c n", p=P)).then_inc(s["cache_in"], 16)
            pool.dma_start(wukv[:], a["mla_wukv"][l]).then_inc(s["cache_in"], 16)
            pool.dma_start(cckv, a["cache_ckv"][0, l]).then_inc(s["cache_in"], 16)
            if l == 0:
                pool.wait_ge(s["x0"], TT)
            else:
                pool.wait_ge(s["x2"], at("x2", l - 1))
            row(lnr[:, 0, :], a["ln1_g"][l]).then_inc(s["ln_in"], 16)
            row(lnr[:, 1, :], a["ln1_b"][l]).then_inc(s["ln_in"], 16)
            pool.dma_start(kpeb[:, 3, 64:96], a["cache_kpe"][0, l]).then_inc(s["cache_in"], 16)
            if l == 0:
                store_group(pool, 1)
                pool.wait_ge(s["mod_out"], 16 * MOD_OUTS)
            for c in range(2):
                mod_row(gates[:, c, :], l, c, 2).then_inc(s["gate_in"], 16)
            if l == 0:
                store_group(pool, 2)
            pool.wait_ge(s["mla_n"], at("mla_n", l))
            pool.dma_start(outs[2][0, l], mla[:, 0, 256:384]).then_inc(s["state_out"], 16)
            pool.dma_start(outs[3][0, l], mla[:, 0, 384:416]).then_inc(s["state_out"], 16)
            pool.wait_ge(s["yc"], at("yc", l))
            if l == 0:
                for g in range(3, MOD_GROUPS):
                    store_group(pool, g)
                pool.wait_ge(s["mod_out"], 16 * MOD_OUTS * (MOD_GROUPS - 1))
            half_rows(l, 1)
            pool.wait_ge(s["v_raw"], at("v_raw", l))
            mod_row(lat_shift, l, 1, 3).then_inc(s["mod12_in"], 16)
            for t in range(TT):
                pool.wait_ge(s["h2"], at("h2", l, t + 1))
                affine(t, "x1")
            pool.wait_ge(s["x1"], at("x1", l))
            row(lnr[:, 0, :], a["ln2_g"][l]).then_inc(s["ln_in"], 16)
            row(lnr[:, 1, :], a["ln2_b"][l]).then_inc(s["ln_in"], 16)
            for c in range(2):
                mod_row(gates[:, c, :], l, c, 5).then_inc(s["gate_in"], 16)
            pool.memset(region_s[:], 0.0).then_inc(s["moe_zero"], 1)
            if l + 1 < DEPTH:
                pool.wait_ge(s["lg_raw"], at("lg_raw", l))
                half_rows(l + 1, 0)
                mod_row(next_lat_shift, l + 1, 1, 0).then_inc(s["mod12_in"], 16)
                pool.wait_ge(s["mod12_in"], 64 * (2 * l + 3))
                pool.wait_ge(s["ln_in"], 32 * (2 * l + 3))
                fuse_rows(pool, link, rows_by_half[0], next_lat_shift, region_w[:, 0:D])
        for t in range(TT):
            pool.wait_ge(s["x2"], at("x2", DEPTH - 1, t + 1))
            dst = outs[0][0] if t == 0 else outs[1][0, (t - 1) * P:t * P]
            pool.dma_start(dst, x[:, t, :]).then_inc(s["y_out"], 16)
        pool.wait_ge(s["state_out"], 16 * 2 * DEPTH)
        pool.wait_ge(s["y_out"], 16 * TT)

    @block.tensor
    def _(pe):

        def filter_hidden(l, i):
            if i == 0:
                if l > 0:
                    pe.wait_ge(s["sin_in"], at("sin_in", l - 1))
                pe.matmul(ps[7][0:FH, 0:TOK], fw[0:EMB, l, 0:64], zT, start=True, stop=True).then_inc(s["filt_in"], 1)
            else:
                pe.wait_ge(s["hid"], at("hid", l, 1))
                pe.matmul(ps[7][0:FH, 0:TOK], fw[:, l, 64:128], hid1, start=True, stop=True).then_inc(s["hid_in"], 1)

        def filter_taps(l):
            pe.wait_ge(s["taps_in"], 48 * (l + 1))
            pe.wait_ge(s["hid"], at("hid", l))
            for t in range(TT):
                for o in range(2):
                    pe.matmul(ps[2 * t + o][:, :], hid2[l][:, t * P:(t + 1) * P], w3[:, o * 512:(o + 1) * 512],
                              start=True, stop=True).then_inc(s["filt_raw"], 1)

        def filter_spectra(l):
            pe.wait_ge(s["filt_eo"], at("filt_eo", l))
            for b in range(3):
                tiles = (0,) if b == 0 else (1, 2)
                if b == 2 and l > 0:
                    pe.wait_ge(s["spec"], at("spec", l, 1))
                for part, (m_ctx, m_lat, src) in enumerate(((G_C, F_C, f_sum), (G_S, F_S, f_dif))):
                    for i, t in enumerate(tiles):
                        o = m_ctx if b == 0 else m_lat + i * 256 + (b - 1) * P
                        mm = pe.matmul(ps[SPEC_BANKS[l][b][part]][:, :], dft[:, o:o + P], src[:, t, :],
                                       start=(i == 0), stop=(i == len(tiles) - 1))
                mm.then_inc(s["spec_raw"], 1)

        def loaded(kind, l, c):
            n = PLACE[kind, l, c]
            pe.wait_ge(ring_full[n % RING], 16 * (n // RING + 1))
            return ring[:, n % RING, :]

        def mod_sums(chunks):
            for g, c in chunks:
                if c == 0 and g >= 2:
                    pe.wait_ge(s["mod_sum"], g)
                w = loaded("mod", g, c).rearrange("p (k n) -> p k n", k=K8)
                for k in range(K8):
                    for j in range(4):
                        mm = pe.matmul(ps[MOD_BANK[g]][32 * j:32 * j + 32, c * 64:c * 64 + 64], cT[:, k, :],
                                       w[:, k, j * 64:j * 64 + 64], start=(k == 0), stop=(k == K8 - 1),
                                       tile_position=(0, 32 * j), skip_group_check=True)
                mm.then_inc(s["chunk_done"], 1)

        def fill(l, c):
            if l == 0:
                mod_sums(FILL[c])

        def late(l, step):
            n = len(MOD_LATE)
            if l == 0:
                mod_sums(MOD_LATE[step * n // LATE_STEPS:(step + 1) * n // LATE_STEPS])

        pe.wait_ge(s["mlp_in"], 32)
        filter_hidden(0, 0)
        pe.wait_ge(s["cT"], 2)
        mod_sums(MOD_START[:3])
        filter_hidden(0, 1)
        mod_sums(MOD_START[3:6])
        filter_hidden(1, 0)
        mod_sums(MOD_START[6:8])
        filter_hidden(1, 1)
        filter_taps(0)
        pe.wait_ge(s["sin_in"], at("sin_in", 1))
        mod_sums(MOD_START[8:10])
        filter_spectra(0)
        mod_sums(MOD_START[10:])
        pe.wait_ge(s["x_in"], 16 * (TT + 2))

        for l in range(DEPTH):
            if l > 0:
                filter_taps(l)

            pe.wait_ge(s["h"], at("h", l))
            if l == 0:
                pe.wait_ge(s["mod_sum"], 1)
                pe.wait_ge(s["spec"], at("spec", l))
            banks = HT_BANKS[l]
            for k in range(K8):
                if banks[k] in banks[:k]:
                    earlier = max(i for i in range(k) if banks[i] == banks[k])
                    pe.wait_ge(s["hT"], at("hT", l, earlier + 1))
                if l > 0 and k == 4:
                    pe.wait_ge(s["filt_eo"], at("filt_eo", l, 1))
                for t in range(TT):
                    mm = pe.transpose(ps[banks[k]][:, t * P:(t + 1) * P], h[:, t, k:D:K8], ident)
                mm.then_inc(s["hT_raw"], 1)
            pe.wait_ge(s["hT"], at("hT", l))
            if l > 0:
                pe.wait_ge(s["filt_eo"], at("filt_eo", l, 2))

            for c in range(2):
                w = loaded("in", l, c).rearrange("p (k n) -> p k n", k=K8)
                for t in range(TT):
                    for k in range(K8):
                        mm = pe.matmul(ps[t][:, c * 256:(c + 1) * 256], act_t[:, k, t * P:(t + 1) * P], w[:, k, :],
                                       start=(k == 0), stop=(k == K8 - 1))
                mm.then_inc(s["chunk_done"], 1)
                fill(l, c)
            if l > 0:
                filter_spectra(l)
            for c in range(6):
                w = loaded("in", l, 2 + c // 2).rearrange("p (k n) -> p k n", k=K8)
                if l > 0 and 1 <= c <= 3:
                    pe.wait_ge(s["spec"], at("spec", l, (0, 2, 2, 3)[c]))
                if c == 4:
                    pe.wait_ge(s["hy"], at("hy", l, 1))
                for k in range(K8):
                    mm = pe.matmul(ps[3 + c % 4][:, 0:TOK], w[:, k, c % 2 * P:c % 2 * P + P], act_t[:, k, :],
                                   start=(k == 0), stop=(k == K8 - 1))
                if c % 2 == 1:
                    mm.then_inc(s["chunk_done"], 1)
                    fill(l, 2 + c // 2)
            pe.wait_ge(s["uv"], at("uv", l))
            for c, (c0, n) in enumerate(IN_CHUNKS[5:]):
                w = loaded("in", l, 5 + c)[:, 0:n * K8].rearrange("p (k n) -> p k n", k=K8)
                for t in range(TT):
                    for k in range(K8):
                        mm = pe.matmul(ps[t][:, c0 - 1280:c0 - 1280 + n], act_t[:, k, t * P:(t + 1) * P],
                                       w[:, k, :], start=(k == 0), stop=(k == K8 - 1))
                mm.then_inc(s["chunk_done"], 1)
                fill(l, 5 + c)

            pe.wait_ge(s["vh"], at("vh", l))
            pe.wait_ge(s["mla"], at("mla", l))
            for hh in range(4):
                mm = pe.matmul(ps[1 + hh // 2][:, hh % 2 * 192:hh % 2 * 192 + 192].rearrange("p (t n) -> p t n", t=TT), wsT[:, hh, :],
                               vh[:, :, hh * GW:(hh + 1) * GW], start=True, stop=True)
                if hh % 2 == 1:
                    mm.then_inc(s["s_raw"], 1)
            pe.wait_ge(s["a"], at("a", l))
            pe.wait_ge(s["hy"], at("hy", l))
            for c in range(2):
                for t in range(TT):
                    mm = pe.transpose(ps[3 + c][:, t * P:(t + 1) * P], uv[:, t, c * P:(c + 1) * P], ident)
                mm.then_inc(s["aT_raw"], 1)

            pe.wait_ge(s["mla_n"], at("mla_n", l))
            pe.wait_ge(s["cache_in"], 64 * (l + 1))
            for c in range(2):
                for t in range(TT):
                    mm = pe.transpose(ps[(6, 2)[c]][:, t * P:(t + 1) * P], mla[:, t, c * P:(c + 1) * P], ident)
                mm.then_inc(s["latT_raw"], 1)
            for t in range(4):
                mm = pe.transpose(ps[0][:, t * P:(t + 1) * P], mla[:, t, 256:384] if t < TT else cckv, ident)
            mm.then_inc(s["latT_raw"], 1)
            for t in range(4):
                mm = pe.transpose(ps[5][0:QK, t * P:(t + 1) * P], kpeb[:, t, :], ident)
            mm.then_inc(s["latT_raw"], 1)

            late(l, 0)
            pe.wait_ge(s["zc"], at("zc", l))
            pe.wait_ge(s["aT"], at("aT", l))
            pe.wait_ge(s["latT"], at("latT", l))
            for o in range(2):
                if o == 1:
                    pe.wait_ge(s["yc"], at("yc", l, 2))
                for t in range(TT):
                    for c in range(2):
                        mm = pe.transpose(ps[t // 2][:, t % 2 * 256 + c * P:t % 2 * 256 + c * P + P],
                                          zc[:, 4 + c, t * P:(t + 1) * P], ident)
                    if t > 0:
                        mm.then_inc(s["ut_raw"], 1)
                late(l, 1 + 2 * o)
                pe.wait_ge(s["ut"], at("ut", l, 2 * o + 2))
                for b in range(3):
                    tiles = (0,) if b == 0 else (1, 2)
                    for part, (m_ctx, m_lat) in enumerate(((G_C, F_C), (G_S, F_S))):
                        for i, t in enumerate(tiles):
                            q = m_ctx if b == 0 else m_lat + i * 256 + (b - 1) * P
                            mm = pe.matmul(ps[2 + b][:, part * 256:part * 256 + 256], dft[:, q:q + P], utok[:, t, :],
                                           start=(i == 0), stop=(i == len(tiles) - 1))
                    mm.then_inc(s["uf_raw"], 1)
                late(l, 2 + 2 * o)
                for c in range(2):
                    pe.wait_ge(s["yf"], at("yf", l, 3 * o + 3))
                    for b in range(3):
                        for part, (m_ctx, m_lat) in enumerate(((G_CT, F_CT), (G_ST, F_ST))):
                            cols = slice(0, P) if b == 0 else slice(P, TOK)
                            q = slice(m_ctx, m_ctx + P) if b == 0 else slice(m_lat + (b - 1) * 256, m_lat + b * 256)
                            mm = pe.matmul(ps[5 + c][:, cols], yfre[:, b, part, c * P:(c + 1) * P], dft[:, q],
                                           start=(b < 2 and part == 0), stop=(b in (0, 2) and part == 1))
                    mm.then_inc(s["yc_raw"], 1)

            pe.wait_ge(s["wuq_sw"], at("wuq_sw", l))
            pe.wait_ge(s["yc"], at("yc", l))
            for hh in range(HEADS):
                b = 2 * (hh % 2)
                if hh >= 2:
                    pe.wait_ge(s["q_pe"], at("q_pe", l, hh - 1))
                    pe.wait_ge(s["q_nope"], at("q_nope", l, hh - 1))
                for c in range(2):
                    pe.matmul(ps[b][0:QK, 0:TOK], wuq[:, c, hh * QK:(hh + 1) * QK], cqT[:, c, :],
                              start=(c == 0), stop=(c == 1))
                for c in range(2):
                    mm = pe.matmul(ps[b + 1][64:96, 0:LAT], wuq_sw[:, c, hh * ROPE:(hh + 1) * ROPE], cqT[:, c, P:TOK],
                                   start=(c == 0), stop=(c == 1))
                mm.then_inc(s["q_raw"], 1)
            pe.wait_ge(s["mod_sum"], MOD_GROUPS)
            for g in range(4):
                if g >= 2:
                    pe.wait_ge(s["kT"], at("kT", l, g - 1))
                for i in range(2):
                    hh = 2 * g + i
                    mm = pe.matmul(ps[4 + 2 * (g % 2) + i][0:64, :], wukv[:, hh * P:hh * P + 64], ckvT,
                                   start=True, stop=True)
                mm.then_inc(s["k_raw"], 1)
            pe.wait_ge(s["q_pe"], at("q_pe", l))
            pe.wait_ge(s["q_nope"], at("q_nope", l))
            wv = wukv[:].rearrange("p (h n) -> p h n", n=P)[:, :, 64:128]
            for t in range(4):
                pe.matmul(ps[t][:, :], ckvT[:, t * P:(t + 1) * P], wv, start=True, stop=True).then_inc(s["v_raw"], 1)

            pe.wait_ge(s["v"], at("v", l))
            pe.wait_ge(s["kT"], at("kT", l))

            def scores(hh):
                b = 2 * (hh % 2)
                if hh >= 2:
                    pe.wait_ge(s["pexp"], at("pexp", l, hh - 1))
                pe.matmul(ps[b][:, 0:384], qT[0:QK, hh, P:2 * P], kT[0:QK, hh, P:KEYS], start=True, stop=True)
                pe.matmul(ps[b][:, 384:512], qT[0:QK, hh, 0:P], kT[0:QK, hh, 0:P], start=True, stop=True)
                pe.matmul(ps[b + 1][:, 0:384], qT[0:QK, hh, 2 * P:3 * P], kT[0:QK, hh, P:KEYS],
                          start=True, stop=True).then_inc(s["sc_raw"], 1)

            scores(0)
            scores(1)
            for hh in range(HEADS):
                if hh + 2 < HEADS:
                    scores(hh + 2)
                pe.wait_ge(s["pn"], at("pn", l, hh + 1))
                if hh > 0:
                    pe.wait_ge(s["pT"], at("pT", l, 2 * hh - 1))
                for i, o in enumerate((0, 512, 384)):
                    mm = pe.transpose(ps[4][:, i * P:(i + 1) * P], probs[hh % 2][:, o:o + P], ident)
                mm.then_inc(s["pT_raw"], 1)
                if hh > 0:
                    pe.wait_ge(s["pT"], at("pT", l, 2 * hh))
                for i, o in enumerate((P, 512 + P, 2 * P, 512 + 2 * P)):
                    mm = pe.transpose(ps[5][:, i * P:(i + 1) * P], probs[hh % 2][:, o:o + P], ident)
                mm.then_inc(s["pT_raw"], 1)
                pe.wait_ge(s["pT"], at("pT", l, 2 * hh + 2))
                if hh % 2 == 0 and hh >= 4:
                    pe.wait_ge(s["oT"], at("oT", l, hh // 2 - 1))
                r = slice(64 * (hh % 2), 64 * (hh % 2) + 64)
                ob = ps[6 + hh // 2 % 2]
                pe.matmul(ob[r, 0:P], v_sb[:, 0, hh * GW:(hh + 1) * GW], probsT[:, 2, :], start=True, stop=True)
                for i in range(3):
                    rhs = probsT[:, (0, 3, 5)[i]:(0, 3, 5)[i] + 2, :].rearrange("p b n -> p (b n)")
                    mm = pe.matmul(ob[r, P:TOK], v_sb[:, 1 + i, hh * GW:(hh + 1) * GW], rhs,
                                   start=(i == 0), stop=(i == 2))
                mm.then_inc(s["pv"], 1)

            def h2_turned(t):
                pe.wait_ge(s["h2"], at("h2", l, t + 1))
                for half in range(2):
                    for k in range(4):
                        mm = pe.transpose(ps[2 * t + half][:, k * P:(k + 1) * P], h[:, t, 4 * half + k:D:K8], ident)
                    mm.then_inc(s["h2T_raw"], 1)

            def router(t):
                pe.wait_ge(s["h2T"], at("h2T", l, 2 * t + 2))
                for k in range(K8):
                    mm = pe.matmul(ps[6][:, t * 36:(t + 1) * 36], act_t[:, k, t * P:(t + 1) * P], wr[:, k, :],
                                   start=(k == 0), stop=(k == K8 - 1))
                return mm

            pe.wait_ge(s["oT"], at("oT", l))
            pe.wait_ge(s["pexp"], at("pexp", l))
            for t in range(TT):
                for c in range(OUT_CHUNKS):
                    w = loaded("out", l, c).rearrange("p (k n) -> p k n", k=2)
                    for half in range(2):
                        for k in range(2):
                            mm = pe.matmul(ps[2 * t + half][:, :], act_t[:, 2 * c + k, t * P:(t + 1) * P],
                                           w[:, k, half * 512:(half + 1) * 512],
                                           start=(c == 0 and k == 0), stop=(c == 3 and k == 1))
                    if t == TT - 1:
                        mm.then_inc(s["chunk_done"], 1)
                if t < TT - 1:
                    mm.then_inc(s["out_raw"], 1)
                if t > 0:
                    h2_turned(t - 1)
            router(0)
            router(1)
            h2_turned(2)
            router(2).then_inc(s["lg_raw"], 1)
            pe.wait_ge(s["oh"], at("oh", l))
            oh = rt[:, 0:12].rearrange("p (t g) -> p t g", t=TT)
            for t in range(TT):
                for i in range(t + 1):
                    pe.matmul(ps[7][:, t * 4:t * 4 + 4], tri if i == t else ones, oh[:, i, :],
                              start=(i == 0), stop=(i == t))
            for i in range(TT):
                mm = pe.matmul(ps[7][:, 12:16], ones, oh[:, i, :], start=(i == 0), stop=(i == 2))
            mm.then_inc(s["cum_raw"], 1)
            pe.wait_ge(s["tgt"], at("tgt", l))
            dw = rt[:, 12:36].rearrange("p (t n) -> p t n", t=TT)

            def gather_half(e, half, g, loop=0, b=3):
                pe.wait_ge(e["sel"], loop * 2 + (g + 1))
                if b == 3 and (half > 0 or g > 0):
                    pe.wait_ge(e["x_lo"], loop * 4 + (2 * g + half))
                for k in range(4 * half, 4 * half + 4):
                    for t in range(TT):
                        mm = pe.matmul(ps[b][:, k % 4 * P:k % 4 * P + P], h[:, t, k:D:K8], sel[:, t, :],
                                       start=(t == 0), stop=(t == TT - 1))
                mm.then_inc(e["x_raw"], 1)

            def gather_rest(e, scattered, loop=0):
                if scattered > 0:
                    pe.wait_ge(e_main["acc"], loop * 2 * TT + TT * scattered)
                for t in range(TT):
                    pe.matmul(ps[7][:, 384:392], sel[:, t, :], dw[:, t, :], start=(t == 0), stop=(t == TT - 1))
                for t in range(TT):
                    mm = pe.transpose(ps[7][:, t * P:(t + 1) * P], sel[:, t, :], ident)
                mm.then_inc(e["picked"], 1)

            def run(experts, slot0, e, chunk0, v0, loop, tokens_in, g0=None):
                q0 = v0 * EPG
                ex_by, v_by = loop * PAIR, loop * 2

                def weights(kind, ex):
                    i = pos(kind, ex, experts)
                    pe.wait_ge(e["lo"], loop * (3 * PAIR) + (RING + chunk0 + i + 1))
                    return [w[:, i % SPLIT, :].rearrange("p (k n) -> p k n", k=2 if kind == "D" else K8)
                            for w in (w_hi, w_lo)]

                def gate_up(ex, kind):
                    j = ex % 2
                    if kind == "G":
                        if q0 > 0 or ex >= 2:
                            pe.wait_ge(e["hid"], ex_by + (q0 + ex - 1))
                        if ex % EPG == 0:
                            sem_in, value, by = tokens_in(ex // EPG)
                            pe.wait_ge(sem_in, loop * by + value)
                    hi, lo = weights(kind, ex)
                    sl = (slot0 + ex // EPG) % 2
                    cols = slice(0, FF) if kind == "G" else slice(FF, 2 * FF)
                    for k in range(K8):
                        for i, (xs, ws) in enumerate(((x_hi, hi), (x_hi, lo), (x_lo, hi))):
                            mm = pe.matmul(ps[j][:, cols], xs[:, sl, k, :], ws[:, k, :],
                                           start=(k == 0 and i == 0), stop=(k == K8 - 1 and i == 2))
                    mm.then_inc(e["done"], 1)

                def turn(ex):
                    pe.wait_ge(e["hid"], ex_by + (q0 + ex + 1))
                    if q0 > 0 or ex >= 1:
                        pe.wait_ge(e["hd_lo"], ex_by + (q0 + ex))
                    for k in range(2):
                        mm = pe.transpose(ps[2][:, k * P:(k + 1) * P], hd[:, ex % 2, k:FF:2], ident)
                    mm.then_inc(e["hd_raw"], 1)

                def down(ex):
                    first, last = ex % EPG == 0, ex % EPG == EPG - 1
                    hi, lo = weights("D", ex)
                    pe.wait_ge(e["hd_lo"], ex_by + (q0 + ex + 1))
                    if first and v0 + ex > 0:
                        pe.wait_ge(e["y"], v_by * 2 + 2 * (v0 + ex // EPG))
                    for k in range(2):
                        for i, (hs, ws) in enumerate(((hd_hi, hi), (hd_hi, lo), (hd_lo, hi))):
                            for half in range(2):
                                mm = pe.matmul(ps[4 + half][:, :], hs[:, ex % 2, k * P:(k + 1) * P],
                                               ws[:, k, half * 512:(half + 1) * 512],
                                               start=(first and k == 0 and i == 0), stop=(last and k == 1 and i == 2),
                                               skip_group_check=True)
                    mm.then_inc(e["done"], 1)

                def scatter(visit, t, b=6):
                    pe.wait_ge(e["y"], v_by * 2 + 2 * (v0 + visit + 1))
                    behind = 0 if visit == 0 and experts == PAIR else 1
                    if TT * (v0 + visit) + t - behind > 0:
                        pe.wait_ge(e["acc"], v_by * TT + (TT * (v0 + visit) + t - behind))
                    for i, y in enumerate((y_hi, y_lo)):
                        for half in range(2):
                            mm = pe.matmul(ps[b + half][:, :], selT[:, (slot0 + visit) % 2, t, :],
                                           y[:, half * 512:(half + 1) * 512], start=(i == 0), stop=(i == 1),
                                           skip_group_check=True)
                    mm.then_inc(e["sct"], 1)

                gate_up(0, "G")
                gate_up(0, "U")
                for ex in range(1, experts):
                    gate_up(ex, "G")
                    turn(ex - 1)
                    gate_up(ex, "U")
                    if experts == PAIR:
                        if ex in GATHER:
                            nth, step = GATHER[ex]
                            if step < 2:
                                gather_half(e, step, g0 + 1 + nth, loop)
                            else:
                                gather_rest(e, v0 + nth, loop)
                        if ex in SCATTER:
                            if ex == min(SCATTER):
                                pe.wait_ge(e["rest"], loop * 2 + (g0 + 2))
                            scatter(0, SCATTER[ex])
                    down(ex - 1)
                turn(experts - 1)
                down(experts - 1)
                if experts == PAIR:
                    pe.wait_ge(e["rest"], loop * 2 + (g0 + 3))
                for t in range(TT):
                    scatter(experts // EPG - 1, t, LAST_BANKS[t])

            g0 = l * GATHERS
            for half in range(2):
                gather_half(e_main, half, g0, b=3 - half)
            gather_rest(e_main, l * GROUPS)
            with pe.Fori(0, GROUPS // 2) as it:
                run(PAIR, 0, e_main, l * MOE_CHUNKS, l * GROUPS, it,
                    lambda visit: (e_main["x_lo"], 2 * (g0 + visit + 1), 4), g0)
            pe.wait_ge(s["regs"], at("regs", l))
            extra = pe.value_load(xi[0:1, 0:1], min_val=0, max_val=EXTRA)
            xe = e_extra[l]
            with pe.If(extra >= 1):
                pe.wait_ge(e_main["acc"], TT * GROUPS * (l + 1))
                run(EPG, 0, xe, 0, 0, 0, lambda visit: (e_main["x_lo"], 2 * (g0 + GATHERS), 0))
                with pe.If(extra >= 2):
                    pe.wait_ge(xe["acc"], TT)
                    for half in range(2):
                        gather_half(xe, half, 0)
                    gather_rest(xe, 0)
                    pe.wait_ge(xe["rest"], 1)
                    run(EPG, 1, xe, EPG * 3, 1, 0, lambda visit: (xe["x_lo"], 2, 0))

    @block.scalar
    def _(act):
        act.dma_start(x[:, 0, :], a["x_prompt"][0]).then_inc(s["x_in"], 16)
        for t in range(2):
            act.dma_start(x[:, 1 + t, :], a["x_sample"][0, t * P:(t + 1) * P]).then_inc(s["x_in"], 16)
        act.dma_start(cst[:], a["consts"]).then_inc(s["x_in"], 16)
        act.dma_start(ropeT[64:96], a["rope_t"]).then_inc(s["x_in"], 16)
        act.wait_ge(s["mod_zero"], 1)
        for l in range(DEPTH):
            bview = a["b_mod"][l].rearrange("(b j n) -> j b n", j=4, n=64)
            for c in range(2):
                act.dma_start(mod_sums[c:P:32, l * 1536:(l + 1) * 1536].rearrange("p (b n) -> p b n", n=64),
                              bview).then_inc(s["bmod_in"], 16)
        act.wait_ge(s["cond_in"], 32)
        act.wait_ge(s["cT"], 1)
        act.activation(cT[:, :, 0:2], craw.rearrange("p c k -> p k c"), ACT.Silu).then_inc(s["cT"], 1)

        def filter_hidden(l, i):
            act.wait_ge(s["sin_in"], at("sin_in", l, i + 1))
            act.activation(hid1 if i == 0 else hid2[l], f_arg, ACT.Sin).then_inc(s["hid"], 1)

        def norm(base, t):
            act.wait_ge(s["ln_var"], base + t + 1)
            act.activation(st[:, 64 + t:65 + t], st[:, 60 + t:61 + t], ACT.Sqrt).then_inc(s["ln_std"], 1)
            act.wait_ge(s["ln_scale"], base + t + 1)
            act.activation(x[:, t, :], x[:, t, :], ACT.Identity, scale=st[:, 124 + t:125 + t],
                           bias=st[:, 76 + t:77 + t]).then_inc(s["normed"], 1)

        def spectra(l):
            for b in range(3):
                act.wait_ge(s["spec_raw"], at("spec_raw", l, b + 1))
                act.activation(spec[:, b, 0, :], ps[SPEC_BANKS[l][b][0]][:, :], ACT.Copy)
                act.activation(spec[:, b, 1, :], ps[SPEC_BANKS[l][b][1]][:, :], ACT.Copy).then_inc(s["spec"], 1)

        filter_hidden(0, 0)
        norm(0, 0)
        filter_hidden(0, 1)
        norm(0, 1)
        filter_hidden(1, 0)
        store_group(act, 0, "mod0_out")
        filter_hidden(1, 1)
        norm(0, 2)
        spectra(0)
        for l in range(DEPTH):
            for k in range(K8):
                act.wait_ge(s["hT_raw"], at("hT_raw", l, k + 1))
                act.activation(act_t[:, k, :], ps[HT_BANKS[l][k]][:, 0:TOK], ACT.Copy).then_inc(s["hT"], 1)
            act.wait_ge(s["chunk_done"], last_chunk("in", l, 1))
            for t in range(TT):
                act.activation(uv[:, t, :], ps[t][:, :], ACT.Gelu_apprx_tanh).then_inc(s["uv"], 1)
            if l > 0:
                spectra(l)
            for c in range(6):
                act.wait_ge(s["chunk_done"], last_chunk("in", l, 2 + c // 2))
                bank = ps[3 + c % 4]
                act.activation(hy[:, c, 1:1 + P], bank[:, 0:P], ACT.Copy)
                mm = act.activation(hy[:, c, 2 + P:2 + TOK], bank[:, P:TOK], ACT.Copy)
                if c % 2 == 1:
                    mm.then_inc(s["hy"], 1)
            act.wait_ge(s["gm_var"], at("gm_var", l))
            act.activation(st[:, 12:24], st[:, 0:12], ACT.Sqrt).then_inc(s["gm_std"], 1)
            act.wait_ge(s["chunk_done"], last_chunk("in", l, 7))
            for t in range(TT):
                act.activation(mla[:, t, :], ps[t][:, 0:MLA_COLS], ACT.Copy).then_inc(s["mla"], 1)
            act.wait_ge(s["mla"], at("mla", l))
            for t in range(TT):
                act.activation(region_k[:, t * 384:t * 384 + 256], mla[:, t, 0:256], ACT.Square, accum_out=st[:, 48 + t:49 + t])
            for t in range(TT):
                mm = act.activation(region_k[:, t * 384 + 256:t * 384 + 384], mla[:, t, 256:384], ACT.Square, accum_out=st[:, 51 + t:52 + t])
            mm.then_inc(s["rms_ss"], 1)
            act.wait_ge(s["rms_var"], at("rms_var", l))
            act.activation(st[:, 54:60], st[:, 48:54], ACT.Sqrt).then_inc(s["rms_std"], 1)
            for c in range(2):
                act.wait_ge(s["aT_raw"], at("aT_raw", l, c + 1))
                act.activation(act_t[:, c, :], ps[3 + c][:, 0:TOK], ACT.Copy).then_inc(s["aT"], 1)
            for c in range(2):
                act.wait_ge(s["latT_raw"], at("latT_raw", l, c + 1))
                act.activation(cqT[:, c, :], ps[(6, 2)[c]][:, 0:TOK], ACT.Copy).then_inc(s["latT"], 1)
            act.wait_ge(s["latT_raw"], at("latT_raw", l, 3))
            act.activation(ckvT, ps[0][:, :], ACT.Copy).then_inc(s["latT"], 1)
            act.wait_ge(s["latT_raw"], at("latT_raw", l, 4))
            for hh in range(HEADS):
                mm = act.activation(kT[64:96, hh, :], ps[5][64:96, :], ACT.Copy)
            mm.then_inc(s["latT"], 1)
            for o in range(2):
                act.wait_ge(s["ut_raw"], at("ut_raw", l, 2 * o + 1))
                act.activation(utok[:, 0:2, :].rearrange("p t n -> p (t n)"), ps[0][:, :], ACT.Copy).then_inc(s["ut"], 1)
                act.wait_ge(s["ut_raw"], at("ut_raw", l, 2 * o + 2))
                act.activation(utok[:, 2, :], ps[1][:, 0:256], ACT.Copy).then_inc(s["ut"], 1)
            for hh in range(HEADS):
                b = 2 * (hh % 2)
                act.wait_ge(s["q_raw"], at("q_raw", l, hh + 1))
                act.activation(qT[0:QK, hh, 0:P], ps[b][0:QK, 0:P], ACT.Copy)
                act.activation(qT[0:64, hh, P:TOK], ps[b][0:64, P:TOK], ACT.Copy).then_inc(s["q_nope"], 1)
            for g in range(4):
                act.wait_ge(s["k_raw"], at("k_raw", l, g + 1))
                act.activation(kT[0:64, 2 * g, :], ps[4 + 2 * (g % 2)][0:64, :], ACT.Copy)
                act.activation(kT[0:64, 2 * g + 1, :], ps[5 + 2 * (g % 2)][0:64, :], ACT.Copy).then_inc(s["kT"], 1)
            for t in range(4):
                act.wait_ge(s["v_raw"], at("v_raw", l, t + 1))
                act.activation(v_sb[:, t, :], ps[t][:, :], ACT.Copy).then_inc(s["v"], 1)
            def exponentials(hh):
                b, pr, c = 2 * (hh % 2), probs[hh % 2], SOFT_COLS[hh % 2]
                act.wait_ge(s["mx"], at("mx", l, hh + 1))
                if hh >= 2:
                    act.wait_ge(s["pT_raw"], at("pT_raw", l, 2 * hh - 2))
                for i, (src, dst) in enumerate(((ps[b][:, 0:384], pr[:, 0:384]),
                                                (ps[b][:, 384:512], pr[:, 384:512]),
                                                (ps[b + 1][:, 0:384], pr[:, 512:896]))):
                    mm = act.activation(dst, src, ACT.Exp, bias=st[:, c + i:c + i + 1], scale=QK_SCALE,
                                        accum_out=st[:, c + 3 + i:c + 4 + i])
                mm.then_inc(s["pexp"], 1)

            exponentials(0)
            for hh in range(HEADS):
                if hh + 1 < HEADS:
                    exponentials(hh + 1)
                act.wait_ge(s["pT_raw"], at("pT_raw", l, 2 * hh + 1))
                if hh > 0:
                    act.wait_ge(s["pv"], at("pv", l, hh))
                act.activation(probsT[:, 0:3, :], ps[4][:, 0:384].rearrange("p (b n) -> p b n", b=3), ACT.Copy)\
                    .then_inc(s["pT"], 1)
                act.wait_ge(s["pT_raw"], at("pT_raw", l, 2 * hh + 2))
                act.activation(probsT[:, 3:7, :], ps[5][:, :].rearrange("p (b n) -> p b n", b=4), ACT.Copy)\
                    .then_inc(s["pT"], 1)
                if hh % 2 == 1:
                    act.wait_ge(s["pv"], at("pv", l, hh + 1))
                    act.activation(act_t[:, 4 + hh // 2, :], ps[6 + hh // 2 % 2][:, 0:TOK], ACT.Copy)\
                        .then_inc(s["oT"], 1)
            def h2_turned(t):
                for half in range(2):
                    act.wait_ge(s["h2T_raw"], at("h2T_raw", l, 2 * t + half + 1))
                    act.activation(act_t[:, 4 * half:4 * half + 4, t * P:(t + 1) * P],
                                   ps[2 * t + half][:, :].rearrange("p (k n) -> p k n", k=4), ACT.Copy)\
                        .then_inc(s["h2T"], 1)

            norm(norms(l, 1, 0), 0)
            norm(norms(l, 1, 0), 1)
            h2_turned(0)
            norm(norms(l, 1, 0), 2)
            h2_turned(1)
            h2_turned(2)
            act.wait_ge(s["lg_sh"], at("lg_sh", l))
            act.activation(rt[:, 300:315], rt[:, 280:295], ACT.Exp).then_inc(s["lg_exp"], 1)

            def gathered(e, half, slot, g, loop=0, b=3):
                act.wait_ge(e["x_raw"], loop * 4 + (2 * g + half + 1))
                act.activation(x_hi[:, slot, 4 * half:4 * half + 4, :],
                               ps[b][:, :].rearrange("p (k n) -> p k n", k=4), ACT.Copy).then_inc(e["x_hi"], 1)

            def picked(e, slot, g, loop=0):
                act.wait_ge(e["picked"], loop * 2 + (g + 1))
                act.activation(selT[:, slot, :, :], ps[7][:, 0:384].rearrange("p (t n) -> p t n", t=TT), ACT.Copy)
                act.activation(wslot[:, slot, :], ps[7][:, 384:392], ACT.Copy).then_inc(e["rest"], 1)

            def run(experts, e, full, full0, chunk0, v0, loop, g0=None):
                q0 = v0 * EPG
                ex_by, v_by, c_by = loop * PAIR, loop * 2, loop * (3 * PAIR)

                def high(c):
                    act.wait_ge(full[c % RING], loop * (16 * 3 * PAIR // RING) + 16 * (full0 + c // RING + 1))
                    act.wait_ge(e["done"], c_by + (chunk0 + c + 1))
                    act.activation(w_hi[:, c % SPLIT, :], ring[:, c % RING, :], ACT.Copy).then_inc(e["hi"], 1)

                for c in range(SPLIT):
                    high(c)
                for c, (kind, ex) in enumerate(order(experts)):
                    if kind == "G" and ex > 0 or (kind, ex) == ("D", experts - 1):
                        turned = ex - 1 if kind == "G" else ex
                        act.wait_ge(e["hd_raw"], ex_by + (q0 + turned + 1))
                        act.activation(hd_hi[:, turned % 2, :], ps[2][:, 0:FF], ACT.Copy).then_inc(e["hd_hi"], 1)
                    if kind == "U":
                        act.wait_ge(e["done"], c_by + (SPLIT + chunk0 + c + 1))
                        if q0 > 0 or ex >= 2:
                            act.wait_ge(e["hid"], ex_by + (q0 + ex - 1))
                        act.activation(sg[:, ex % 2, :], ps[ex % 2][:, 0:FF], ACT.Silu).then_inc(e["silu"], 1)
                        if experts == PAIR and ex in GATHER:
                            nth, step = GATHER[ex]
                            if step < 2:
                                gathered(e, step, 1 - nth, g0 + 1 + nth, loop)
                            else:
                                picked(e, 1 - nth, g0 + 1 + nth, loop)
                    if kind == "D" and ex % EPG == EPG - 1:
                        act.wait_ge(e["done"], c_by + (SPLIT + chunk0 + c + 1))
                        if v0 + ex // EPG > 0:
                            act.wait_ge(e["sct"], v_by * TT + TT * (v0 + ex // EPG))
                        act.activation(y_hi[:, 0:512], ps[4][:, :], ACT.Copy)
                        act.activation(y_hi[:, 512:1024], ps[5][:, :], ACT.Copy).then_inc(e["y"], 1)
                    if c + SPLIT < 3 * experts:
                        high(c + SPLIT)

            g0 = l * GATHERS
            for half in range(2):
                gathered(e_main, half, 0, g0, b=3 - half)
            picked(e_main, 0, g0)
            act.wait_ge(s["mod0_out"], 16 * MOD_OUTS)
            act.wait_ge(s["mod_out"], 16 * MOD_OUTS * (MOD_GROUPS - 1))
            with act.Fori(0, GROUPS // 2) as it:
                run(PAIR, e_main, moe_full, l * MOE_CHUNKS // RING, l * MOE_CHUNKS, l * GROUPS, it, g0)
            act.wait_ge(s["regs"], at("regs", l))
            extra = act.value_load(xi[0:1, 0:1], min_val=0, max_val=EXTRA)
            xe = e_extra[l]
            with act.If(extra >= 1):
                act.wait_ge(e_main["done"], SPLIT + (l + 1) * MOE_CHUNKS)
                act.wait_ge(e_main["sct"], TT * GROUPS * (l + 1))
                run(EPG, xe, x_full[l], 0, 0, 0, 0)
                with act.If(extra >= 2):
                    for half in range(2):
                        gathered(xe, half, 1, 0)
                    picked(xe, 1, 0)
                    run(EPG, xe, x_full[l], EPG * 3 // RING, EPG * 3, 1, 0)
            for t in range(TT):
                norm(norms(l, 2, 0), t)

    @block.vector
    def _(dve):
        steps = [0]

        def link(ins):
            steps[0] += 1
            ins.then_inc(s["dve_step"], 1)
            dve.wait_ge(s["dve_step"], steps[0])

        def norm_stats(t):
            xt, lnst = x[:, t, :], st[:, 80 + 14 * t:94 + 14 * t]
            dve.bn_stats(lnst[:, 0:6], xt[:, 0:512])
            link(dve.bn_stats(lnst[:, 6:12], xt[:, 512:1024]))
            link(dve.bn_aggr(lnst[:, 12:14], lnst[:, 0:12]))
            dve.tensor_scalar(st[:, 60 + t:61 + t], lnst[:, 13:14], LN_EPS, None, ALU.add).then_inc(s["ln_var"], 1)

        def norm_scale(base, t):
            dve.wait_ge(s["ln_std"], base + t + 1)
            rstd = st[:, 124 + t:125 + t]
            link(dve.reciprocal(rstd, st[:, 64 + t:65 + t]))
            dve.tensor_scalar(st[:, 76 + t:77 + t], st[:, 92 + 14 * t:93 + 14 * t], -1.0, rstd, ALU.mult, ALU.mult)\
                .then_inc(s["ln_scale"], 1)

        def affine(base, t, done):
            dve.wait_ge(s["normed"], base + t + 1)
            link(dve.tensor_tensor(x[:, t, :], x[:, t, :], lnr[:, 0, :], ALU.mult))
            dve.tensor_tensor(x[:, t, :], x[:, t, :], lnr[:, 1, :], ALU.add).then_inc(s[done], 1)

        def modulated(half, t, done, base=None):
            three, shift_lat = rows_by_half[half], (next_lat_shift, lat_shift)[half]
            scale, shift = (three[:, 1, :], three[:, 0, :]) if t == 0 else (three[:, 2, :], shift_lat)
            if base is None:
                link(dve.scalar_tensor_tensor(h[:, t, :], scale, 1.0, x[:, t, :], ALU.add, ALU.mult))
            else:
                dve.wait_ge(s["normed"], base + t + 1)
                link(dve.tensor_tensor(h[:, t, :], scale, x[:, t, :], ALU.mult))
            dve.tensor_tensor(h[:, t, :], h[:, t, :], shift, ALU.add).then_inc(s[done], 1)

        dve.memset(cT, 0.0).then_inc(s["cT"], 1)
        dve.memset(mod_sums, 0.0).then_inc(s["mod_zero"], 1)
        link(dve.memset(xi[:], 0))
        for e in [e_main] + e_extra:
            dve.memset(st[:, 79:80], 0.0).then_inc(e["lo"], RING)
            link(dve.memset(st[:, 122:123], 0.0))
            dve.memset(st[:, 122:123], 0.0).then_inc(e["done"], SPLIT)
            link(dve.memset(st[:, 79:80], 0.0))

        def filter_hidden(l, i):
            if i == 0:
                dve.wait_ge(s["filt_in"], at("filt_in", l))
                if l > 0:
                    dve.wait_ge(s["hid"], at("hid", l - 1))
            else:
                dve.wait_ge(s["hid_in"], at("hid_in", l))
            link(dve.tensor_scalar(f_arg, ps[7][0:FH, 0:TOK], fw[:, l, 128 + i:129 + i], fw[:, l, 130 + i:131 + i],
                                   ALU.add, ALU.mult))
            link(dve.tensor_scalar(f_n, f_arg, 0.5 / math.pi, MAGIC, ALU.mult, ALU.add))
            link(dve.tensor_scalar(f_n, f_n, MAGIC, None, ALU.subtract))
            link(dve.scalar_tensor_tensor(f_arg, f_n, -TWO_PI_HI, f_arg, ALU.mult, ALU.add))
            link(dve.scalar_tensor_tensor(f_arg, f_n, -TWO_PI_LO, f_arg, ALU.mult, ALU.add))
            dve.tensor_scalar(f_arg, f_arg, PI_SAFE, -PI_SAFE, ALU.min, ALU.max).then_inc(s["sin_in"], 1)

        def filter_taps(l):
            dve.wait_ge(s["taps_in"], 48 * (l + 1))
            for t in range(TT):
                for o in range(2):
                    dve.wait_ge(s["filt_raw"], at("filt_raw", l, 2 * t + o + 1))
                    raw = ps[2 * t + o]
                    dve.tensor_tensor(f_tmp[:, 0:CH], raw[:, 0:CH], decay[:, t, :], ALU.mult)
                    link(dve.scalar_tensor_tensor(f_tmp[:, CH:2 * CH], raw[:, CH:2 * CH], cst[:, C_MASK + t:C_MASK + t + 1],
                                                  decay[:, t, :], ALU.mult, ALU.mult))
                    dve.tensor_tensor(f_sum[:, t, o * CH:(o + 1) * CH], f_tmp[:, 0:CH], f_tmp[:, CH:2 * CH], ALU.add)
                    last = dve.tensor_tensor(f_dif[:, t, o * CH:(o + 1) * CH], f_tmp[:, 0:CH], f_tmp[:, CH:2 * CH],
                                             ALU.subtract)
                    if o == 0:
                        link(last)
                    else:
                        last.then_inc(s["filt_eo"], 1)
                        dve.wait_ge(s["filt_eo"], at("filt_eo", l, t + 1))

        def swap_queries(l):
            dve.wait_ge(s["cache_in"], 64 * (l + 1))
            for c in range(2):
                pe_cols = wuq[:, c, :].rearrange("p (h n) -> p h n", n=QK)
                sw = wuq_sw[:, c, :].rearrange("p (h n) -> p h n", n=ROPE)
                dve.tensor_copy(sw[:, :, 0:ROPE:2], pe_cols[:, :, 65:QK:2])
                last = dve.tensor_copy(sw[:, :, 1:ROPE:2], pe_cols[:, :, 64:QK:2])
            last.then_inc(s["wuq_sw"], 1)

        dve.wait_ge(s["mlp_in"], 32)
        filter_hidden(0, 0)
        dve.wait_ge(s["x_in"], 16 * (TT + 2))
        dve.wait_ge(s["ln_in"], 32)

        def add_group(g):
            dve.wait_ge(s["chunk_done"], last_chunk("mod", g, MOD_GROUP - 1))
            sums = mod_sums[:, g * 512:(g + 1) * 512]
            dve.tensor_tensor(sums, sums, ps[MOD_BANK[g]][:, :], ALU.add).then_inc(s["mod_sum"], 1)

        def input_norm(t):
            norm_stats(t)
            norm_scale(0, t)
            affine(0, t, "x0")

        input_norm(0)
        filter_hidden(0, 1)
        input_norm(1)
        filter_hidden(1, 0)
        dve.wait_ge(s["bmod_in"], 16 * 2 * DEPTH)
        dve.wait_ge(s["mod_zero"], 1)
        add_group(0)
        filter_hidden(1, 1)
        input_norm(2)
        filter_taps(0)

        for l in range(DEPTH):
            if l == 0:
                dve.wait_ge(s["x0"], TT)
                dve.wait_ge(s["mod12_in"], 64)
                for t in range(TT):
                    modulated(0, t, "h")
            dve.wait_ge(s["h"], at("h", l))
            if l > 0:
                filter_taps(l)
            dve.wait_ge(s["small_in"], 16 * SMALL_LOADS * (l + 1))
            for col in (0, 1 + P, 2 + TOK):
                link(dve.memset(hy[:, :, col:col + 1], 0.0))
            link(dve.memset(kpeb[:, :, 0:64], 0.0))
            if l == 0:
                add_group(1)
                add_group(2)

            v4 = uv[:, :, CH:2 * CH].rearrange("p t (h d) -> p t h d", h=4)
            vh4 = vh.rearrange("p t (h d) -> p t h d", h=4)
            sq4 = utok.rearrange("p t (h d) -> p t h d", h=4)

            def per_head(c):
                return st[:, c:c + 12].rearrange("p (t h) -> p t h", t=TT)

            dve.wait_ge(s["uv"], at("uv", l))
            link(dve.tensor_reduce(per_head(0), v4, AX.X, ALU.add))
            link(dve.tensor_scalar(st[:, 0:12], st[:, 0:12], 1.0 / GW, None, ALU.mult))
            link(dve.tensor_tensor(vh4, v4, per_head(0).unsqueeze(3).to_broadcast([P, TT, 4, GW]), ALU.subtract))
            link(dve.tensor_tensor(sq4, vh4, vh4, ALU.mult))
            link(dve.tensor_reduce(per_head(0), sq4, AX.X, ALU.add))
            dve.tensor_scalar(st[:, 0:12], st[:, 0:12], 1.0 / GW, LN_EPS, ALU.mult, ALU.add).then_inc(s["gm_var"], 1)

            dve.wait_ge(s["gm_std"], at("gm_std", l))
            link(dve.reciprocal(st[:, 24:36], st[:, 12:24]))
            link(dve.tensor_tensor(vh4, vh4, per_head(24).unsqueeze(3).to_broadcast([P, TT, 4, GW]), ALU.mult))
            link(dve.tensor_tensor(vh, vh, rows[:, 0:256].unsqueeze(1).to_broadcast([P, TT, 256]), ALU.mult))
            dve.tensor_tensor(vh, vh, rows[:, 256:512].unsqueeze(1).to_broadcast([P, TT, 256]), ALU.add)\
                .then_inc(s["vh"], 1)

            dve.wait_ge(s["hT_raw"], at("hT_raw", l))
            for c in range(6):
                dve.wait_ge(s["hy"], at("hy", l, c // 2 + 1))
                for o, i, n in ((0, 0, P), (P, P + 1, LAT)):
                    link(dve.tensor_scalar(zc[:, c, o:o + n], hy[:, c, i + 1:i + 1 + n], cw[:, 1, c:c + 1],
                                           cw[:, 3, c:c + 1], ALU.mult, ALU.add))
                    link(dve.scalar_tensor_tensor(zc[:, c, o:o + n], hy[:, c, i:i + n], cw[:, 0, c:c + 1],
                                                  zc[:, c, o:o + n], ALU.mult, ALU.add))
                    last = dve.scalar_tensor_tensor(zc[:, c, o:o + n], hy[:, c, i + 2:i + 2 + n], cw[:, 2, c:c + 1],
                                                    zc[:, c, o:o + n], ALU.mult, ALU.add)
                last.then_inc(s["zc"], 1)
                if l == 0 and c == 3:
                    add_group(3)
            dve.wait_ge(s["rms_ss"], at("rms_ss", l))
            dve.tensor_scalar(st[:, 48:51], st[:, 48:51], 1.0 / 256, RMS_EPS, ALU.mult, ALU.add)
            dve.tensor_scalar(st[:, 51:54], st[:, 51:54], 1.0 / 128, RMS_EPS, ALU.mult, ALU.add).then_inc(s["rms_var"], 1)

            dve.wait_ge(s["rms_std"], at("rms_std", l))
            dve.wait_ge(s["mla"], at("mla", l))
            link(dve.reciprocal(st[:, 70:76], st[:, 54:60]))
            for t in range(TT):
                cq, ckv = mla[:, t, 0:256], mla[:, t, 256:384]
                dve.scalar_tensor_tensor(cq, cq, st[:, 70 + t:71 + t], rows[:, 512:768], ALU.mult, ALU.mult)
                dve.scalar_tensor_tensor(ckv, ckv, st[:, 73 + t:74 + t], rows[:, 768:896], ALU.mult, ALU.mult)
            pe2 = mla[:, 1:3, 384:416]
            cos = cst[:, C_COS:C_COS + 64].rearrange("p (t n) -> p t n", t=2)
            sin = cst[:, C_SIN:C_SIN + 64].rearrange("p (t n) -> p t n", t=2)
            turn = rt[:, 200:264].rearrange("p (t n) -> p t n", t=2)
            dve.tensor_copy(kpeb[:, 0, 64:96], mla[:, 0, 384:416])
            dve.tensor_tensor(kpeb[:, 1:3, 64:96], pe2, cos, ALU.mult)
            dve.tensor_tensor(turn[:, :, 0:ROPE:2], pe2[:, :, 1:ROPE:2], sin[:, :, 0:ROPE:2], ALU.mult)
            link(dve.tensor_tensor(turn[:, :, 1:ROPE:2], pe2[:, :, 0:ROPE:2], sin[:, :, 1:ROPE:2], ALU.mult))
            dve.tensor_tensor(kpeb[:, 1:3, 64:96], kpeb[:, 1:3, 64:96], turn, ALU.add).then_inc(s["mla_n"], 1)

            for hh in range(4):
                if hh % 2 == 0:
                    dve.wait_ge(s["s_raw"], at("s_raw", l, hh // 2 + 1))
                mixed = ps[1 + hh // 2][:, hh % 2 * 192:hh % 2 * 192 + 192].rearrange("p (t n) -> p t n", t=TT)
                u = uv[:, :, hh * GW:(hh + 1) * GW]
                last = dve.scalar_tensor_tensor(u, mixed, bs_c[:, hh:hh + 1], u, ALU.add, ALU.mult)
            last.then_inc(s["a"], 1)

            dve.wait_ge(s["zc"], at("zc", l))
            if l == 0:
                add_group(4)
            swap_queries(l)
            for o in range(2):
                for b in range(3):
                    dve.wait_ge(s["uf_raw"], at("uf_raw", l, 3 * o + b + 1))
                    uc, us = ps[2 + b][:, 0:CH], ps[2 + b][:, CH:2 * CH]
                    hc, hs = spec[:, b, 0, o * CH:(o + 1) * CH], spec[:, b, 1, o * CH:(o + 1) * CH]
                    for part, (f, g, op) in enumerate(((hc, hs, ALU.subtract), (hs, hc, ALU.add))):
                        dve.tensor_tensor(ytmp[:, 0:CH], uc, f, ALU.mult)
                        link(dve.tensor_tensor(ytmp[:, CH:2 * CH], us, g, ALU.mult))
                        last = dve.tensor_tensor(yfre[:, b, part, :], ytmp[:, 0:CH], ytmp[:, CH:2 * CH], op)
                        if part == 0:
                            link(last)
                    last.then_inc(s["yf"], 1)
                    dve.wait_ge(s["yf"], at("yf", l, 3 * o + b + 1))
                for c in range(2):
                    dve.wait_ge(s["yc_raw"], at("yc_raw", l, 2 * o + c + 1))
                    cur = zc[:, 4 + c, :]
                    link(dve.scalar_tensor_tensor(cur, cur, hyb[:, o, c:c + 1], ps[5 + c][:, 0:TOK], ALU.mult, ALU.add))
                    dst = cur if o == 0 else act_t[:, 2 + c, :]
                    dve.tensor_tensor(dst, cur, zc[:, 2 * o + c, :], ALU.mult).then_inc(s["yc"], 1)
                dve.wait_ge(s["yc"], at("yc", l, 2 * o + 2))

            if l == 0:
                add_group(5)
            for hh in range(HEADS):
                b = 2 * (hh % 2)
                dve.wait_ge(s["q_raw"], at("q_raw", l, hh + 1))
                dve.wait_ge(s["q_nope"], at("q_nope", l, hh + 1))
                dst = qT[64:96, hh, P:TOK]
                dve.tensor_tensor(qtmp[64:96, :], ps[b][64:96, P:TOK], ropeT[64:96, 0, :], ALU.mult)
                link(dve.tensor_tensor(dst, ps[b + 1][64:96, 0:LAT], ropeT[64:96, 1, :], ALU.mult))
                dve.tensor_tensor(dst, dst, qtmp[64:96, :], ALU.add).then_inc(s["q_pe"], 1)
                dve.wait_ge(s["q_pe"], at("q_pe", l, hh + 1))
            def maxima(hh):
                b, c = 2 * (hh % 2), SOFT_COLS[hh % 2]
                dve.wait_ge(s["sc_raw"], at("sc_raw", l, hh + 1))
                dve.reduce_max(st[:, c + 9:c + 10], ps[b][:, 0:384], AX.X)
                dve.reduce_max(st[:, c + 10:c + 11], ps[b][:, 384:512], AX.X)
                link(dve.reduce_max(st[:, c + 11:c + 12], ps[b + 1][:, 0:384], AX.X))
                dve.tensor_scalar(st[:, c:c + 3], st[:, c + 9:c + 12], -QK_SCALE, None, ALU.mult).then_inc(s["mx"], 1)

            maxima(0)
            for hh in range(HEADS):
                if hh + 1 < HEADS:
                    maxima(hh + 1)
                c, pr = SOFT_COLS[hh % 2], probs[hh % 2]
                dve.wait_ge(s["pexp"], at("pexp", l, hh + 1))
                link(dve.reciprocal(st[:, c + 6:c + 9], st[:, c + 3:c + 6]))
                for i, (o, n) in enumerate(((0, 384), (384, P), (512, 384))):
                    last = dve.tensor_scalar(pr[:, o:o + n], pr[:, o:o + n], st[:, c + 6 + i:c + 7 + i], None, ALU.mult)
                last.then_inc(s["pn"], 1)

            dve.wait_ge(s["gate_in"], 32 * (2 * l + 1))
            dve.wait_ge(s["ln_in"], 32 * (2 * l + 2))
            dve.wait_ge(s["mod12_in"], 64 * (2 * l + 2))
            fuse_rows(dve, link, rows_by_half[1], lat_shift, region_k[:, 0:D])
            if l > 0:
                dve.wait_ge(s["x2"], at("x2", l - 1))
            for t in range(TT):
                if t < TT - 1:
                    dve.wait_ge(s["out_raw"], at("out_raw", l, t + 1))
                else:
                    dve.wait_ge(s["chunk_done"], last_chunk("out", l, OUT_CHUNKS - 1))
                for half in range(2):
                    cols = slice(half * 512, (half + 1) * 512)
                    last = dve.tensor_tensor(h[:, t, cols], ps[2 * t + half][:, :], gates[:, min(t, 1), cols], ALU.mult)
                link(last)
                link(dve.scalar_tensor_tensor(x[:, t, :], x[:, t, :], ALPHA, h[:, t, :], ALU.mult, ALU.add))
                norm_stats(t)
                norm_scale(norms(l, 1, 0), t)
                modulated(1, t, "h2", norms(l, 1, 0))

            logits = rt[:, 40:148].rearrange("p (t n) -> p t n", t=TT)

            def col3(c, n=1):
                return rt[:, c:c + 3 * n].rearrange("p (t n) -> p t n", t=TT)

            def const(c, n):
                return cst[:, c:c + n].unsqueeze(1).to_broadcast([P, TT, n])

            def first_max(values, n, c_max, c_eq, c_pri, c_pm, rank, out):
                link(dve.tensor_reduce(rt[:, c_max:c_max + 3], values, AX.X, ALU.max))
                link(dve.tensor_tensor(col3(c_eq, n), values, col3(c_max).to_broadcast([P, TT, n]), ALU.is_ge))
                link(dve.tensor_tensor(col3(c_pri, n), col3(c_eq, n), const(rank, n), ALU.mult))
                link(dve.tensor_reduce(rt[:, c_pm:c_pm + 3], col3(c_pri, n), AX.X, ALU.max))
                return dve.tensor_tensor(out, col3(c_pri, n), col3(c_pm).to_broadcast([P, TT, n]), ALU.is_equal)

            dve.wait_ge(s["lg_raw"], at("lg_raw", l))
            link(dve.tensor_tensor(logits, ps[6][:, 0:108].rearrange("p (t n) -> p t n", t=TT),
                                   rows[:, 896:932].unsqueeze(1).to_broadcast([P, TT, 36]), ALU.add))
            oh = col3(0, 4)
            first_max(logits[:, :, 0:4], 4, 150, 156, 168, 153, C_RANK, oh).then_inc(s["oh"], 1)
            dve.wait_ge(s["oh"], at("oh", l))
            dve.tensor_tensor(col3(280, 4), logits[:, :, 0:4], col3(150).to_broadcast([P, TT, 4]), ALU.subtract)
            prod = rt[:, 184:280].rearrange("p (t g e) -> p t g e", t=TT, g=4)
            for t in range(TT):
                last = dve.tensor_tensor(prod[:, t], logits[:, t, 4:36].rearrange("p (g e) -> p g e", g=4),
                                         oh[:, t, :].unsqueeze(2).to_broadcast([P, 4, 8]), ALU.mult)
            link(last)
            e_in = col3(316, 8)
            link(dve.tensor_reduce(e_in, prod.rearrange("p t g e -> p t e g"), AX.X, ALU.add))
            oh1, oh2, e_2nd = col3(344, 8), col3(392, 8), col3(368, 8)
            link(first_max(e_in, 8, 340, 184, 208, 232, C_GE, oh1))
            link(dve.scalar_tensor_tensor(e_2nd, oh1, -BIG, e_in, ALU.mult, ALU.add))
            link(first_max(e_2nd, 8, 416, 184, 208, 232, C_GE, oh2))
            dve.tensor_tensor(rt[:, 292:295], rt[:, 416:419], rt[:, 340:343], ALU.subtract).then_inc(s["lg_sh"], 1)
            dve.wait_ge(s["lg_exp"], at("lg_exp", l))
            link(dve.tensor_reduce(rt[:, 419:422], col3(300, 4), AX.X, ALU.add))
            link(dve.scalar_tensor_tensor(rt[:, 422:425], rt[:, 312:315], 1.0, rt[:, 419:422], ALU.add, ALU.mult))
            link(dve.reciprocal(rt[:, 425:428], rt[:, 422:425]))
            link(dve.tensor_tensor(rt[:, 428:431], rt[:, 425:428], rt[:, 312:315], ALU.mult))
            link(dve.tensor_tensor(oh1, oh1, col3(425).to_broadcast([P, TT, 8]), ALU.mult))
            link(dve.tensor_tensor(oh2, oh2, col3(428).to_broadcast([P, TT, 8]), ALU.mult))
            link(dve.tensor_tensor(col3(12, 8), oh1, oh2, ALU.add))
            dve.wait_ge(s["cum_raw"], at("cum_raw", l))
            link(dve.tensor_tensor(col3(432, 4), oh, ps[7][:, 0:12].rearrange("p (t n) -> p t n", t=TT), ALU.mult))
            link(dve.tensor_reduce(rt[:, 444:447], col3(432, 4), AX.X, ALU.add))
            link(dve.tensor_scalar(rt[:, 448:451], rt[:, 444:447], float(P), None, ALU.is_ge))
            link(dve.scalar_tensor_tensor(rt[:, 451:454], rt[:, 444:447], 2.0 * P, rt[:, 448:451], ALU.is_ge, ALU.add))
            link(dve.scalar_tensor_tensor(rt[:, 454:457], rt[:, 451:454], -float(P), rt[:, 444:447], ALU.mult, ALU.add))
            link(dve.tensor_scalar(rt[:, 457:461], ps[7][:, 12:16], P + 1.0, None, ALU.is_ge))
            link(dve.scalar_tensor_tensor(rt[:, 457:461], ps[7][:, 12:16], 2.0 * P + 1, rt[:, 457:461], ALU.is_ge, ALU.add))
            link(dve.memset(rt[:, 461:462], 0.0))
            for g in range(GROUPS):
                link(dve.tensor_tensor(rt[:, 462 + g:463 + g], rt[:, 461 + g:462 + g], rt[:, 457 + g:458 + g], ALU.add))
            link(dve.tensor_tensor(col3(432, 4), oh, const(C_GI, 4), ALU.mult))
            link(dve.tensor_reduce(rt[:, 466:469], col3(432, 4), AX.X, ALU.add))
            link(dve.tensor_tensor(col3(432, 4), oh, rt[:, 461:465].unsqueeze(1).to_broadcast([P, TT, 4]), ALU.mult))
            link(dve.tensor_reduce(rt[:, 469:472], col3(432, 4), AX.X, ALU.add))
            link(dve.scalar_tensor_tensor(rt[:, 469:472], rt[:, 469:472], GROUPS - 1.0, rt[:, 451:454], ALU.add, ALU.add))
            link(dve.tensor_tensor(rt[:, 469:472], rt[:, 469:472], rt[:, 466:469], ALU.subtract))
            link(dve.tensor_tensor(rt[:, 469:472], rt[:, 469:472], rt[:, 448:451], ALU.mult))
            link(dve.tensor_tensor(rt[:, 469:472], rt[:, 469:472], rt[:, 466:469], ALU.add))
            n_v = GROUPS + EXTRA
            tgt = col3(474, n_v)
            link(dve.tensor_tensor(tgt, col3(469).to_broadcast([P, TT, n_v]), const(C_VI, n_v), ALU.is_equal))
            link(dve.tensor_scalar(rt[:, 454:457], rt[:, 454:457], 1.0, None, ALU.add))
            dve.tensor_tensor(tgt, tgt, col3(454).to_broadcast([P, TT, n_v]), ALU.mult).then_inc(s["tgt"], 1)
            dve.wait_ge(s["tgt"], at("tgt", l))
            def pick(v, e, loop=0):
                for t in range(TT):
                    who = tgt[:, t, bass.ds(loop * 2 + v, 1)]
                    last = dve.tensor_scalar(sel[:, t, :], iota, who, None, ALU.is_equal)
                last.then_inc(e["sel"], 1)

            def gathered(e, half, slot, g, loop=0, b=3):
                dve.wait_ge(e["x_hi"], loop * 4 + (2 * g + half + 1))
                tokens = ps[b][:, :].rearrange("p (k n) -> p k n", k=4)
                dve.tensor_tensor(x_lo[:, slot, 4 * half:4 * half + 4, :], tokens,
                                  x_hi[:, slot, 4 * half:4 * half + 4, :].bitcast(F32), ALU.subtract)\
                    .then_inc(e["x_lo"], 1)

            def run(experts, slot0, e, chunk0, v0, loop, rest_in, g0=None):
                q0 = v0 * EPG
                ex_by, v_by, c_by = loop * PAIR, loop * 2, loop * (3 * PAIR)

                def low(c):
                    dve.wait_ge(e["hi"], c_by + (chunk0 + c + 1))
                    dve.tensor_tensor(w_lo[:, c % SPLIT, :], ring[:, c % RING, :], w_hi[:, c % SPLIT, :].bitcast(F32),
                                      ALU.subtract).then_inc(e["lo"], 1)

                def summed(visit, t, b=6):
                    dve.wait_ge(e["sct"], v_by * TT + (TT * (v0 + visit) + t + 1))
                    for half in range(2):
                        dst = moe[:, t, half * 512:(half + 1) * 512]
                        last = dve.tensor_tensor(dst, dst, ps[b + half][:, :], ALU.add)
                    last.then_inc(e["acc"], 1)

                for c in range(SPLIT):
                    low(c)
                for c, (kind, ex) in enumerate(order(experts)):
                    if kind == "G" and ex > 0 or (kind, ex) == ("D", experts - 1):
                        turned = ex - 1 if kind == "G" else ex
                        dve.wait_ge(e["hd_hi"], ex_by + (q0 + turned + 1))
                        dve.tensor_tensor(hd_lo[:, turned % 2, :], ps[2][:, 0:FF],
                                          hd_hi[:, turned % 2, :].bitcast(F32), ALU.subtract).then_inc(e["hd_lo"], 1)
                    if kind == "U":
                        if ex % EPG == 0:
                            sem_in, value, by = rest_in(ex // EPG)
                            dve.wait_ge(sem_in, loop * by + value)
                        dve.wait_ge(e["silu"], ex_by + (q0 + ex + 1))
                        if q0 > 0 or ex >= 2:
                            dve.wait_ge(e["hd_raw"], ex_by + (q0 + ex - 1))
                        sl = (slot0 + ex // EPG) % 2
                        dve.scalar_tensor_tensor(hd[:, ex % 2, :], ps[ex % 2][:, FF:2 * FF],
                                                 wslot[:, sl, ex % EPG:ex % EPG + 1], sg[:, ex % 2, :],
                                                 ALU.mult, ALU.mult).then_inc(e["hid"], 1)
                        if experts == PAIR:
                            if ex in GATHER and GATHER[ex][1] < 2:
                                nth, step = GATHER[ex]
                                gathered(e, step, 1 - nth, g0 + 1 + nth, loop)
                            if ex in SCATTER:
                                summed(0, SCATTER[ex])
                            if ex in (1, 8):
                                nth = ex // 8
                                dve.wait_ge(e["picked"], loop * 2 + (g0 + 1 + nth))
                                pick(1 + nth, e, loop)
                    if kind == "D" and ex % EPG == EPG - 1:
                        dve.wait_ge(e["y"], v_by * 2 + (2 * (v0 + ex // EPG) + 1))
                        for half in range(2):
                            part = slice(half * 512, (half + 1) * 512)
                            last = dve.tensor_tensor(y_lo[:, part], ps[4 + half][:, :], y_hi[:, part].bitcast(F32),
                                                     ALU.subtract)
                        last.then_inc(e["y"], 1)
                    if c + SPLIT < 3 * experts:
                        low(c + SPLIT)
                for t in range(TT):
                    summed(experts // EPG - 1, t, LAST_BANKS[t])

            g0 = l * GATHERS
            pick(0, e_main)
            for i in range(EXTRA):
                link(dve.tensor_scalar(rt[:, 432:435], rt[:, 462:465], float(i), None, ALU.is_le))
                link(dve.tensor_reduce(rt[:, 496 + i:497 + i], rt[:, 432:435], AX.X, ALU.add))
            link(dve.tensor_copy(xi[:, 1:3], rt[:, 496:498]))
            dve.tensor_copy(xi[:, 0:1], rt[:, 465:466]).then_inc(s["regs"], 1)
            for half in range(2):
                gathered(e_main, half, 0, g0, b=3 - half)
            dve.wait_ge(s["moe_zero"], l + 1)
            with dve.Fori(0, GROUPS // 2) as it:
                run(PAIR, 0, e_main, l * MOE_CHUNKS, l * GROUPS, it, lambda visit: (e_main["rest"], g0 + visit + 1, 2), g0)
            dve.wait_ge(e_main["acc"], TT * GROUPS * (l + 1))
            extra = dve.value_load(xi[0:1, 0:1], min_val=0, max_val=EXTRA)
            xe = e_extra[l]
            with dve.If(extra >= 1):
                run(EPG, 0, xe, 0, 0, 0, lambda visit: (e_main["rest"], g0 + GATHERS, 0))
                dve.wait_ge(xe["acc"], TT)
                with dve.If(extra >= 2):
                    dve.wait_ge(e_main["picked"], g0 + GATHERS)
                    pick(5, xe)
                    for half in range(2):
                        gathered(xe, half, 1, 0)
                    run(EPG, 1, xe, EPG * 3, 1, 0, lambda visit: (xe["rest"], 1, 0))
                    dve.wait_ge(xe["acc"], 2 * TT)

            dve.wait_ge(s["gate_in"], 32 * (2 * l + 2))
            dve.wait_ge(s["ln_in"], 32 * (2 * l + 3))
            dve.wait_ge(s["x1"], at("x1", l))
            base = norms(l, 2, 0)

            def normed_use(t):
                if l + 1 < DEPTH:
                    modulated(0, t, "h", base)
                else:
                    affine(base, t, "x2")

            if l + 1 < DEPTH:
                dve.wait_ge(s["pool_step"], fused_steps(l + 1))
            for t in range(TT):
                link(dve.tensor_tensor(moe[:, t, :], moe[:, t, :], gates[:, min(t, 1), :], ALU.mult))
                link(dve.scalar_tensor_tensor(x[:, t, :], x[:, t, :], ALPHA, moe[:, t, :], ALU.mult, ALU.add))
                norm_stats(t)
                if t >= 1:
                    norm_scale(base, t - 1)
                if t >= 2:
                    normed_use(t - 2)
            norm_scale(base, TT - 1)
            normed_use(TT - 2)
            normed_use(TT - 1)

    ctx.close()


def packed(w):
    def flat(name):
        return np.asarray(w[name]).reshape(DEPTH, -1)

    def by_partition(name, outer):
        v = np.asarray(w[name]).reshape(DEPTH, outer, -1, P)
        return v.transpose(0, 3, 1, 2).reshape(DEPTH, P, -1)

    router = np.concatenate([np.asarray(w["moe_w_gr"]), np.asarray(w["moe_w_er"]).reshape(DEPTH, D, -1)], 2)
    columns = [by_partition("gm_bs", 4), by_partition("hy_conv_w", 3), by_partition("hy_conv_b", 1),
               by_partition("hy_bias", 2)]
    w1 = np.zeros((DEPTH, FH, FH), np.float32)
    w1[:, :EMB] = np.asarray(w["hy_f_w1"])
    return dict(
        rows=np.concatenate([flat(n) for n in ("gm_ln_g", "gm_ln_b", "mla_gq", "mla_gkv", "moe_b_gr", "moe_b_er")], 1),
        cols=np.concatenate(columns, 2),
        fw=np.concatenate([w1, np.asarray(w["hy_f_w2"]), np.asarray(w["hy_f_b1"])[:, :, None],
                           np.asarray(w["hy_f_b2"])[:, :, None], np.asarray(w["hy_f_freq"]).transpose(0, 2, 1)], 2),
        gm_ws_t=np.asarray(w["gm_ws"]).transpose(0, 3, 1, 2).reshape(DEPTH, P, -1),
        w_router=router.reshape(DEPTH, P, -1),
    )


def tables():
    f8 = np.float64
    cst = np.zeros((P, C_END))
    cst[:, C_ID:C_ID + P] = np.eye(P)
    cst[:, C_TRI:C_TRI + P] = np.triu(np.ones((P, P)), 1)
    cst[:, C_ONE:C_ONE + P] = 1.0
    cst[:, C_IOTA:C_IOTA + P] = np.arange(1, P + 1)
    cst[:, C_RANK:C_RANK + 4] = np.arange(4, 0, -1)
    cst[:, C_GE:C_GE + 8] = np.arange(8, 0, -1)
    cst[:, C_GI:C_GI + 4] = np.arange(4)
    cst[:, C_VI:C_VI + 6] = np.arange(6)
    cst[:, C_MASK:C_MASK + 3] = 1.0
    cst[0, C_MASK:C_MASK + 2] = 0.0
    n = ROPE // 4
    inv = (np.float32(10000.0) ** (-np.arange(n, dtype=np.float32) / np.float32(n))).astype(np.float32)
    p = np.arange(LAT)
    ang = np.concatenate([(p // 64)[:, None].astype(np.float32) * inv, (p % 64)[:, None].astype(np.float32) * inv], 1)
    cos = np.repeat(np.cos(ang.astype(f8)), 2, axis=1)
    sin = np.repeat(np.sin(ang.astype(f8)), 2, axis=1)
    sin[:, 0::2] *= -1.0
    cst[:, C_COS:C_COS + 64] = cos.reshape(2, P, ROPE).transpose(1, 0, 2).reshape(P, 64)
    cst[:, C_SIN:C_SIN + 64] = sin.reshape(2, P, ROPE).transpose(1, 0, 2).reshape(P, 64)
    rope_t = np.stack([cos.T, sin.T], 1)
    dft = np.zeros((P, DFT_COLS))
    for L, oc, osn, oct_, ost in ((P, G_C, G_S, G_CT, G_ST), (LAT, F_C, F_S, F_CT, F_ST)):
        arg = np.pi * np.outer(np.arange(L), 2 * np.arange(L) + 1) / (2 * L)
        for o, m in ((oc, np.cos(arg)), (osn, np.sin(arg)), (oct_, np.cos(arg).T / L), (ost, np.sin(arg).T / L)):
            dft[:, o:o + L * L // P] = m.reshape(L // P, P, L).transpose(1, 0, 2).reshape(P, -1)
    feats, decays = [], []
    deltas = np.abs(np.linspace(math.log(1e-2) / 1.5, math.log(1e-2) / 0.3, CH))
    for L in (P, LAT):
        t = np.linspace(0.0, 1.0, L)[:, None]
        bands = (EMB - 1) // 2
        w = 2.0 * math.pi * np.arange(L)[:, None] / L
        f = np.linspace(1e-4, bands - 1, bands)[None]
        feats.append(np.concatenate([t, np.cos(f * w), -np.sin(f * w)], -1))
        decays.append(np.exp(-t * deltas))
    z_t = np.concatenate(feats, 0).T
    decay = np.concatenate(decays, 0).reshape(TT, P, CH).transpose(1, 0, 2)
    out = dict(consts=cst, rope_t=rope_t, dft=dft, z_t=z_t, decay=decay)
    return {k: np.ascontiguousarray(v, dtype=np.float32) for k, v in out.items()}


_INS = ("x_prompt", "x_sample", "c", "cache_ckv", "cache_kpe", "c_ctx", "ln_in_g", "ln_in_b", "w_mod", "b_mod", "w_in",
        "hy_f_w3", "mla_wuq", "mla_wukv", "w_out", "ln1_g", "ln1_b", "ln2_g", "ln2_b",
        "moe_w_gate", "moe_w_up", "moe_w_down")
_OUTS = ((1, P, D), (1, LAT, D), (1, DEPTH, P, P), (1, DEPTH, P, ROPE))


def kernel(**inputs):
    import concourse.bacc as _bacc
    from concourse.bass_utils import run_bass_kernel_spmd as _run

    nc = _bacc.Bacc("TRN2", target_bir_lowering=False, num_devices=1)
    arrays, aps = {}, {}
    for name, value in [(n, inputs[n]) for n in _INS] + list(packed(inputs).items()) + list(tables().items()):
        arr = np.ascontiguousarray(value)
        arrays[f"in_{name}"] = arr
        aps[name] = nc.dram_tensor(f"in_{name}", arr.shape, mybir.dt.from_np(arr.dtype), kind="ExternalInput").ap()
    outs = [nc.dram_tensor(f"out_{i}", shape, F32, kind="ExternalOutput").ap() for i, shape in enumerate(_OUTS)]
    build(nc, aps, outs)
    r = _run(nc, [arrays], core_ids=[0])
    return tuple(r.results[0][f"out_{i}"] for i in range(len(_OUTS)))
```
